# Optimizing a Trainium2 kernel written in Bass

```python
import math
import jax, jax.numpy as jnp
from jax import lax
import numpy as np

D_MODEL = 1024
BATCH = 1
SEQ = 256
DEPTH = 2

DN_ALPHA = (2.0 * DEPTH) ** 0.25
DN_BETA = (8.0 * DEPTH) ** -0.25
LN_EPS = 1e-5
NEG_INF = -1e30

D_FF = 256 * ((8 * D_MODEL // 3 + 255) // 256)
MACARON_WEIGHT = 0.5

CONV_CH = D_MODEL
CONV_WIDTH = 31

SSM_D_INNER = D_MODEL
SSM_HEAD_DIM = 64
SSM_HEADS = SSM_D_INNER // SSM_HEAD_DIM
SSM_GROUPS = 4
SSM_HEADS_PER_GROUP = SSM_HEADS // SSM_GROUPS
SSM_STATE = 128
SSM_CONV_WIDTH = 4
SSM_CHUNK = 256
SSM_CONV_DIM = SSM_D_INNER + 2 * SSM_GROUPS * SSM_STATE

NSA_HEAD_DIM = 64
NSA_HEADS = D_MODEL // NSA_HEAD_DIM
NSA_KV_HEADS = 4
NSA_GQA = NSA_HEADS // NSA_KV_HEADS
CMP_LEN = 32
CMP_STRIDE = 16
CMP_HIDDEN = 2 * NSA_HEAD_DIM
SEL_BLOCK = 64
N_SELECT = 16
WINDOW = 512
Q_BLOCK = 64
FORCED_SCORE = 1e4
ROPE_THETA = 10000.0

N_BRANCH = 3
A_IN = 2 * CONV_CH
B_IN = 2 * SSM_D_INNER + 2 * SSM_GROUPS * SSM_STATE + SSM_HEADS
C_IN = NSA_HEADS * NSA_HEAD_DIM + 6 * NSA_KV_HEADS * NSA_HEAD_DIM + 3 * NSA_HEADS
GATE_IN = N_BRANCH * D_MODEL
IN_COLS = A_IN + B_IN + C_IN + GATE_IN


def _split(x, sizes):
    return jnp.split(x, [int(s) for s in np.cumsum(sizes)[:-1]], axis=-1)

def layer_norm(x, g, b):
    x32 = x.astype(jnp.float32)
    mu = jnp.mean(x32, -1, keepdims=True)
    var = jnp.mean(jnp.square(x32 - mu), -1, keepdims=True)
    return ((x32 - mu) * lax.rsqrt(var + LN_EPS) * g + b).astype(x.dtype)

def rms_norm(x, g):
    x32 = x.astype(jnp.float32)
    return x32 * lax.rsqrt(jnp.mean(jnp.square(x32), -1, keepdims=True) + LN_EPS) * g

def causal_dwconv(x, w, b):
    width, ch = w.shape
    y = lax.conv_general_dilated(x, w[:, None, :].astype(x.dtype), (1,), [(width - 1, 0)],
                                 dimension_numbers=('NWC', 'WIO', 'NWC'), feature_group_count=ch)
    return y + b

def rope(x, pos):
    half = x.shape[-1] // 2
    inv_freq = ROPE_THETA ** (-jnp.arange(half, dtype=jnp.float32) / half)
    ang = pos.astype(jnp.float32)[:, None] * inv_freq[None, :]
    cos = jnp.cos(ang)[:, None, :]
    sin = jnp.sin(ang)[:, None, :]
    x32 = x.astype(jnp.float32)
    x1, x2 = x32[..., :half], x32[..., half:]
    return jnp.concatenate([x1 * cos - x2 * sin, x2 * cos + x1 * sin], -1).astype(x.dtype)

def modulate(h, shift, scale):
    return h * (1.0 + scale) + shift

def swiglu_ffn(u, w_gate, w_up, w_down):
    return (jax.nn.silu(u @ w_gate) * (u @ w_up)) @ w_down

def conformer_conv(a_in, conv_w, conv_b, norm_g, norm_b):
    val, gate = _split(a_in, [CONV_CH, CONV_CH])
    a = val * jax.nn.sigmoid(gate)
    a = causal_dwconv(a, conv_w, conv_b)
    return jax.nn.silu(layer_norm(a, norm_g, norm_b))

def ssd_chunked(x, a, b, c):
    bsz, seq, ng, nr, hp = x.shape
    chunk = math.gcd(SSM_CHUNK, seq)
    nc = seq // chunk
    xc = x.reshape(bsz, nc, chunk, ng, nr, hp)
    bc = b.reshape(bsz, nc, chunk, ng, -1)
    cc = c.reshape(bsz, nc, chunk, ng, -1)
    a_cs = jnp.cumsum(a.reshape(bsz, nc, chunk, ng, nr).transpose(0, 3, 4, 1, 2), axis=-1)
    causal = jnp.tril(jnp.ones((chunk, chunk), bool))
    seg = jnp.exp(jnp.where(causal, a_cs[..., :, None] - a_cs[..., None, :], NEG_INF))
    cb = jnp.einsum('bclgn,bcsgn->bgcls', cc, bc)
    y_diag = jnp.einsum('bgrcls,bcsgrp->bclgrp', cb[:, :, None] * seg, xc)
    decay_in = jnp.exp(a_cs[..., -1:] - a_cs)
    chunk_states = jnp.einsum('bclgn,bgrcl,bclgrp->cbgrpn', bc, decay_in, xc)
    chunk_decay = jnp.exp(a_cs[..., -1]).transpose(3, 0, 1, 2)

    def step(h, inp):
        st, dec = inp
        return h * dec[..., None, None] + st, h

    h0 = jnp.zeros(chunk_states.shape[1:], chunk_states.dtype)
    _, h_prev = lax.scan(step, h0, (chunk_states, chunk_decay))
    y_off = jnp.einsum('bclgn,cbgrpn,bgrcl->bclgrp', cc, h_prev, jnp.exp(a_cs))
    return (y_diag + y_off).reshape(bsz, seq, ng, nr, hp)

def mamba2_ssd(ssm_in, conv_w, conv_b, dt_bias, a_log, d_skip, norm_w):
    bsz, seq, _ = ssm_in.shape
    f32 = jnp.float32
    gn = SSM_GROUPS * SSM_STATE
    z, xbc, dt = _split(ssm_in, [SSM_D_INNER, SSM_CONV_DIM, SSM_HEADS])
    xbc = jax.nn.silu(causal_dwconv(xbc, conv_w, conv_b))
    xs, b_in, c_in = _split(xbc, [SSM_D_INNER, gn, gn])
    dt = jax.nn.softplus(dt.astype(f32) + dt_bias.astype(f32)).reshape(bsz, seq, SSM_GROUPS, SSM_HEADS_PER_GROUP)
    a = -jnp.exp(a_log.astype(f32)).reshape(SSM_GROUPS, SSM_HEADS_PER_GROUP)
    xh = xs.astype(f32).reshape(bsz, seq, SSM_GROUPS, SSM_HEADS_PER_GROUP, SSM_HEAD_DIM)
    bm = b_in.astype(f32).reshape(bsz, seq, SSM_GROUPS, SSM_STATE)
    cm = c_in.astype(f32).reshape(bsz, seq, SSM_GROUPS, SSM_STATE)
    y = ssd_chunked(xh * dt[..., None], a * dt, bm, cm)
    y = y + d_skip.astype(f32).reshape(SSM_GROUPS, SSM_HEADS_PER_GROUP, 1) * xh
    y = y.reshape(bsz, seq, SSM_D_INNER) * jax.nn.silu(z.astype(f32))
    return rms_norm(y, norm_w).astype(ssm_in.dtype)

def compress_blocks(kv, pe, w1, w2):
    bsz, seq, nkv, hd = kv.shape
    n_cmp = (seq - CMP_LEN) // CMP_STRIDE + 1
    idx = jnp.arange(n_cmp)[:, None] * CMP_STRIDE + jnp.arange(CMP_LEN)[None, :]
    blocks = kv[:, idx] + pe[:, None, :]
    flat = blocks.transpose(0, 1, 3, 2, 4).reshape(bsz, n_cmp, nkv, CMP_LEN * hd)
    return jax.nn.gelu(flat @ w1) @ w2

def nsa_attention(nsa_in, pe_k, pe_v, k_w1, k_w2, v_w1, v_w2):
    bsz, seq, _ = nsa_in.shape
    dt_ = nsa_in.dtype
    f32 = jnp.float32
    kvd = NSA_KV_HEADS * NSA_HEAD_DIM
    q, k_c, v_c, k_s, v_s, k_w, v_w, gate_logits = _split(nsa_in, [NSA_HEADS * NSA_HEAD_DIM] + [kvd] * 6 + [3 * NSA_HEADS])
    pos = jnp.arange(seq)
    kv_shape = (bsz, seq, NSA_KV_HEADS, NSA_HEAD_DIM)
    q = rope(q.reshape(bsz, seq, NSA_HEADS, NSA_HEAD_DIM), pos).reshape(bsz, seq, NSA_KV_HEADS, NSA_GQA, NSA_HEAD_DIM)
    n_cmp = (seq - CMP_LEN) // CMP_STRIDE + 1
    cmp_end = jnp.arange(n_cmp) * CMP_STRIDE + CMP_LEN - 1
    k_cmp = rope(compress_blocks(k_c.reshape(kv_shape), pe_k, k_w1, k_w2), cmp_end)
    v_cmp = compress_blocks(v_c.reshape(kv_shape), pe_v, v_w1, v_w2)
    n_sb = seq // SEL_BLOCK
    n_sel = min(N_SELECT, n_sb)
    blk_shape = (bsz, n_sb, SEL_BLOCK, NSA_KV_HEADS, NSA_HEAD_DIM)
    k_sel = rope(k_s.reshape(kv_shape), pos).reshape(blk_shape).transpose(0, 3, 1, 2, 4)
    v_sel = v_s.reshape(blk_shape).transpose(0, 3, 1, 2, 4)
    pad = ((0, 0), (WINDOW, 0), (0, 0), (0, 0))
    k_win = jnp.pad(rope(k_w.reshape(kv_shape), pos), pad)
    v_win = jnp.pad(v_w.reshape(kv_shape), pad)
    gates = jax.nn.sigmoid(gate_logits.astype(f32)).astype(dt_).reshape(bsz, seq, NSA_KV_HEADS, NSA_GQA, 3)
    c_start = jnp.arange(n_cmp) * CMP_STRIDE
    s_start = jnp.arange(n_sb) * SEL_BLOCK
    overlap = ((c_start[:, None] < s_start[None, :] + SEL_BLOCK) &
               (c_start[:, None] + CMP_LEN > s_start[None, :])).astype(f32)
    scale = NSA_HEAD_DIM ** -0.5
    b_idx = jnp.arange(bsz)[:, None, None, None]
    g_idx = jnp.arange(NSA_KV_HEADS)[None, :, None, None]
    blk_ids = jnp.arange(n_sb)

    def query_block(i):
        q0 = i * Q_BLOCK
        t = q0 + jnp.arange(Q_BLOCK)
        qb = lax.dynamic_slice_in_dim(q, q0, Q_BLOCK, axis=1)
        s = jnp.einsum('bqgrd,bngd->bgrqn', qb, k_cmp).astype(f32) * scale
        cmask = cmp_end[None, :] <= t[:, None]
        p_cmp = jax.nn.softmax(jnp.where(cmask, s, NEG_INF), -1) * cmask
        o_cmp = jnp.einsum('bgrqn,bngd->bqgrd', p_cmp.astype(dt_), v_cmp)
        imp = jnp.einsum('bgrqn,nj->bgqj', p_cmp, overlap)
        cur = (t // SEL_BLOCK)[:, None]
        forced = (blk_ids[None, :] == 0) | (blk_ids[None, :] == cur) | (blk_ids[None, :] == cur - 1)
        future = blk_ids[None, :] * SEL_BLOCK > t[:, None]
        imp = jnp.where(forced, FORCED_SCORE, jnp.where(future, -1.0, imp))
        _, sel = lax.top_k(imp, n_sel)
        kg = k_sel[b_idx, g_idx, sel]
        vg = v_sel[b_idx, g_idx, sel]
        s = jnp.einsum('bqgrd,bgqkld->bgrqkl', qb, kg).astype(f32) * scale
        kpos = sel[..., None] * SEL_BLOCK + jnp.arange(SEL_BLOCK)
        smask = (kpos <= t[None, None, :, None, None])[:, :, None]
        s = jnp.where(smask, s, NEG_INF).reshape(bsz, NSA_KV_HEADS, NSA_GQA, Q_BLOCK, n_sel * SEL_BLOCK)
        p_sel = jax.nn.softmax(s, -1).reshape(bsz, NSA_KV_HEADS, NSA_GQA, Q_BLOCK, n_sel, SEL_BLOCK)
        o_sel = jnp.einsum('bgrqkl,bgqkld->bqgrd', p_sel.astype(dt_), vg)
        kw = lax.dynamic_slice_in_dim(k_win, q0, WINDOW + Q_BLOCK, axis=1)
        vw = lax.dynamic_slice_in_dim(v_win, q0, WINDOW + Q_BLOCK, axis=1)
        wpos = q0 - WINDOW + jnp.arange(WINDOW + Q_BLOCK)
        wmask = (wpos[None, :] <= t[:, None]) & (wpos[None, :] > t[:, None] - WINDOW) & (wpos[None, :] >= 0)
        s = jnp.einsum('bqgrd,bkgd->bgrqk', qb, kw).astype(f32) * scale
        p_win = jax.nn.softmax(jnp.where(wmask, s, NEG_INF), -1)
        o_win = jnp.einsum('bgrqk,bkgd->bqgrd', p_win.astype(dt_), vw)
        g = lax.dynamic_slice_in_dim(gates, q0, Q_BLOCK, axis=1)
        return g[..., 0:1] * o_cmp + g[..., 1:2] * o_sel + g[..., 2:3] * o_win

    out = lax.map(query_block, jnp.arange(seq // Q_BLOCK))
    return out.transpose(1, 0, 2, 3, 4, 5).reshape(bsz, seq, NSA_HEADS * NSA_HEAD_DIM)

def hybrid_token_mixer(u, w_in, conv_a_w, conv_a_b, norm_a_g, norm_a_b, w_a_out,
                       ssm_conv_w, ssm_conv_b, ssm_dt_bias, ssm_a_log, ssm_d, ssm_norm_w, w_b_out,
                       cmp_pe_k, cmp_pe_v, cmp_k_w1, cmp_k_w2, cmp_v_w1, cmp_v_w2, w_c_out, w_o):
    bsz, seq, _ = u.shape
    proj = jnp.einsum('bsd,de->bse', u, w_in)
    a_in, b_in, c_in, g_in = _split(proj, [A_IN, B_IN, C_IN, GATE_IN])
    y_a = conformer_conv(a_in, conv_a_w, conv_a_b, norm_a_g, norm_a_b) @ w_a_out
    y_b = mamba2_ssd(b_in, ssm_conv_w, ssm_conv_b, ssm_dt_bias, ssm_a_log, ssm_d, ssm_norm_w) @ w_b_out
    y_c = nsa_attention(c_in, cmp_pe_k, cmp_pe_v, cmp_k_w1, cmp_k_w2, cmp_v_w1, cmp_v_w2) @ w_c_out
    g = jax.nn.sigmoid(g_in.astype(jnp.float32)).astype(u.dtype).reshape(bsz, seq, N_BRANCH, D_MODEL)
    merged = g[:, :, 0] * y_a + g[:, :, 1] * y_b + g[:, :, 2] * y_c
    return merged @ w_o

def first_inputs(seed: int = 0) -> dict:
    key = jax.random.key(seed)
    keys = iter(jax.random.split(key, 48))
    f32 = jnp.float32
    L = DEPTH

    def normal(shape, scale):
        return jax.random.normal(next(keys), shape, f32) * scale

    def uniform(shape, lo, hi):
        return jax.random.uniform(next(keys), shape, f32, lo, hi)

    kvd = NSA_KV_HEADS * NSA_HEAD_DIM
    col_scale = np.concatenate([
        np.ones(A_IN + B_IN + NSA_HEADS * NSA_HEAD_DIM),
        np.tile(np.concatenate([np.ones(kvd), np.full(kvd, DN_BETA)]), 3),
        np.ones(3 * NSA_HEADS + GATE_IN)]).astype(np.float32)
    dt0 = jnp.exp(uniform((L, SSM_HEADS), math.log(1e-3), math.log(1e-1)))
    cmp_in = CMP_LEN * NSA_HEAD_DIM
    return {
        'x': normal((BATCH, SEQ, D_MODEL), 1.0),
        'c': normal((BATCH, D_MODEL), 1.0),
        'ada_w': normal((L, D_MODEL, 9 * D_MODEL), 0.5 * D_MODEL ** -0.5),
        'ada_b': normal((L, 9 * D_MODEL), 0.01),
        'ln_g': 1.0 + normal((L, 3, D_MODEL), 0.02),
        'ln_b': normal((L, 3, D_MODEL), 0.02),
        'ffn_w_gate': normal((L, 2, D_MODEL, D_FF), D_MODEL ** -0.5),
        'ffn_w_up': normal((L, 2, D_MODEL, D_FF), D_MODEL ** -0.5),
        'ffn_w_down': normal((L, 2, D_FF, D_MODEL), DN_BETA * D_FF ** -0.5),
        'w_in': normal((L, D_MODEL, IN_COLS), D_MODEL ** -0.5) * jnp.asarray(col_scale),
        'conv_a_w': normal((L, CONV_WIDTH, CONV_CH), CONV_WIDTH ** -0.5),
        'conv_a_b': normal((L, CONV_CH), 0.01),
        'norm_a_g': 1.0 + normal((L, CONV_CH), 0.02),
        'norm_a_b': normal((L, CONV_CH), 0.02),
        'w_a_out': normal((L, CONV_CH, D_MODEL), CONV_CH ** -0.5),
        'ssm_conv_w': normal((L, SSM_CONV_WIDTH, SSM_CONV_DIM), SSM_CONV_WIDTH ** -0.5),
        'ssm_conv_b': normal((L, SSM_CONV_DIM), 0.01),
        'ssm_dt_bias': dt0 + jnp.log(-jnp.expm1(-dt0)),
        'ssm_a_log': jnp.log(uniform((L, SSM_HEADS), 1.0, 16.0)),
        'ssm_d': 1.0 + normal((L, SSM_HEADS), 0.1),
        'ssm_norm_w': 1.0 + normal((L, SSM_D_INNER), 0.02),
        'w_b_out': normal((L, SSM_D_INNER, D_MODEL), SSM_D_INNER ** -0.5),
        'cmp_pe_k': normal((L, CMP_LEN, NSA_HEAD_DIM), 0.02),
        'cmp_pe_v': normal((L, CMP_LEN, NSA_HEAD_DIM), 0.02),
        'cmp_k_w1': normal((L, cmp_in, CMP_HIDDEN), cmp_in ** -0.5),
        'cmp_k_w2': normal((L, CMP_HIDDEN, NSA_HEAD_DIM), CMP_HIDDEN ** -0.5),
        'cmp_v_w1': normal((L, cmp_in, CMP_HIDDEN), cmp_in ** -0.5),
        'cmp_v_w2': normal((L, CMP_HIDDEN, NSA_HEAD_DIM), CMP_HIDDEN ** -0.5),
        'w_c_out': normal((L, NSA_HEADS * NSA_HEAD_DIM, D_MODEL), (NSA_HEADS * NSA_HEAD_DIM) ** -0.5),
        'w_o': normal((L, D_MODEL, D_MODEL), DN_BETA * D_MODEL ** -0.5),
    }

def first_block(x, c, ada_w, ada_b, ln_g, ln_b, ffn_w_gate, ffn_w_up, ffn_w_down, w_in,
              conv_a_w, conv_a_b, norm_a_g, norm_a_b, w_a_out,
              ssm_conv_w, ssm_conv_b, ssm_dt_bias, ssm_a_log, ssm_d, ssm_norm_w, w_b_out,
              cmp_pe_k, cmp_pe_v, cmp_k_w1, cmp_k_w2, cmp_v_w1, cmp_v_w2, w_c_out, w_o):
    bsz = c.shape[0]
    h = x
    for l in range(DEPTH):
        mod = (jax.nn.silu(c) @ ada_w[l] + ada_b[l]).reshape(bsz, 3, 3, 1, D_MODEL)
        u = modulate(h, mod[:, 0, 0], mod[:, 0, 1])
        y = swiglu_ffn(u, ffn_w_gate[l, 0], ffn_w_up[l, 0], ffn_w_down[l, 0])
        h = layer_norm(DN_ALPHA * h + MACARON_WEIGHT * mod[:, 0, 2] * y, ln_g[l, 0], ln_b[l, 0])
        u = modulate(h, mod[:, 1, 0], mod[:, 1, 1])
        y = hybrid_token_mixer(u, w_in[l], conv_a_w[l], conv_a_b[l], norm_a_g[l], norm_a_b[l], w_a_out[l],
                               ssm_conv_w[l], ssm_conv_b[l], ssm_dt_bias[l], ssm_a_log[l], ssm_d[l], ssm_norm_w[l], w_b_out[l],
                               cmp_pe_k[l], cmp_pe_v[l], cmp_k_w1[l], cmp_k_w2[l], cmp_v_w1[l], cmp_v_w2[l], w_c_out[l], w_o[l])
        h = layer_norm(DN_ALPHA * h + mod[:, 1, 2] * y, ln_g[l, 1], ln_b[l, 1])
        u = modulate(h, mod[:, 2, 0], mod[:, 2, 1])
        y = swiglu_ffn(u, ffn_w_gate[l, 1], ffn_w_up[l, 1], ffn_w_down[l, 1])
        h = layer_norm(DN_ALPHA * h + MACARON_WEIGHT * mod[:, 2, 2] * y, ln_g[l, 2], ln_b[l, 2])
    return h


ATT_HEADS = 8
ATT_KV_HEADS = 2
ATT_HEAD_DIM = 64
ATT_GROUP = ATT_HEADS // ATT_KV_HEADS
WINDOW_2 = 128
ATT_BLOCK = 128
ROPE_DIM = ATT_HEAD_DIM // 4
ROPE_THETA_2 = 500000.0
M_HEADS = 4
M_QK_DIM = 64
M_V_DIM = 128
M_CHUNK = 64
D_FF_2 = 4 * D_MODEL
EPS = 1e-6

ATT_Q_W = ATT_HEADS * ATT_HEAD_DIM
ATT_KV_W = ATT_KV_HEADS * ATT_HEAD_DIM
M_QK_W = M_HEADS * M_QK_DIM
M_V_W = M_HEADS * M_V_DIM
IN_WIDTHS = (ATT_Q_W, ATT_KV_W, ATT_KV_W, M_QK_W, M_QK_W, M_V_W, M_V_W, 2 * M_HEADS, 2 * D_MODEL)
D_IN = sum(IN_WIDTHS)


def rmsnorm(x, gain):
    x32 = x.astype(jnp.float32)
    inv = lax.rsqrt(jnp.mean(x32 * x32, axis=-1, keepdims=True) + EPS)
    return (x32 * inv).astype(x.dtype) * gain

def rope_tables(seq_len):
    pos = jnp.arange(seq_len, dtype=jnp.float32)
    inv_freq = ROPE_THETA_2 ** (-jnp.arange(0, ROPE_DIM, 2, dtype=jnp.float32) / ROPE_DIM)
    ang = pos[:, None] * inv_freq[None, :]
    return jnp.cos(ang), jnp.sin(ang)

def partial_rope(x, cos, sin):
    half = ROPE_DIM // 2
    x1 = x[..., :half].astype(jnp.float32)
    x2 = x[..., half:ROPE_DIM].astype(jnp.float32)
    c = cos[None, :, None, :]
    s = sin[None, :, None, :]
    return jnp.concatenate([(x1 * c - x2 * s).astype(x.dtype),
                            (x2 * c + x1 * s).astype(x.dtype),
                            x[..., ROPE_DIM:]], axis=-1)

def sliding_window_attention(q, k, v, sinks):
    B, S, _, hd = q.shape
    nb = S // ATT_BLOCK
    qb = q.reshape(B, nb, ATT_BLOCK, ATT_KV_HEADS, ATT_GROUP, hd)

    def with_prev(t):
        tb = t.reshape(B, nb, ATT_BLOCK, ATT_KV_HEADS, hd)
        prev = jnp.pad(tb, ((0, 0), (1, 0), (0, 0), (0, 0), (0, 0)))[:, :-1]
        return jnp.concatenate([prev, tb], axis=2)

    kb, vb = with_prev(k), with_prev(v)
    scores = jnp.einsum('bnqhgd,bnkhd->bnhgqk', qb, kb).astype(jnp.float32) * (hd ** -0.5)
    blk = jnp.arange(nb)[:, None, None]
    qpos = blk * ATT_BLOCK + jnp.arange(ATT_BLOCK)[None, :, None]
    kpos = (blk - 1) * ATT_BLOCK + jnp.arange(2 * ATT_BLOCK)[None, None, :]
    valid = (kpos >= 0) & (kpos <= qpos) & (qpos - kpos < WINDOW_2)
    scores = jnp.where(valid[None, :, None, None], scores, -jnp.inf)
    sink = sinks.astype(jnp.float32).reshape(ATT_KV_HEADS, ATT_GROUP)[None, None, :, :, None, None]
    m = jnp.maximum(jnp.max(scores, axis=-1, keepdims=True), sink)
    p = jnp.exp(scores - m)
    probs = (p / (jnp.sum(p, axis=-1, keepdims=True) + jnp.exp(sink - m))).astype(v.dtype)
    out = jnp.einsum('bnhgqk,bnkhd->bnqhgd', probs, vb)
    return out.reshape(B, S, ATT_HEADS * hd)

def mlstm_chunkwise(q, k, v, i_pre, f_pre):
    f32 = jnp.float32
    B, S, H, dk = q.shape
    dv = v.shape[-1]
    L = M_CHUNK
    nc = S // L

    def chunks(t):
        return t.astype(f32).reshape(B, nc, L, H, -1).transpose(0, 1, 3, 2, 4)

    q = chunks(q) * (dk ** -0.5)
    k = chunks(k)
    v = chunks(v)
    log_f = jax.nn.log_sigmoid(f_pre.astype(f32)).reshape(B, nc, L, H).transpose(0, 1, 3, 2)
    log_i = i_pre.astype(f32).reshape(B, nc, L, H).transpose(0, 1, 3, 2)
    b = jnp.cumsum(log_f, axis=-1)
    g = b[..., -1]

    w_end = g[..., None] - b + log_i
    m_loc = jnp.max(w_end, axis=-1)
    e = jnp.exp(w_end - m_loc[..., None])
    dC = jnp.einsum('bnhlv,bnhlk->bnhvk', v * e[..., None], k)
    dn = jnp.einsum('bnhl,bnhlk->bnhk', e, k)

    def step(carry, inp):
        C, n, m = carry
        dC_c, dn_c, g_c, m_loc_c = inp
        m_new = jnp.maximum(g_c + m, m_loc_c)
        a = jnp.exp(g_c + m - m_new)
        s = jnp.exp(m_loc_c - m_new)
        C_new = a[..., None, None] * C + s[..., None, None] * dC_c
        n_new = a[..., None] * n + s[..., None] * dn_c
        return (C_new, n_new, m_new), (C, n, m)

    init = (jnp.zeros((B, H, dv, dk), f32), jnp.zeros((B, H, dk), f32), jnp.zeros((B, H), f32))
    xs = (jnp.moveaxis(dC, 1, 0), jnp.moveaxis(dn, 1, 0), jnp.moveaxis(g, 1, 0), jnp.moveaxis(m_loc, 1, 0))
    _, (C_prev, n_prev, m_prev) = lax.scan(step, init, xs)
    C_prev = jnp.moveaxis(C_prev, 0, 1)
    n_prev = jnp.moveaxis(n_prev, 0, 1)
    m_prev = jnp.moveaxis(m_prev, 0, 1)

    causal = jnp.tril(jnp.ones((L, L), dtype=bool))
    log_d = jnp.where(causal, b[..., :, None] - b[..., None, :] + log_i[..., None, :], -jnp.inf)
    log_inter = b + m_prev[..., None]
    m_t = jnp.maximum(log_inter, jnp.max(log_d, axis=-1))
    w = jnp.exp(log_d - m_t[..., None]) * jnp.einsum('bnhlk,bnhsk->bnhls', q, k)
    a_inter = jnp.exp(log_inter - m_t)
    num = jnp.einsum('bnhls,bnhsv->bnhlv', w, v) + a_inter[..., None] * jnp.einsum('bnhvk,bnhlk->bnhlv', C_prev, q)
    den = jnp.sum(w, axis=-1) + a_inter * jnp.einsum('bnhk,bnhlk->bnhl', n_prev, q)
    h = num / jnp.maximum(jnp.abs(den), jnp.exp(-m_t))[..., None]
    return h.transpose(0, 1, 3, 2, 4).reshape(B, S, H, dv)

def hybrid_layer(x, cos, sin, norm_mix, w_in, att_q_norm, att_k_norm, att_sinks, m_gate_bias,
                 m_head_norm, w_att_branch, w_m_branch, w_out, norm_ffn, w_ff1, w_ff2):
    B, S, _ = x.shape
    h = rmsnorm(x, norm_mix)
    z = h @ w_in
    splits = [int(s) for s in np.cumsum(IN_WIDTHS)[:-1]]
    q_a, k_a, v_a, q_m, k_m, v_m, o_m, if_m, gates = jnp.split(z, splits, axis=-1)

    q_a = partial_rope(rmsnorm(q_a.reshape(B, S, ATT_HEADS, ATT_HEAD_DIM), att_q_norm), cos, sin)
    k_a = partial_rope(rmsnorm(k_a.reshape(B, S, ATT_KV_HEADS, ATT_HEAD_DIM), att_k_norm), cos, sin)
    v_a = v_a.reshape(B, S, ATT_KV_HEADS, ATT_HEAD_DIM)
    att = sliding_window_attention(q_a, k_a, v_a, att_sinks)

    i_pre, f_pre = jnp.split(if_m + m_gate_bias, 2, axis=-1)
    hm = mlstm_chunkwise(q_m.reshape(B, S, M_HEADS, M_QK_DIM),
                         k_m.reshape(B, S, M_HEADS, M_QK_DIM),
                         v_m.reshape(B, S, M_HEADS, M_V_DIM), i_pre, f_pre).astype(x.dtype)
    hm = rmsnorm(hm, m_head_norm.reshape(M_HEADS, M_V_DIM)).reshape(B, S, M_V_W)
    hm = hm * jax.nn.sigmoid(o_m)

    g_a, g_m = jnp.split(gates, 2, axis=-1)
    mixed = jax.nn.sigmoid(g_a) * (att @ w_att_branch) + jax.nn.sigmoid(g_m) * (hm @ w_m_branch)
    x = x + mixed @ w_out

    u = jax.nn.relu(rmsnorm(x, norm_ffn) @ w_ff1)
    return x + (u * u) @ w_ff2

def second_inputs(seed: int = 0) -> dict:
    key = jax.random.key(seed)
    ks = jax.random.split(key, 16)
    nrm = jax.random.normal
    f32 = jnp.float32
    x = nrm(ks[0], (BATCH, SEQ, D_MODEL), f32)
    norm_mix = 1.0 + 0.02 * nrm(ks[1], (DEPTH, D_MODEL), f32)
    w_in = nrm(ks[2], (DEPTH, D_MODEL, D_IN), f32) * D_MODEL ** -0.5
    att_q_norm = 1.0 + 0.02 * nrm(ks[3], (DEPTH, ATT_HEAD_DIM), f32)
    att_k_norm = 1.0 + 0.02 * nrm(ks[4], (DEPTH, ATT_HEAD_DIM), f32)
    att_sinks = 0.5 * nrm(ks[5], (DEPTH, ATT_HEADS), f32)
    i_bias = -1.0 + 0.1 * nrm(ks[6], (DEPTH, M_HEADS), f32)
    f_bias = 3.0 + 0.5 * nrm(ks[7], (DEPTH, M_HEADS), f32)
    m_gate_bias = jnp.concatenate([i_bias, f_bias], axis=-1)
    m_head_norm = 1.0 + 0.02 * nrm(ks[8], (DEPTH, M_V_W), f32)
    w_att_branch = nrm(ks[9], (DEPTH, ATT_Q_W, D_MODEL), f32) * ATT_Q_W ** -0.5
    w_m_branch = nrm(ks[10], (DEPTH, M_V_W, D_MODEL), f32) * M_V_W ** -0.5
    w_out = nrm(ks[11], (DEPTH, D_MODEL, D_MODEL), f32) * D_MODEL ** -0.5
    norm_ffn = 1.0 + 0.02 * nrm(ks[12], (DEPTH, D_MODEL), f32)
    w_ff1 = nrm(ks[13], (DEPTH, D_MODEL, D_FF_2), f32) * D_MODEL ** -0.5
    w_ff2 = nrm(ks[14], (DEPTH, D_FF_2, D_MODEL), f32) * D_FF_2 ** -0.5
    return {"x": x, "norm_mix": norm_mix, "w_in": w_in, "att_q_norm": att_q_norm,
            "att_k_norm": att_k_norm, "att_sinks": att_sinks, "m_gate_bias": m_gate_bias,
            "m_head_norm": m_head_norm, "w_att_branch": w_att_branch, "w_m_branch": w_m_branch,
            "w_out": w_out, "norm_ffn": norm_ffn, "w_ff1": w_ff1, "w_ff2": w_ff2}

def second_block(x, norm_mix, w_in, att_q_norm, att_k_norm, att_sinks, m_gate_bias, m_head_norm,
              w_att_branch, w_m_branch, w_out, norm_ffn, w_ff1, w_ff2):
    cos, sin = rope_tables(x.shape[1])
    for layer in range(DEPTH):
        x = hybrid_layer(x, cos, sin, norm_mix[layer], w_in[layer], att_q_norm[layer],
                         att_k_norm[layer], att_sinks[layer], m_gate_bias[layer],
                         m_head_norm[layer], w_att_branch[layer], w_m_branch[layer],
                         w_out[layer], norm_ffn[layer], w_ff1[layer], w_ff2[layer])
    return x


def setup_inputs(seed=0):
    out = dict(first_inputs(seed))
    for name, value in second_inputs(seed + 1).items():
        if name != "x":
            out[name + "_2"] = value
    return out


def reference(
    x, c, ada_w, ada_b, ln_g, ln_b, ffn_w_gate, ffn_w_up, ffn_w_down, w_in, conv_a_w, conv_a_b,
    norm_a_g, norm_a_b, w_a_out, ssm_conv_w, ssm_conv_b, ssm_dt_bias, ssm_a_log, ssm_d,
    ssm_norm_w, w_b_out, cmp_pe_k, cmp_pe_v, cmp_k_w1, cmp_k_w2, cmp_v_w1, cmp_v_w2, w_c_out,
    w_o, norm_mix_2, w_in_2, att_q_norm_2, att_k_norm_2, att_sinks_2, m_gate_bias_2,
    m_head_norm_2, w_att_branch_2, w_m_branch_2, w_out_2, norm_ffn_2, w_ff1_2, w_ff2_2,
):
    x = first_block(
        x, c, ada_w, ada_b, ln_g, ln_b, ffn_w_gate, ffn_w_up, ffn_w_down, w_in, conv_a_w,
        conv_a_b, norm_a_g, norm_a_b, w_a_out, ssm_conv_w, ssm_conv_b, ssm_dt_bias, ssm_a_log,
        ssm_d, ssm_norm_w, w_b_out, cmp_pe_k, cmp_pe_v, cmp_k_w1, cmp_k_w2, cmp_v_w1, cmp_v_w2,
        w_c_out, w_o,
    )
    return second_block(
        x, norm_mix_2, w_in_2, att_q_norm_2, att_k_norm_2, att_sinks_2, m_gate_bias_2,
        m_head_norm_2, w_att_branch_2, w_m_branch_2, w_out_2, norm_ffn_2, w_ff1_2, w_ff2_2,
    )


_drawn_inputs = setup_inputs


def setup_inputs(seed=0):
    import zlib

    import numpy as np

    out = dict(_drawn_inputs(seed))
    spreads = {}
    factors = {'ada_b': 8.0,
     'conv_a_b': 8.0,
     'norm_a_g': 8.0,
     'norm_a_b': 8.0,
     'ssm_conv_b': 8.0,
     'ssm_a_log': 2.668,
     'ssm_d': 6.433,
     'ssm_norm_w': 8.0,
     'cmp_pe_k': 8.0,
     'cmp_pe_v': 8.0,
     'cmp_k_w1': 8.0,
     'cmp_k_w2': 8.0,
     'cmp_v_w1': 4.925,
     'cmp_v_w2': 4.173,
     'norm_mix_2': 3.054,
     'att_q_norm_2': 8.0,
     'att_k_norm_2': 8.0,
     'att_sinks_2': 61.792,
     'm_head_norm_2': 7.019}
    for name, (base, spread) in spreads.items():
        noise = np.random.default_rng([zlib.crc32(name.encode()), seed]).standard_normal(out[name].shape)
        drawn = base * np.exp(spread * noise) if base else spread * noise
        out[name] = __import__('jax').numpy.asarray(drawn.astype(out[name].dtype))
    for name, factor in factors.items():
        out[name] = (out[name] * factor).astype(out[name].dtype)
    return out
```

```python
from contextlib import ExitStack

import numpy as np

import concourse.bass as bass
from concourse import mybir

F32 = mybir.dt.float32
BF16 = mybir.dt.bfloat16
ALU = mybir.AluOpType
ACT = mybir.ActivationFunctionType
AX = mybir.AxisListType.X

P = 128
S = 256
D = 1024
ND = D // P
DEPTH = 2
RING = 12
FF = 2816
NF = FF // P
FF2 = 4096
NF2 = FF2 // P
TAPS_A, TAPS_B = 31, 4
NXB = 16
CMP = 15
ALPHA = (2.0 * DEPTH) ** 0.25
NEG = -1e30

C_ADA = 0
C_FFN0 = C_ADA + 72
C_MIX = C_FFN0 + 3 * NF
C_GLU = C_MIX
C_XBC = C_GLU + 16
C_Z = C_XBC + 16
C_SMALL = C_Z + 8
C_Q = C_SMALL + 1
C_KC = C_Q + 8
C_VC = C_KC + 2
C_KS = C_VC + 2
C_KW = C_KS + 2
C_VS = C_KW + 2
C_VW = C_VS + 2
C_CK = C_VW + 2
C_CV = C_CK + 2
C_OUT = C_CV + 2
C_WO = C_OUT + 48
C_FFN1 = C_WO + 8
N1 = C_FFN1 + 3 * NF

E_Q = 0
E_K = 4
E_V = 5
E_IF = 6
E_QM = 7
E_KM = 9
E_VM = 11
E_OM = 15
E_BR = 19
E_OUT = E_BR + 24
E_FFN = E_OUT + 8
N2 = E_FFN + 2 * NF2


def offsets(parts):
    at, out = 0, {}
    for name, n in parts:
        out[name] = at
        at += n
    out["all"] = at
    return out


PAR1 = offsets([("ada_b", 72), ("ln_g", 24), ("ln_b", 24), ("aw", ND * TAPS_A), ("ab", 8), ("ag", 8), ("abb", 8),
                ("xw", NXB * TAPS_B), ("xb", NXB), ("nw", 8), ("dsk", 8), ("dtb", 1), ("alog", 1),
                ("pek", 16), ("pev", 16), ("w2k", 128), ("w2v", 64)])
PAR2 = offsets([("nmix", 8), ("nffn", 8), ("qn", 1), ("kn", 1), ("sink", 8), ("ib", 1), ("fb", 1), ("hn", 4)])
CON = offsets([("ident", 128), ("mean", 128), ("ones", 128), ("neg", 128), ("tri", 384), ("eps", 1), ("eps2", 1),
               ("valid", 1)])
CON1 = offsets([("rot", 128), ("dup", 256), ("rdup", 256), ("cos", 256), ("sin", 256), ("cmask", 32)])
CON2 = offsets([("blk", 128), ("mean128", 128), ("rot", 128), ("dup", 256), ("band", 128), ("cosq", 256),
                ("sinq", 256), ("cosk", 256), ("sink", 256), ("tri8", 384)])


def constants():
    f = np.float32
    p = np.arange(P)
    con = np.zeros((P, CON["all"]), f)
    def put(a, off, name, v):
        a[:, off[name]:off[name] + v.shape[1]] = v
    put(con, CON, "ident", np.eye(P, dtype=f))
    put(con, CON, "mean", np.full((P, P), 1.0 / D, f))
    put(con, CON, "ones", np.ones((P, P), f))
    put(con, CON, "neg", np.where(p[None, :] > p[:, None], NEG, 0.0))
    tri = (p[:, None] <= p[None, :]).astype(f)
    tri3 = np.concatenate([tri, np.ones((P, P), f), tri], 1)
    put(con, CON, "tri", tri3)
    put(con, CON, "eps", np.full((P, 1), 1e-5, f))
    put(con, CON, "eps2", np.full((P, 1), 1e-6, f))
    put(con, CON, "valid", (p[:, None] >= 31).astype(f))

    con1 = np.zeros((P, CON1["all"]), f)
    rot = np.zeros((P, P), f)
    for m in range(P):
        d = m % 64
        rot[m + 32 if d < 32 else m - 32, m] = -1.0 if d < 32 else 1.0
    dup = np.zeros((2, P, P), f)
    for par in range(2):
        for m in range(P):
            dup[par, par * 64 + m % 64, m] = 1.0
    put(con1, CON1, "rot", rot)
    put(con1, CON1, "dup", np.concatenate([dup[0], dup[1]], 1))
    put(con1, CON1, "rdup", np.concatenate([rot @ dup[0], rot @ dup[1]], 1))
    half = 32
    inv = (10000.0 ** (-np.arange(half, dtype=f) / f(half))).astype(f)
    ang = np.arange(S, dtype=f)[:, None] * inv[None, :]
    put(con1, CON1, "cos", np.tile(np.cos(ang).T, (4, 1)).astype(f))
    put(con1, CON1, "sin", np.tile(np.sin(ang).T, (4, 1)).astype(f))
    t = np.arange(S).reshape(2, P)
    ends = np.arange(16) * 16 + 31
    cm = np.where(ends[None, None, :] <= t[:, :, None], 0.0, NEG)
    put(con1, CON1, "cmask", cm.transpose(1, 0, 2).reshape(P, 32))

    con2 = np.zeros((P, CON2["all"]), f)
    put(con2, CON2, "blk", np.kron(np.eye(2), np.full((64, 64), 1.0 / 64)))
    put(con2, CON2, "mean128", np.full((P, P), 1.0 / P, f))
    rot2 = np.zeros((P, P), f)
    for m in range(P):
        d = m % 64
        if d < 16:
            rot2[m + 8 if d < 8 else m - 8, m] = -1.0 if d < 8 else 1.0
    put(con2, CON2, "rot", rot2)
    put(con2, CON2, "dup", np.concatenate([dup[0], dup[1]], 1))
    put(con2, CON2, "band", np.where(p[None, :] <= p[:, None], NEG, 0.0))
    inv = (f(500000.0) ** (-np.arange(0, 16, 2, dtype=f) / f(16))).astype(f)
    ang = (np.arange(S, dtype=f)[:, None] * inv[None, :]).T
    cos, sin = np.ones((64, S), f), np.zeros((64, S), f)
    cos[0:8] = cos[8:16] = np.cos(ang)
    sin[0:8] = sin[8:16] = np.sin(ang)
    for name, tab, by in (("cosq", cos, 0.125), ("sinq", sin, 0.125), ("cosk", cos, 1.0), ("sink", sin, 1.0)):
        put(con2, CON2, name, np.tile(tab, (2, 1)) * f(by))
    put(con2, CON2, "tri8", tri3 * f(0.125))
    return con, con1, con2


class Stream:

    def __init__(self, per_layer, landed, done):
        self.n, self.landed, self.done = per_layer, landed, done

    def uses(self, slot):
        return (self.n - slot + RING - 1) // RING

    def landed_value(self, l, i, rounds=0):
        return 16 * (l * self.uses(i % RING) + i // RING + 1 + rounds)

    def done_value(self, l, i, rounds=0):
        return l * self.n + i + 1 + RING + rounds * RING

    def last(self, slot):
        return self.n - 1 - (self.n - 1 - slot) % RING


SIGNALS1 = dict(
    layer_done=1, par=16, ada_sum=9, mod_raw=9, u=3, silu=2 * NF, hid=2 * NF, scaled=24, resid=24, mu=4, cent=32,
    sq=40, var=5, sd=5, sg=8, glu=8, copied=23, aconv=8, xconv=16, xsilu=16, kcopy=2, kpe=2, rotp=12, rope=12,
    cmph=1, gelu=1, kc1=1, kcr=1, kc2=1, kcmp=1, vb=1, vbc=1, anrs=8, anorm=8, pv=8, outsg=24, outm=24, dtabs=1, dtexp=1, dtv=1,
    dtt=1, dttc=1, acs=1, acsc=1, xt=4, xdt=4, cb=4, cbm=4, bc=16, ee=16, arg=16, mm=16, yh=16, yb=8, ysil=8, bnorm=8,
    cs=2, cmx=2, cex=2, cp=2, ct=2, ptc=2, sc=16, nmx=16, ex=16, pr=16, tr=16, ptt=16, ov=4, oc=4, bias_a=1)
SIGNALS2 = dict(
    layer_done=1, par=16, usq=16, uvar=2, usd=2, u=2, copied=11, hsq=4, hvar=9, hsd=9, qn=5, rotp=5, rope=5, dup=1,
    dupc=1, fexp=1, mt=1, rt=1, mtc=1, qk=4, qkm=4, bc=4, me=4, arg=4, ee=4, mm=4, num=4, absd=4, hh=4, hm=4,
    sc=4, nmx=4, ex=4, pr=4, tr=4, ptt=4, pv=4, oc=2, outsg=8, outm=8, relu=NF2, hid=NF2, xres=8)


class Buffers:
    pass


def memory(nc, ctx):
    def sb(name, n, dt=F32):
        return ctx.enter_context(nc.sbuf_tensor(name, [P, n], dt))
    m = Buffers()
    def tiles(a, n):
        return a.rearrange("p (n t) -> p n t", n=n)
    m.ring = sb("ring", RING * 1024)
    m.h = tiles(sb("h", ND * S)[:], ND)
    m.u = tiles(sb("u", ND * S)[:], ND)
    eb = sb("eb", 2048)
    pt = sb("pt", 4096)
    ap_ = sb("ap", ND * (S + TAPS_A - 1))
    ac = sb("ac", ND * S)
    xp = sb("xp", NXB * (S + TAPS_B - 1))
    xc = sb("xc", NXB * S)
    z = sb("z", ND * S)
    qr = sb("qr", ND * S)
    kv = sb("kv", 2048)
    kraw = sb("kraw", 1024)
    kr = sb("kr", 2048)
    vt = sb("vt", 1024)
    gr = sb("gr", 512)
    vb = sb("vb", 1024)
    small = sb("small", 512)
    sg = sb("sg", 1024)
    st = sb("st", 512)
    m.con = sb("con", CON["all"])
    m.con_of = lambda name, n=P, at=0: m.con[:, CON[name] + at:CON[name] + at + n]
    m.conb = sb("conb", max(CON1["all"], CON2["all"]))
    m.par = sb("par", PAR1["all"])
    m.cvec = sb("cvec", 16)
    m.mod = sb("mod", 72)
    m.sc1 = sb("sc1", 24)
    m.zero = sb("zero", 512, BF16)

    m.eb, m.pt = eb, pt
    m.ada = [eb[:, 0:1024], eb[:, 1024:2048]]
    m.sq = tiles(eb[:], ND)
    m.silu = tiles(pt[:, 0:1024], 4)
    m.hid = tiles(pt[:, 1024:2048], 4)
    m.apad = tiles(ap_[:], ND)
    m.merged = tiles(ap_[:, 0:ND * S], ND)
    m.ac = tiles(ac[:], ND)
    m.oT = m.ac
    m.xpad = tiles(xp[:], NXB)
    m.xdt = xp[:, 0:2048].rearrange("p (a f) -> p a f", a=2)
    m.yb = tiles(xp[:, 2048:4096], ND)
    m.xc = tiles(xc[:], NXB)
    m.pcmp = xc[:, 0:1024].rearrange("p (a h n) -> p a h n", a=2, h=16)
    m.ptc = xc[:, 1024:2048].rearrange("p (g t) -> p g t", g=4)
    m.z = tiles(z[:], ND)
    m.qr = tiles(qr[:], ND)
    m.kc = kv[:, 0:1024].rearrange("p (g t) -> p g t", g=4)
    m.vc = kv[:, 1024:2048].rearrange("p (g t) -> p g t", g=4)
    m.kp = [eb[:, 0:960].rearrange("p (j c) -> p j c", j=16), eb[:, 1024:1984].rearrange("p (j c) -> p j c", j=16)]
    m.kraw = kraw[:].rearrange("p (b n t) -> p b n t", b=2, n=2)
    m.kr = kr[:].rearrange("p (b g t) -> p b g t", b=2, g=4)
    m.vt = vt[:].rearrange("p (b a f) -> p b a f", b=2, a=2)
    m.gr = gr[:].rearrange("p (g r n) -> p g r n", g=4, r=4)
    m.vb = vb[:].rearrange("p (g i f) -> p g i f", g=4, i=2)
    m.gk = small[:, 0:60]
    m.kcr = small[:, 60:120]
    m.kcmp = small[:, 120:180]
    m.gates = small[:, 180:276].rearrange("p (a c) -> p a c", a=2)
    m.dtt = small[:, 276:340]
    m.nacs = small[:, 340:372]
    m.cst = small[:, 372:436].rearrange("p (k a h) -> p k a h", k=2, a=2)
    m.nmx = small[:, 436:444].rearrange("p (b r) -> p b r", b=2)
    m.sums = small[:, 444:452].rearrange("p (b r) -> p b r", b=2)
    m.fac = small[:, 452:460].rearrange("p (b r) -> p b r", b=2)
    m.esink = small[:, 460:468].rearrange("p (b r) -> p b r", b=2)
    m.aexp = small[:, 468:469]
    m.dtw = kv[0:16, 0:1280].rearrange("p (k t) -> p k t", k=5)
    m.cbm = kv[:, 1280:2048].rearrange("p (b t) -> p b t", b=2)
    m.dtraw = pt[0:16, 2048:2304]
    m.sg = tiles(sg[:], 4)
    m.sd, m.rs = st[:, 0:256], st[:, 256:512]
    m.ee = pt[:, 0:768].rearrange("p (b t) -> p b t", b=2)
    m.mm = pt[:, 768:1536].rearrange("p (b t) -> p b t", b=2)
    m.e = eb[:].rearrange("p (b r k) -> p b r k", b=2, r=4)
    m.ptt = pt[:].rearrange("p (b k r q) -> p b k r q", b=4, k=2, r=4)
    m.qk_raw = [ac[:, i * 256:(i + 1) * 256] for i in range(5)]
    m.hsq = [eb[:, i * 256:(i + 1) * 256] for i in range(5)]
    m.tmp = [sg[:, 0:256], sg[:, 256:512]]
    m.qa = tiles(qr[:, 0:1024], 4)
    m.qm = qr[:, 1024:1536].rearrange("p (n t) -> p n t", n=2)
    m.km = qr[:, 1536:2048].rearrange("p (n t) -> p n t", n=2)
    m.ka = kr[:, 0:512].rearrange("p (g t) -> p g t", g=2)
    m.kda = kr[:, 512:768]
    m.va = vt[:, 0:256].rearrange("p (a f) -> p a f", a=2)
    m.vm = xc[:, 0:1024].rearrange("p (a f) -> p a f", a=2)
    m.om = tiles(xc[:, 1024:2048], 4)
    m.ow = kv[0:4, 0:2048].rearrange("p (k t) -> p k t", k=8)
    m.att = tiles(z[:, 0:1024], 4)
    m.hm = tiles(z[:, 1024:2048], 4)
    m.rt = small[:, 0:8].rearrange("p (a h) -> p a h", a=2)
    m.qkm = xc[:, 2048:2816].rearrange("p (b t) -> p b t", b=2)
    m.em = xc[:, 2816:3328].rearrange("p (b t) -> p b t", b=2)
    m.den = xc[:, 3328:3840].rearrange("p (b t) -> p b t", b=2)
    m.mx = small[:, 8:16].rearrange("p (b r) -> p b r", b=2)
    m.ps = ctx.enter_context(nc.psum_tensor("ps", [P, 8, 512], F32))
    return m


def chunk_tile(m, i, k, a=0, b=P):
    at = (i % RING) * 1024 + k * P
    return m.ring[:, at + a:at + b]


def two(ps, bank, a=0, n=256):
    return ps[:, bank, a:a + 2 * n].rearrange("p (n t) -> p n t", n=2)



def stream_weights(sp, m, source, stream, earlier=None):
    def load(l, i, rounds=0):
        src = source[bass.ds(l * stream.n + i + rounds * RING, 1)].rearrange("a p n -> (a p) n")
        at = (i % RING) * 1024
        sp.dma_start(m.ring[:, at:at + 1024], src).then_inc(stream.landed[i % RING], 16)

    whole = stream.n // RING
    with sp.Fori(0, DEPTH) as l:
        for s in range(RING):
            if earlier:
                sp.wait_ge(earlier.done, earlier.done_value(DEPTH - 1, earlier.last(s)))
            sp.wait_ge(stream.done, l * stream.n + stream.last(s) - stream.n + 1 + RING)
            load(l, s)
        with sp.Fori(0, whole - 1) as it:
            for s in range(RING):
                sp.wait_ge(stream.done, stream.done_value(l, s, it))
                load(l, RING + s, it)
        for i in range(whole * RING, stream.n):
            sp.wait_ge(stream.done, stream.done_value(l, i - RING))
            load(l, i)



def tensor1(nc, t, m, sem, stream):
    ps, con = m.ps, m.con_of
    landed, done = stream.landed, stream.done
    mm = nc.tensor.matmul

    def layer(l):
        at = lambda name, k: l * SIGNALS1[name] + k
        landed_at = lambda i, rounds=0: stream.landed_value(l, i, rounds)
        done_at = lambda i, rounds=0: stream.done_value(l, i, rounds)
        c1 = lambda name, n=P, at=0: m.conb[:, CON1[name] + at:CON1[name] + at + n]

        def project(i, out, k0=0, rounds=0, cols=(0, P)):
            t.wait_ge(landed[i % RING], landed_at(i, rounds))
            for k in range(ND):
                last = mm(out, chunk_tile(m, i, k, *cols), m.u[:, k], start=k == 0, stop=k == ND - 1)
            return last

        def accumulate_ones(bank, src, signal, k0, ones):
            for n in range(ND):
                t.wait_ge(sem[signal], at(signal, k0 + n + 1))
                last = mm(ps[:, bank, 0:S], ones, src[:, n], start=n == 0, stop=n == ND - 1)
            return last

        def layer_norm(at, src, sq, mu_bank, var_bank, resid_k):
            accumulate_ones(mu_bank, src, resid_k[0], resid_k[1], con("mean")).then_inc(sem["mu"], 1)
            rms(at[0], sq, var_bank)

        def rms(k, sq, bank):
            accumulate_ones(bank, sq, "sq", 8 * k, con("mean")).then_inc(sem["var"], 1)

        def ffn(q, cb):
            for b in range(4):
                mm(ps[:, b, :], m.zero[:, 0:P], m.zero[:], start=True, stop=False, skip_group_check=True)

            def up(i, f, rounds=0):
                project(i, ps[:, 4 + f % 4, 0:S], rounds=rounds).then_inc(done, 1)
                project(i + 1, ps[:, 4 + f % 4, S:2 * S], rounds=rounds).then_inc(done, 1)

            def down(i, f, fk, rounds=0, last=False):
                t.wait_ge(landed[i % RING], landed_at(i, rounds))
                t.wait_ge(sem["hid"], at("hid", q * NF + fk + 1))
                for n in range(ND):
                    x = mm(ps[:, n // 2, (n % 2) * S:(n % 2 + 1) * S], chunk_tile(m, i, n), m.hid[:, f % 4],
                           start=False, stop=last, skip_group_check=True)
                x.then_inc(done, 1)

            up(cb, 0)
            with t.Fori(0, 5) as it:
                for j in range(4):
                    up(cb + 2 + 3 * j, 1 + j, it)
                    down(cb + 4 + 3 * j, j, 4 * it + j, it)
            up(cb + 62, 21)
            down(cb + 64, 20, 20)
            down(cb + 65, 21, 21, last=True)

        for cg in range(9):
            t.wait_ge(sem["ada_sum"], at("ada_sum", cg + 1))
            for j in range(8):
                last = mm(ps[:, 0, cg * 8 + j:cg * 8 + j + 1], m.ada[cg % 2][:, j * P:(j + 1) * P],
                          con("ones", 1), start=True, stop=True)
            last.then_inc(sem["mod_raw"], 1)

        t.wait_ge(sem["u"], at("u", 1))
        ffn(0, C_FFN0)
        layer_norm((0,), m.h, m.u, 4, 5, ("resid", 0))

        t.wait_ge(sem["u"], at("u", 2))
        unit = lambda j: 4 + j % 4
        j = 0
        for n in range(8):
            if n >= 4:
                t.wait_ge(sem["glu"], at("glu", n - 3))
            project(C_GLU + 2 * n, ps[:, unit(j), 0:S]).then_inc(done, 1)
            project(C_GLU + 2 * n + 1, ps[:, unit(j), S:2 * S]).then_inc(done, 1)
            j += 1
        for n in range(12):
            if n < 4:
                t.wait_ge(sem["glu"], at("glu", n + 5))
            else:
                t.wait_ge(sem["copied"], at("copied", n - 3))
            project(C_XBC + 2 * n, ps[:, unit(j), 0:S]).then_inc(done, 1)
            project(C_XBC + 2 * n + 1, ps[:, unit(j), S:2 * S]).then_inc(done, 1)
            j += 1
        t.wait_ge(sem["copied"], at("copied", 9))
        t.wait_ge(landed[C_SMALL % RING], landed_at(C_SMALL))
        for a in range(2):
            for k in range(ND):
                mm(ps[:, unit(j), a * 48:a * 48 + 48], m.u[:, k, a * P:(a + 1) * P],
                   chunk_tile(m, C_SMALL, k, 0, 48), start=k == 0, stop=k == ND - 1)
        for k in range(ND):
            last = mm(ps[0:16, unit(j), S:2 * S], chunk_tile(m, C_SMALL, k, 64, 80), m.u[:, k],
                      start=k == 0, stop=k == ND - 1)
        last.then_inc(done, 1)
        j += 1
        for n in range(8):
            t.wait_ge(sem["copied"], at("copied", 10 + n))
            project(C_Q + 2 * n, ps[:, unit(j), 0:S]).then_inc(done, 1)
            project(C_Q + 2 * n + 1, ps[:, unit(j), S:2 * S]).then_inc(done, 1)
            j += 1
        for b in range(2):
            t.wait_ge(sem["copied"], at("copied", 18 + b))
            for c in range(2):
                i = C_VS + 2 * b + c
                t.wait_ge(landed[i % RING], landed_at(i))
                for a in range(2):
                    for k in range(ND):
                        last = mm(ps[:, unit(j), a * S + c * P:a * S + (c + 1) * P], m.u[:, k, a * P:(a + 1) * P],
                                  chunk_tile(m, i, k), start=k == 0, stop=k == ND - 1)
                last.then_inc(done, 1)
            j += 1
        for n in range(4):
            t.wait_ge(sem["copied"], at("copied", 20 + n))
            for c in range(2):
                last = mm(ps[:, unit(j), c * S:(c + 1) * S], c1("rot"), m.qr[:, 2 * n + c], start=True, stop=True)
            last.then_inc(sem["rotp"], 1)
            j += 1
        for b in range(2):
            for g in range(4):
                t.wait_ge(sem["rope"], at("rope", 4 * b + g + 1))
                src = m.kraw[:, b, g // 2]
                mm(ps[:, unit(j), 0:S], c1("dup", P, (g % 2) * P), src, start=True, stop=True)
                mm(ps[:, unit(j), S:2 * S], c1("rdup", P, (g % 2) * P), src, start=True, stop=True)\
                    .then_inc(sem["rotp"], 1)
                j += 1
        t.wait_ge(sem["rope"], at("rope", 9))
        for b in range(2):
            t.wait_ge(sem["kpe"], at("kpe", b + 1))
            for c in range(2):
                i = C_CK + 2 * b + c
                t.wait_ge(landed[i % RING], landed_at(i))
                for k in range(8):
                    last = mm(ps[:, unit(j), b * 64:b * 64 + 60], chunk_tile(m, i, k), m.kp[b][:, 8 * c + k],
                              start=c == 0 and k == 0, stop=c == 1 and k == 7)
                last.then_inc(done, 1)
        j += 1
        t.wait_ge(sem["rope"], at("rope", 10))
        t.wait_ge(sem["gelu"], at("gelu", 1))
        mm(ps[:, unit(j), 0:60], m.par[:, PAR1["w2k"]:PAR1["w2k"] + P], m.gk, start=True, stop=True)\
            .then_inc(sem["kc1"], 1)
        j += 1
        t.wait_ge(sem["rope"], at("rope", 11))
        t.wait_ge(sem["kcr"], at("kcr", 1))
        mm(ps[:, unit(j), 0:60], c1("rot"), m.kcr, start=True, stop=True).then_inc(sem["kc2"], 1)
        j += 1
        t.wait_ge(sem["rope"], at("rope", 12))
        for g in range(4):
            last = mm(ps[:, unit(j), g * 64:(g + 1) * 64], m.gr[:, g].rearrange("p r n -> p (r n)"),
                      m.par[:, PAR1["w2v"]:PAR1["w2v"] + 64], start=True, stop=True)
        last.then_inc(sem["vb"], 1)
        j += 1

        layer_norm((1,), m.ac, m.sq, 0, 1, ("aconv", 0))

        def out_tile(branch, src, n, j):
            i = C_OUT + 16 * branch + 2 * n
            project(i, ps[:, unit(j), 0:S]).then_inc(done, 1)
            if n == 0 and branch == 0:
                t.wait_ge(sem["anorm"], at("anorm", 8))
            if n == 0 and branch == 1:
                t.wait_ge(sem["bnorm"], at("bnorm", 8))
            if n == 0 and branch == 2:
                t.wait_ge(sem["oc"], at("oc", 4))
            t.wait_ge(landed[(i + 1) % RING], landed_at(i + 1))
            for k in range(ND):
                last = mm(ps[:, unit(j), S:2 * S], chunk_tile(m, i + 1, k), src[:, k], start=k == 0, stop=k == 7)
            last.then_inc(done, 1)
            return j + 1

        t.wait_ge(sem["gelu"], at("gelu", 1))
        j = out_tile(0, m.ac, 0, j)
        t.wait_ge(sem["kcr"], at("kcr", 1))
        j = out_tile(0, m.ac, 1, j)
        t.wait_ge(sem["kcmp"], at("kcmp", 1))
        j = out_tile(0, m.ac, 2, j)
        t.wait_ge(sem["vbc"], at("vbc", 1))
        j = out_tile(0, m.ac, 3, j)
        for n in range(4, 8):
            t.wait_ge(sem["outm"], at("outm", n - 3))
            j = out_tile(0, m.ac, n, j)

        ident16 = m.con[0:16, CON["ident"]:CON["ident"] + 16]
        t.wait_ge(sem["outm"], at("outm", 5))
        t.wait_ge(sem["dtv"], at("dtv", 1))
        for k in range(4):
            last = mm(ps[:, unit(j), 16 * k:16 * k + 16], m.dtw[:, 3 + k // 2, (k % 2) * P:(k % 2 + 1) * P],
                      ident16, start=True, stop=True)
        last.then_inc(sem["dtt"], 1)
        j += 1
        t.wait_ge(sem["outm"], at("outm", 6))
        t.wait_ge(sem["dttc"], at("dttc", 1))
        tri, ones = con("tri"), con("ones")
        adt = [m.dtt[:, 32:48], m.dtt[:, 48:64]]
        b = unit(j)
        mm(ps[:, b, 0:16], tri, adt[0], start=True, stop=True)
        mm(ps[:, b, 16:32], ones, adt[0], start=True, stop=False)
        mm(ps[:, b, 16:32], tri, adt[1], start=False, stop=True)
        mm(ps[0:16, b, 256:512], adt[0], con("tri", 256), start=True, stop=False)
        mm(ps[0:16, b, 384:512], adt[1], tri, start=False, stop=True).then_inc(sem["acs"], 1)
        j += 1
        for h in range(4):
            if h < 2:
                t.wait_ge(sem["outm"], at("outm", 7 + h))
            elif h == 2:
                t.wait_ge(sem["dttc"], at("dttc", 1))
            else:
                t.wait_ge(sem["acsc"], at("acsc", 1))
            t.wait_ge(sem["xsilu"], at("xsilu", 8))
            for n in range(4):
                f = 4 * (h % 2) + n
                last = nc.tensor.transpose(ps[:, unit(j), n * P:(n + 1) * P],
                                           m.xc[:, f, (h // 2) * P:(h // 2 + 1) * P], con("ident"))
            last.then_inc(sem["xt"], 1)
            j += 1
        def ssm_head(h):
            t.wait_ge(sem["mm"], at("mm", h + 1))
            out = ps[64 * (h % 2):64 * (h % 2) + 64, h // 4, ((h // 2) % 2) * S:((h // 2) % 2 + 1) * S]
            x = m.xdt[:, :, 64 * h:64 * h + 64]
            mm(out, x[:, 0], m.mm[:, h % 2, 0:S], start=True, stop=False)
            mm(out[:, P:S], x[:, 1], m.mm[:, h % 2, S:S + P], start=False, stop=True).then_inc(sem["yh"], 1)

        t.wait_ge(sem["xsilu"], at("xsilu", 16))
        t.wait_ge(sem["acsc"], at("acsc", 1))
        for g in range(4):
            if g == 0:
                t.wait_ge(sem["xdt"], at("xdt", 1))
            else:
                t.wait_ge(sem["arg"], at("arg", 4 * g - 3))
            B, C = m.xc[:, 8 + g], m.xc[:, 12 + g]
            mm(ps[:, unit(j), 0:256], B[:, 0:P], C, start=True, stop=True)
            mm(ps[:, unit(j), 256:384], B[:, P:S], C[:, P:S], start=True, stop=True).then_inc(sem["cb"], 1)
            j += 1
            for r in range(4):
                h = 4 * g + r
                if r == 3:
                    t.wait_ge(sem["cbm"], at("cbm", g + 1))
                elif g == 0:
                    t.wait_ge(sem["xdt"], at("xdt", r + 2))
                else:
                    t.wait_ge(sem["arg"], at("arg", 4 * g - 2 + r))
                mm(ps[:, unit(j), 0:S], m.con[0:16, CON["ident"] + h:CON["ident"] + h + 1].to_broadcast([16, P]),
                   m.dtw[:, 2], start=True, stop=True).then_inc(sem["bc"], 1)
                j += 1
                if h >= 1:
                    ssm_head(h - 1)
        ssm_head(15)
        rms(2, m.sq, 4)
        for n in range(8):
            if n < 4:
                t.wait_ge(sem["arg"], at("arg", 13 + n))
            else:
                t.wait_ge(sem["outm"], at("outm", 5 + n))
            j = out_tile(1, m.yb, n, j)

        kcmp = m.kcmp.rearrange("p (g n) -> p g n", g=4)
        for a in range(2):
            t.wait_ge(sem["outm"], at("outm", 14 + 2 * a))
            for h in range(16):
                lo = 64 * (h % 2)
                o = (h // 2) * 16
                last = mm(ps[:, unit(j + h % 2), o:o + CMP], m.qr[lo:lo + 64, h // 2, a * P:(a + 1) * P],
                          kcmp[lo:lo + 64, h // 4], start=True, stop=True)
            last.then_inc(sem["cs"], 1)
            j += 2
        for k in range(2):
            t.wait_ge(sem["cmx"], at("cmx", 1))
            t.wait_ge(sem["cp"], at("cp", 2))
            for g in (2 * k, 2 * k + 1):
                for a in range(2):
                    last = nc.tensor.transpose(ps[:, unit(j), (g % 2) * S + a * P:(g % 2) * S + (a + 1) * P],
                                               m.pcmp[:, a, 4 * g:4 * g + 4].rearrange("p r n -> p (r n)"),
                                               con("ident"))
            last.then_inc(sem["ct"], 1)
            j += 1

        def scores(i):
            g, a, b = i // 4, (i // 2) % 2, i % 2
            kl = P * (a + 1)
            if i >= 2:
                t.wait_ge(sem["ex"], at("ex", i - 1))
            for r in range(4):
                h = 4 * g + r
                lo = 64 * (h % 2)
                last = mm(score_view(ps, i, a)[:, place_of(r)], m.qr[lo:lo + 64, h // 2, a * P:(a + 1) * P],
                          m.kr[lo:lo + 64, b, g, 0:kl], start=True, stop=True)
            last.then_inc(sem["sc"], 1)

        def turn(i):
            a = (i // 2) % 2
            t.wait_ge(sem["pr"], at("pr", i + 1))
            if i >= 1:
                t.wait_ge(sem["ptt"], at("ptt", i))
            for k in range(a + 1):
                for r in range(4):
                    last = nc.tensor.transpose(ps[:, 2 + k, r * P:(r + 1) * P], m.e[:, i % 2, r, k * P:(k + 1) * P],
                                               con("ident"))
            last.then_inc(sem["tr"], 1)

        def values(i2):
            g, a = i2 // 2, i2 % 2
            o = ps[:, g % 2, :].rearrange("p (i t) -> p i t", i=2)
            if a == 0:
                if g >= 2:
                    t.wait_ge(sem["oc"], at("oc", g - 1))
                for i in range(2):
                    mm(o[:, i], m.vb[:, g, i], m.ptc[:, g], start=i == 0, stop=False, skip_group_check=True)
            t.wait_ge(sem["ptt"], at("ptt", 2 * i2 + 2))
            for b in range(2):
                for k in range(a + 1):
                    for par in range(2):
                        last = mm(o[64 * par:64 * par + 64, :, a * P:(a + 1) * P],
                                  m.vt[:, b, k, g * 64:(g + 1) * 64],
                                  m.ptt[:, (2 * i2 + b) % 4, k, 2 * par:2 * par + 2], start=False, stop=a == 1 and b == 1 and k == 1,
                                  skip_group_check=True)
            last.then_inc(sem["pv"], 1)

        t.wait_ge(sem["ptc"], at("ptc", 2))
        scores(0)
        for i in range(16):
            if i + 1 < 16:
                scores(i + 1)
            turn(i)
            if i >= 2 and i % 2 == 0:
                values(i // 2 - 1)
        values(7)
        for n in range(8):
            if n < 4:
                t.wait_ge(sem["ptc"], at("ptc", 2))
            else:
                t.wait_ge(sem["outm"], at("outm", 13 + n))
            j = out_tile(2, m.oT, n, j)

        t.wait_ge(sem["outm"], at("outm", 24))
        for n in range(8):
            if n >= 4:
                t.wait_ge(sem["scaled"], at("scaled", 5 + n))
            t.wait_ge(landed[(C_WO + n) % RING], landed_at(C_WO + n))
            for k in range(ND):
                last = mm(ps[:, unit(j), 0:S], chunk_tile(m, C_WO + n, k), m.merged[:, k], start=k == 0, stop=k == 7)
            last.then_inc(done, 1)
            j += 1
        layer_norm((3,), m.h, m.u, 0, 1, ("resid", 8))

        t.wait_ge(sem["u"], at("u", 3))
        ffn(1, C_FFN1)
        layer_norm((4,), m.h, m.u, 4, 5, ("resid", 16))

    with t.Fori(0, DEPTH) as l:
        layer(l)


def place_of(r):
    return (r % 2) * 2 + r // 2


def score_view(ps, i, a):
    b = 4 + 2 * (i % 2)
    return ps[:, b:b + 2, :].rearrange("p b (r k) -> p (b r) k", r=2)[:, :, 0:P * (a + 1)]





def scalar1(nc, a, m, sem, stream, par_source):
    ps, con = m.ps, m.con_of
    landed, done = stream.landed, stream.done
    act = nc.scalar.activation

    def layer(l):
        at = lambda name, k: l * SIGNALS1[name] + k
        landed_at = lambda i, rounds=0: stream.landed_value(l, i, rounds)
        done_at = lambda i, rounds=0: stream.done_value(l, i, rounds)
        par = lambda name, at=0, n=1: m.par[:, PAR1[name] + at:PAR1[name] + at + n]
        gate = lambda i, n: m.mod[:, (3 * i + 2) * 8 + n:(3 * i + 2) * 8 + n + 1]
        bank = lambda j: 4 + j % 4

        a.wait_ge(sem["layer_done"], at("layer_done", 1))
        a.dma_start(m.par[:], par_source[bass.ds(l, 1)].rearrange("a p n -> (a p) n")).then_inc(sem["par"], 16)

        def ffn(q, cb):
            def silu(i, f, rounds=0):
                a.wait_ge(done, done_at(i, rounds))
                act(m.silu[:, f % 4], ps[:, 4 + f % 4, 0:S], ACT.Silu).then_inc(sem["silu"], 1)
            silu(cb + 1, 0)
            with a.Fori(0, 5) as it:
                for j in range(4):
                    silu(cb + 3 + 3 * j, 1 + j, it)
            silu(cb + 63, 21)
            a.wait_ge(done, done_at(cb + 65))
            for n in range(ND):
                act(m.u[:, n], ps[:, n // 2, (n % 2) * S:(n % 2 + 1) * S], ACT.Identity, scale=gate(2 * q, n))\
                    .then_inc(sem["scaled"], 1)

        def squares(k, src, dst, signal, k0, var_bank):
            for n in range(ND):
                a.wait_ge(sem[signal], at(signal, k0 + n + 1))
                act(dst[:, n], src[:, n], ACT.Square).then_inc(sem["sq"], 1)
            a.wait_ge(sem["var"], at("var", k + 1))
            act(m.sd, ps[:, var_bank, 0:S], ACT.Sqrt, bias=con("eps", 1)).then_inc(sem["sd"], 1)

        ffn(0, C_FFN0)
        squares(0, m.h, m.u, "cent", 0, 5)

        j = 0
        for n in range(8):
            a.wait_ge(done, done_at(C_GLU + 2 * n + 1))
            if n >= 4:
                a.wait_ge(sem["glu"], at("glu", n - 3))
            act(m.sg[:, n % 4], ps[:, bank(j), S:2 * S], ACT.Sigmoid).then_inc(sem["sg"], 1)
            j += 1
        copied = sem["copied"]
        for n in range(8):
            a.wait_ge(done, done_at(C_XBC + 2 * n + 1))
            act(m.xpad[:, 2 * n:2 * n + 2, TAPS_B - 1:], two(ps, bank(j)), ACT.Copy).then_inc(copied, 1)
            j += 1
        for n in range(4):
            a.wait_ge(done, done_at(C_Z + 2 * n + 1))
            act(m.z[:, 2 * n:2 * n + 2], two(ps, bank(j)), ACT.Silu).then_inc(copied, 1)
            j += 1
        a.wait_ge(done, done_at(C_SMALL))
        act(m.gates, two(ps, bank(j), 0, 48), ACT.Sigmoid)
        act(m.dtraw, ps[0:16, bank(j), S:2 * S], ACT.Identity, bias=par("dtb")[0:16]).then_inc(copied, 1)
        j += 1
        for n in range(4):
            a.wait_ge(done, done_at(C_Q + 2 * n + 1))
            act(m.qr[:, 2 * n:2 * n + 2], two(ps, bank(j)), ACT.Copy, scale=0.125).then_inc(copied, 1)
            j += 1
        for b, dst in enumerate((m.kc, m.vc)):
            a.wait_ge(done, done_at(C_KC + 2 * b + 1))
            for par_ in range(2):
                for nxt in range(2):
                    last = act(dst[64 * nxt:64 * nxt + 64, par_::2, 0:S - nxt],
                               two(ps[64 * par_:64 * par_ + 64], bank(j))[:, :, nxt:S], ACT.Copy)
            last.then_inc(copied, 1)
            j += 1
        for b in range(2):
            a.wait_ge(done, done_at(C_KS + 2 * b + 1))
            act(m.kraw[:, b], two(ps, bank(j)), ACT.Copy).then_inc(copied, 1)
            j += 1
        for b in range(2):
            a.wait_ge(done, done_at(C_VS + 2 * b + 1))
            act(m.vt[:, b], two(ps, bank(j)), ACT.Copy).then_inc(copied, 1)
            j += 1
        for n in range(NXB):
            a.wait_ge(sem["xconv"], at("xconv", n + 1))
            act(m.xc[:, n], m.xc[:, n], ACT.Silu).then_inc(sem["xsilu"], 1)
        j += 12
        a.wait_ge(done, done_at(C_CV + 1))
        act(m.gk, ps[:, bank(j), 0:60], ACT.Gelu_apprx_tanh)
        for r in range(4):
            last = act(m.gr[:, :, r, 0:CMP], ps[:, bank(j), 64:124].rearrange("p (g n) -> p g n", g=4),
                       ACT.Gelu_apprx_tanh)
        last.then_inc(sem["gelu"], 1)
        j += 1
        a.wait_ge(sem["kc1"], at("kc1", 1))
        act(m.kcr, ps[:, bank(j), 0:60], ACT.Copy).then_inc(sem["kcr"], 1)
        j += 3

        act(m.dtw[:, 0], m.dtraw, ACT.Abs)
        act(m.aexp[0:16], par("alog")[0:16], ACT.Exp)
        a.drain()
        act(m.dtw[:, 1], m.dtw[:, 0], ACT.Exp, scale=-1.0).then_inc(sem["dtexp"], 1)

        squares(1, m.ac, m.sq, "cent", 8, 1)
        for n in range(ND):
            a.wait_ge(sem["anrs"], at("anrs", n + 1))
            act(m.ac[:, n], m.ac[:, n], ACT.Silu, scale=par("ag", n), bias=par("abb", n)).then_inc(sem["anorm"], 1)

        def out_gates(branch, j):
            for n in range(8):
                a.wait_ge(done, done_at(C_OUT + 16 * branch + 2 * n + 1))
                k = 8 * branch + n
                if k >= 4:
                    a.wait_ge(sem["outm"], at("outm", k - 3))
                act(m.sg[:, n % 4], ps[:, bank(j), 0:S], ACT.Sigmoid).then_inc(sem["outsg"], 1)
                j += 1
            return j

        j = out_gates(0, j)

        j += 1
        a.wait_ge(sem["acs"], at("acs", 1))
        act(m.nacs, ps[:, bank(j), 0:32], ACT.Copy, scale=-1.0)
        act(m.dtw[:, 2], ps[0:16, bank(j), S:2 * S], ACT.Copy).then_inc(sem["acsc"], 1)
        j += 5
        for h in range(16):
            a.wait_ge(sem["arg"], at("arg", h + 1))
            act(m.ee[:, h % 2], m.ee[:, h % 2], ACT.Exp).then_inc(sem["ee"], 1)
        j += 20
        squares(2, m.yb, m.sq, "ysil", 0, 4)
        j = out_gates(1, j)

        for k in range(2):
            a.wait_ge(sem["cmx"], at("cmx", k + 1))
            act(m.pcmp[:, k, :, 0:CMP], m.pcmp[:, k, :, 0:CMP], ACT.Exp).then_inc(sem["cex"], 1)
        j += 4
        for k in range(2):
            a.wait_ge(sem["ct"], at("ct", k + 1))
            act(m.ptc[:, 2 * k:2 * k + 2], two(ps, bank(j)), ACT.Copy).then_inc(sem["ptc"], 1)
            j += 1

        def exps(i):
            k = (i // 2) % 2
            a.wait_ge(sem["nmx"], at("nmx", i + 1))
            if i >= 2:
                a.wait_ge(sem["tr"], at("tr", i - 1))
            for r in range(4):
                last = act(m.e[:, i % 2, r, 0:P * (k + 1)], score_view(ps, i, k)[:, r], ACT.Exp,
                           bias=m.nmx[:, i % 2, r:r + 1], accum_out=m.sums[:, i % 2, r:r + 1])
            last.then_inc(sem["ex"], 1)

        def turned(i):
            k = (i // 2) % 2
            a.wait_ge(sem["tr"], at("tr", i + 1))
            if i >= 4:
                a.wait_ge(sem["pv"], at("pv", (i - 4) // 2 + 1))
            act(m.ptt[:, i % 4, 0:k + 1].rearrange("p k r q -> p k (r q)"), ps[:, 2:3 + k, :], ACT.Copy)\
                .then_inc(sem["ptt"], 1)

        def heads_out(g):
            a.wait_ge(sem["pv"], at("pv", 2 * g + 2))
            act(m.oT[:, 2 * g:2 * g + 2], two(ps, g % 2), ACT.Copy).then_inc(sem["oc"], 1)

        exps(0)
        for i in range(16):
            if i + 1 < 16:
                exps(i + 1)
            turned(i)
            if i % 4 == 0 and i:
                heads_out(i // 4 - 1)
        heads_out(3)
        j = out_gates(2, j)

        for n in range(ND):
            a.wait_ge(done, done_at(C_WO + n))
            act(m.u[:, n], ps[:, bank(j), 0:S], ACT.Identity, scale=gate(1, n)).then_inc(sem["scaled"], 1)
            j += 1
        squares(3, m.h, m.u, "cent", 16, 1)
        ffn(1, C_FFN1)
        squares(4, m.h, m.u, "cent", 24, 5)

    with a.Fori(0, DEPTH) as l:
        layer(l)



def vector1(nc, v, m, sem, stream):
    ps, con = m.ps, m.con_of
    landed, done = stream.landed, stream.done
    tt, ts, stt = nc.vector.tensor_tensor, nc.vector.tensor_scalar, nc.vector.scalar_tensor_tensor

    def layer(l):
        at = lambda name, k: l * SIGNALS1[name] + k
        landed_at = lambda i, rounds=0: stream.landed_value(l, i, rounds)
        done_at = lambda i, rounds=0: stream.done_value(l, i, rounds)
        par = lambda name, at=0, n=1: m.par[:, PAR1[name] + at:PAR1[name] + at + n]
        c1 = lambda name, n=P, at=0: m.conb[:, CON1[name] + at:CON1[name] + at + n]
        bank = lambda j: 4 + j % 4

        for cg in range(9):
            if cg >= 2:
                v.wait_ge(sem["mod_raw"], at("mod_raw", cg - 1))
            acc = m.ada[cg % 2]
            for k in range(ND):
                i = C_ADA + cg * 8 + k
                v.wait_ge(landed[i % RING], landed_at(i))
                w = m.ring[:, (i % RING) * 1024:(i % RING + 1) * 1024]
                if k == 0:
                    last = ts(acc, w, m.cvec[:, k:k + 1], None, ALU.mult)
                else:
                    last = stt(acc, w, m.cvec[:, k:k + 1], acc, ALU.mult, ALU.add)
                last.then_inc(done, 1)
                v.drain()
            v.nop().then_inc(sem["ada_sum"], 1)
        v.wait_ge(sem["par"], at("par", 16))
        v.wait_ge(sem["mod_raw"], at("mod_raw", 9))
        tt(m.mod[:], ps[:, 0, 0:72], par("ada_b", 0, 72), ALU.add)
        v.drain()
        for i in range(3):
            ts(m.sc1[:, 8 * i:8 * i + 8], m.mod[:, (3 * i + 1) * 8:(3 * i + 2) * 8], 1.0, None, ALU.add)
        for i in (0, 2):
            g = m.mod[:, (3 * i + 2) * 8:(3 * i + 3) * 8]
            ts(g, g, 0.5, None, ALU.mult)
        v.drain()

        def modulate(i):
            for n in range(ND):
                last = ts(m.u[:, n], m.h[:, n], m.sc1[:, 8 * i + n:8 * i + n + 1],
                          m.mod[:, 24 * i + n:24 * i + n + 1], ALU.mult, ALU.add)
            last.then_inc(sem["u"], 1)

        def residual(k0):
            for n in range(ND):
                v.wait_ge(sem["scaled"], at("scaled", k0 + n + 1))
                stt(m.h[:, n], m.h[:, n], ALPHA, m.u[:, n], ALU.mult, ALU.add).then_inc(sem["resid"], 1)

        def centre(k, src, bank_, k0):
            v.wait_ge(sem["mu"], at("mu", k + 1))
            for n in range(ND):
                tt(src[:, n], src[:, n], ps[:, bank_, 0:S], ALU.subtract).then_inc(sem["cent"], 1)

        def inverse_root(k):
            v.wait_ge(sem["sd"], at("sd", k + 1))
            nc.vector.reciprocal(m.rs, m.sd)
            v.drain()

        def norm(i, at, bank_):
            centre(at[0], m.h, bank_, 0)
            inverse_root(at[1])
            for n in range(ND):
                tt(m.h[:, n], m.h[:, n], m.rs, ALU.mult)
            v.drain()
            for n in range(ND):
                last = ts(m.h[:, n], m.h[:, n], par("ln_g", 8 * i + n), par("ln_b", 8 * i + n), ALU.mult, ALU.add)
            v.drain()
            return last

        def ffn(q):
            def hidden(f, fk):
                v.wait_ge(sem["silu"], at("silu", q * NF + fk + 1))
                tt(m.hid[:, f % 4], ps[:, 4 + f % 4, S:2 * S], m.silu[:, f % 4], ALU.mult)\
                    .then_inc(sem["hid"], 1)
            hidden(0, 0)
            with v.Fori(0, 5) as it:
                for j in range(4):
                    hidden(1 + j, 4 * it + 1 + j)
            hidden(21, 21)
            residual(16 * q)

        modulate(0)
        ffn(0)
        norm(0, (0, 0), 4)
        modulate(1)

        nc.vector.memset(m.apad[:, :, 0:TAPS_A - 1], 0.0)
        nc.vector.memset(m.xpad[:, :, 0:TAPS_B - 1], 0.0)
        j = 0
        for n in range(8):
            v.wait_ge(sem["sg"], at("sg", n + 1))
            tt(m.apad[:, n, TAPS_A - 1:], ps[:, bank(j), 0:S], m.sg[:, n % 4], ALU.mult).then_inc(sem["glu"], 1)
            j += 1
        v.drain()

        def conv(dst, src, w, b, taps, lo, hi, signal):
            for k in range(taps):
                for n in range(lo, hi):
                    if k == 0:
                        ts(dst[:, n], src[:, n, 0:S], par(w, n * taps), par(b, n), ALU.mult, ALU.add)
                    else:
                        last = stt(dst[:, n], src[:, n, k:k + S], par(w, n * taps + k), dst[:, n], ALU.mult, ALU.add)
                        if k == taps - 1:
                            last.then_inc(sem[signal], 1)
                v.drain()

        conv(m.ac, m.apad, "aw", "ab", TAPS_A, 0, ND, "aconv")
        for q in range(2):
            v.wait_ge(sem["copied"], at("copied", 4 * q + 4))
            conv(m.xc, m.xpad, "xw", "xb", TAPS_B, 8 * q, 8 * q + 8, "xconv")
        for b, (src, pe) in enumerate(((m.kc, "pek"), (m.vc, "pev"))):
            v.wait_ge(sem["copied"], at("copied", 18 + b))
            for q in range(16):
                last = ts(m.kp[b][:, q].rearrange("p (g n) -> p g n", g=4), src[:, :, 2 * q:2 * q + 225:16],
                          par(pe, q), None, ALU.add)
            last.then_inc(sem["kpe"], 1)
        j = 31

        def both(t, n=2, k=S):
            return t.rearrange("p (a t) -> p a t", a=1).to_broadcast([P, n, k])
        cos, sin = c1("cos", S), c1("sin", S)
        for n in range(4):
            v.wait_ge(sem["rotp"], at("rotp", n + 1))
            q, tmp = m.qr[:, 2 * n:2 * n + 2], m.sg[:, 2 * (n % 2):2 * (n % 2) + 2]
            tt(tmp, two(ps, bank(j)), both(sin), ALU.mult)
            tt(q, q, both(cos), ALU.mult)
            v.drain()
            tt(q, q, tmp, ALU.add).then_inc(sem["rope"], 1)
            j += 1
        for n in range(8):
            v.wait_ge(sem["rotp"], at("rotp", 5 + n))
            k, tmp = m.kr[:, n // 4, n % 4], m.sg[:, n % 4]
            tt(tmp, ps[:, bank(j), S:2 * S], sin, ALU.mult)
            tt(k, ps[:, bank(j), 0:S], cos, ALU.mult)
            v.drain()
            tt(k, k, tmp, ALU.add).then_inc(sem["rope"], 1)
            j += 1
        j += 2
        v.drain()
        v.wait_ge(sem["kc2"], at("kc2", 1))
        g4 = lambda t: t.rearrange("p (g n) -> p g n", g=4)
        ends = lambda t: both(t[:, 31:S:16], 4, CMP)
        tmp = m.sg[:, 0, 0:60]
        tt(g4(tmp), g4(ps[:, bank(j), 0:60]), ends(sin), ALU.mult)
        tt(g4(m.kcmp), g4(m.kcr), ends(cos), ALU.mult)
        v.drain()
        tt(m.kcmp, m.kcmp, tmp, ALU.add).then_inc(sem["kcmp"], 1)
        j += 1
        v.wait_ge(sem["vb"], at("vb", 1))
        for r in range(4):
            last = nc.vector.tensor_copy(m.vb[32 * r:32 * r + 32, :, r // 2, (r % 2) * 64:(r % 2) * 64 + 64],
                                         ps[32 * r:32 * r + 32, bank(j), 0:256].rearrange("p (g d) -> p g d", g=4))
        last.then_inc(sem["vbc"], 1)
        j += 1

        v.wait_ge(sem["dtexp"], at("dtexp", 1))
        log1p(nc, v, m.dtw[:, 1], m.dtw[:, 0], m.dtw[:, 2], m.dtw[:, 3], m.dtw[:, 4])
        ts(m.dtw[:, 0], m.dtraw, 0.0, None, ALU.max)
        v.drain()
        tt(m.dtw[:, 3], m.dtw[:, 3], m.dtw[:, 0], ALU.add)
        v.drain()
        ts(m.dtw[:, 4], m.dtw[:, 3], m.aexp[0:16], -1.0, ALU.mult, ALU.mult).then_inc(sem["dtv"], 1)

        centre(1, m.ac, 0, 8)
        inverse_root(1)
        for n in range(ND):
            tt(m.ac[:, n], m.ac[:, n], m.rs, ALU.mult).then_inc(sem["anrs"], 1)

        def merge(branch, j):
            for n in range(8):
                v.wait_ge(sem["outsg"], at("outsg", 8 * branch + n + 1))
                y, g = ps[:, bank(j), S:2 * S], m.sg[:, n % 4]
                if branch == 0:
                    last = tt(m.merged[:, n], y, g, ALU.mult)
                else:
                    tt(g, y, g, ALU.mult)
                    v.drain()
                    last = tt(m.merged[:, n], m.merged[:, n], g, ALU.add)
                last.then_inc(sem["outm"], 1)
                j += 1
            return j

        j = merge(0, j)

        v.wait_ge(sem["dtt"], at("dtt", 1))
        nc.vector.tensor_copy(m.dtt, ps[:, bank(j), 0:64]).then_inc(sem["dttc"], 1)
        v.drain()
        j += 2
        for h in range(4):
            v.wait_ge(sem["xt"], at("xt", h + 1))
            a, o = h // 2, h % 2
            dt = m.dtt[:, 16 * a + 8 * o:16 * a + 8 * o + 8].rearrange("p (h d) -> p h d", d=1).to_broadcast([P, 8, 64])
            tt(m.xdt[:, a, 512 * o:512 * o + 512].rearrange("p (h d) -> p h d", h=8),
               ps[:, bank(j), :].rearrange("p (h d) -> p h d", h=8), dt, ALU.mult).then_inc(sem["xdt"], 1)
            j += 1
        def exponent(h, j):
            if h % 4 == 0:
                v.wait_ge(sem["cb"], at("cb", h // 4 + 1))
                tt(m.cbm[:, (h // 4) % 2], ps[:, bank(j), 0:384], con("tri", 384), ALU.mult)\
                    .then_inc(sem["cbm"], 1)
                j += 1
            v.wait_ge(sem["bc"], at("bc", h + 1))
            ts(m.ee[:, h % 2, 0:S], ps[:, bank(j), 0:S], m.nacs[:, h:h + 1], 0.0, ALU.add, ALU.min)
            ts(m.ee[:, h % 2, S:S + P], ps[:, bank(j), P:S], m.nacs[:, 16 + h:17 + h], 0.0, ALU.add, ALU.min)\
                .then_inc(sem["arg"], 1)
            return j + 1

        j = exponent(0, j)
        for h in range(16):
            v.drain()
            v.wait_ge(sem["ee"], at("ee", h + 1))
            if h >= 2:
                v.wait_ge(sem["yh"], at("yh", h - 1))
            tt(m.mm[:, h % 2], m.ee[:, h % 2], m.cbm[:, (h // 4) % 2], ALU.mult).then_inc(sem["mm"], 1)
            if h + 1 < 16:
                j = exponent(h + 1, j)
        for n in range(ND):
            v.wait_ge(sem["yh"], at("yh", 4 * (n // 2) + 4))
            stt(m.yb[:, n], m.xc[:, n], par("dsk", n), ps[:, n // 2, (n % 2) * S:(n % 2 + 1) * S], ALU.mult, ALU.add)
        v.drain()
        for n in range(ND):
            tt(m.yb[:, n], m.yb[:, n], m.z[:, n], ALU.mult).then_inc(sem["ysil"], 1)
        inverse_root(2)
        for n in range(ND):
            stt(m.yb[:, n], m.yb[:, n], par("nw", n), m.rs, ALU.mult, ALU.mult).then_inc(sem["bnorm"], 1)
        j = merge(1, j)

        nc.vector.memset(m.pcmp, 0.0)
        v.drain()
        wide = lambda t, n, k: t.rearrange("p (h d) -> p h d", d=1).to_broadcast([P, n, k])
        for a in range(2):
            v.wait_ge(sem["cs"], at("cs", a + 1))
            p = m.pcmp[:, a, :, 0:CMP]
            for odd in range(2):
                s = ps[:, bank(j + odd), 0:128].rearrange("p (h n) -> p h n", h=8)[:, :, 0:CMP]
                tt(p[:, odd::2], s, both(c1("cmask", CMP, 16 * a), 8, CMP), ALU.add)
            v.drain()
            nc.vector.tensor_reduce(m.cst[:, 0, a], p, AX, ALU.max)
            v.drain()
            tt(p, p, wide(m.cst[:, 0, a], 16, CMP), ALU.subtract).then_inc(sem["cmx"], 1)
            j += 2
        for a in range(2):
            p, f = m.pcmp[:, a, :, 0:CMP], m.cst[:, 1, a]
            v.wait_ge(sem["cex"], at("cex", a + 1))
            nc.vector.tensor_reduce(f, p, AX, ALU.add)
            v.drain()
            nc.vector.reciprocal(f, f)
            v.drain()
            tt(f, f, m.gates[:, a, 0:48:3], ALU.mult)
            v.drain()
            if a == 0:
                ts(f, f, con("valid", 1), None, ALU.mult)
                v.drain()
            tt(p, p, wide(f, 16, CMP), ALU.mult).then_inc(sem["cp"], 1)
        j += 2

        def maxima(i):
            a = (i // 2) % 2
            v.wait_ge(sem["sc"], at("sc", i + 1))
            s = score_view(ps, i, a)
            diag = s[:, :, a * P:(a + 1) * P]
            tt(diag, diag, both(con("neg"), 4, P), ALU.add)
            v.drain()
            nc.vector.tensor_reduce(m.nmx[:, i % 2], s, AX, ALU.max, negate=True).then_inc(sem["nmx"], 1)

        def weights(i):
            g, a, b = i // 4, (i // 2) % 2, i % 2
            f = m.fac[:, i % 2]
            v.wait_ge(sem["ex"], at("ex", i + 1))
            nc.vector.reciprocal(f, m.sums[:, i % 2])
            v.drain()
            gate = m.gates[:, a, 12 * g:12 * g + 12].rearrange("p (i q c) -> p q i c", i=2, q=2)[:, :, :, 1 + b]
            ff = f.rearrange("p (q i) -> p q i", q=2)
            tt(ff, ff, gate, ALU.mult)
            v.drain()
            for r in range(4):
                p = m.e[:, i % 2, r, 0:P * (a + 1)]
                last = ts(p, p, f[:, r:r + 1], None, ALU.mult)
            last.then_inc(sem["pr"], 1)

        maxima(0)
        for i in range(16):
            if i + 1 < 16:
                maxima(i + 1)
            weights(i)
        j = merge(2, j)

        residual(8)
        norm(1, (2, 3), 0)
        modulate(2)
        ffn(1)
        last = norm(2, (3, 4), 4)
        v.nop().then_inc(sem["layer_done"], 1)

    with v.Fori(0, DEPTH) as l:
        layer(l)


def log1p(nc, v, y, z, z2, out, p):
    tt, ts, stt = nc.vector.tensor_tensor, nc.vector.tensor_scalar, nc.vector.scalar_tensor_tensor
    ts(z, y, 2.0, None, ALU.add)
    v.drain()
    nc.vector.reciprocal(z, z)
    v.drain()
    tt(z, z, y, ALU.mult)
    v.drain()
    tt(z2, z, z, ALU.mult)
    v.drain()
    ts(p, z2, 1.0 / 15, None, ALU.mult)
    v.drain()
    for c in (13, 11, 9, 7, 5, 3):
        stt(p, p, 1.0 / c, z2, ALU.add, ALU.mult)
        v.drain()
    stt(out, p, 1.0, z, ALU.add, ALU.mult)
    v.drain()
    ts(out, out, 2.0, None, ALU.mult)
    v.drain()



def tensor2(nc, t, m, sem, stream):
    ps, con = m.ps, m.con_of
    landed, done = stream.landed, stream.done
    mm = nc.tensor.matmul

    def layer(l):
        at = lambda name, k: l * SIGNALS2[name] + k
        landed_at = lambda i, rounds=0: stream.landed_value(l, i, rounds)
        done_at = lambda i, rounds=0: stream.done_value(l, i, rounds)
        c2 = lambda name, n=P, at=0: m.conb[:, CON2[name] + at:CON2[name] + at + n]
        unit = lambda j: 4 + j % 4

        def project(i, out, rounds=0, cols=(0, P)):
            t.wait_ge(landed[i % RING], landed_at(i, rounds))
            for k in range(ND):
                last = mm(out, chunk_tile(m, i, k, *cols), m.u[:, k], start=k == 0, stop=k == ND - 1)
            return last

        def token_major(i, bank, width, at):
            t.wait_ge(landed[i % RING], landed_at(i))
            for a in range(2):
                for k in range(ND):
                    last = mm(ps[:, bank, a * width + at:a * width + at + P], m.u[:, k, a * P:(a + 1) * P],
                              chunk_tile(m, i, k), start=k == 0, stop=k == ND - 1)
            return last

        def rms(k):
            for n in range(ND):
                t.wait_ge(sem["usq"], at("usq", 8 * k + n + 1))
                last = mm(ps[:, 0, 0:S], con("mean"), m.sq[:, n], start=n == 0, stop=n == ND - 1)
            last.then_inc(sem["uvar"], 1)

        rms(0)
        t.wait_ge(sem["u"], at("u", 1))
        j = 0
        def pair(i, j):
            project(i, ps[:, unit(j), 0:S]).then_inc(done, 1)
            project(i + 1, ps[:, unit(j), S:2 * S]).then_inc(done, 1)
            return j + 1
        j = pair(E_Q, j)
        j = pair(E_Q + 2, j)
        project(E_K, ps[:, unit(j), 0:S]).then_inc(done, 1)
        j += 1
        token_major(E_V, unit(j), P, 0).then_inc(done, 1)
        j += 1
        t.wait_ge(sem["copied"], at("copied", 1))
        project(E_IF, ps[0:4, unit(j), 0:S], cols=(0, 4))
        project(E_IF, ps[0:4, unit(j), S:2 * S], cols=(4, 8)).then_inc(done, 1)
        j += 1
        t.wait_ge(sem["copied"], at("copied", 2))
        j = pair(E_QM, j)
        t.wait_ge(sem["copied"], at("copied", 3))
        j = pair(E_KM, j)
        for q in range(2):
            t.wait_ge(sem["copied"], at("copied", 4 + q))
            for c in range(2):
                token_major(E_VM + 2 * q + c, unit(j), S, c * P).then_inc(done, 1)
            j += 1
        t.wait_ge(sem["copied"], at("copied", 6))
        j = pair(E_OM, j)
        t.wait_ge(sem["copied"], at("copied", 7))
        j = pair(E_OM + 2, j)
        for n in range(5):
            if n < 4:
                t.wait_ge(sem["copied"], at("copied", 8 + n))
            else:
                t.wait_ge(sem["hsd"], at("hsd", 1))
            mm(ps[:, unit(j), 0:S], c2("blk"), m.hsq[n], start=True, stop=True).then_inc(sem["hvar"], 1)
            j += 1
        for n in range(5):
            if n < 4:
                t.wait_ge(sem["hsd"], at("hsd", 2 + n))
            else:
                t.wait_ge(sem["rope"], at("rope", 1))
            t.wait_ge(sem["qn"], at("qn", n + 1))
            mm(ps[:, unit(j), 0:S], c2("rot"), m.qk_raw[n], start=True, stop=True).then_inc(sem["rotp"], 1)
            j += 1
        t.wait_ge(sem["rope"], at("rope", 5))
        mm(ps[:, unit(j), 0:S], c2("dup"), m.kda, start=True, stop=True)
        mm(ps[:, unit(j), S:2 * S], c2("dup", P, P), m.kda, start=True, stop=True).then_inc(sem["dup"], 1)
        j += 1
        t.wait_ge(sem["mt"], at("mt", 1))
        for a in range(2):
            last = mm(ps[:, unit(j), 4 * a:4 * a + 4], m.ow[:, 3, a * P:(a + 1) * P],
                      m.con[0:4, CON["ident"]:CON["ident"] + 4], start=True, stop=True)
        last.then_inc(sem["rt"], 1)

        def scores(i):
            g, a = i // 2, i % 2
            if i >= 2:
                t.wait_ge(sem["ex"], at("ex", i - 1))
            for r in range(4):
                lo = 64 * (r % 2)
                last = mm(score_view(ps, i, a)[:, place_of(r)], m.qa[lo:lo + 64, 2 * g + r // 2, a * P:(a + 1) * P],
                          m.ka[lo:lo + 64, g, 0:P * (a + 1)], start=True, stop=True)
            last.then_inc(sem["sc"], 1)

        def turn(i):
            t.wait_ge(sem["pr"], at("pr", i + 1))
            if i >= 1:
                t.wait_ge(sem["ptt"], at("ptt", i))
            for k in range(i % 2 + 1):
                for r in range(4):
                    last = nc.tensor.transpose(ps[:, 2 + k, r * P:(r + 1) * P], m.e[:, i % 2, r, k * P:(k + 1) * P],
                                               con("ident"))
            last.then_inc(sem["tr"], 1)

        def values(i):
            g, a = i // 2, i % 2
            o = ps[:, g, :].rearrange("p (i t) -> p i t", i=2)
            t.wait_ge(sem["ptt"], at("ptt", i + 1))
            for k in range(a + 1):
                for q in range(2):
                    last = mm(o[64 * q:64 * q + 64, :, a * P:(a + 1) * P], m.va[:, k, g * 64:(g + 1) * 64],
                              m.ptt[:, i, k, 2 * q:2 * q + 2], start=a == 0, stop=a == 1 and k == 1,
                              skip_group_check=True)
            last.then_inc(sem["pv"], 1)

        t.wait_ge(sem["dupc"], at("dupc", 1))
        t.wait_ge(sem["mtc"], at("mtc", 1))
        scores(0)
        for i in range(4):
            if i + 1 < 4:
                scores(i + 1)
            turn(i)
            if i >= 1:
                values(i - 1)
        values(3)

        t.wait_ge(sem["oc"], at("oc", 2))
        j = 0

        def head_out(h):
            t.wait_ge(sem["mm"], at("mm", h + 1))
            for a, lhs in enumerate((m.vm, None)):
                o = ps[:, h, a * S:(a + 1) * S]
                left = lambda s: con("ones") if lhs is None else m.vm[:, s, h * P:(h + 1) * P]
                mm(o, left(0), m.mm[:, h % 2, 0:S], start=True, stop=False)
                last = mm(o[:, P:S], left(1), m.mm[:, h % 2, S:S + P], start=False, stop=True)
            last.then_inc(sem["num"], 1)

        for h in range(4):
            lo = 64 * (h % 2)
            if h >= 2:
                t.wait_ge(sem["qkm"], at("qkm", h - 1))
            q, k = m.qm[lo:lo + 64, h // 2], m.km[lo:lo + 64, h // 2]
            mm(ps[:, unit(j), 0:S], k[:, 0:P], q, start=True, stop=True)
            mm(ps[:, unit(j), S:S + P], k[:, P:S], q[:, P:S], start=True, stop=True).then_inc(sem["qk"], 1)
            j += 1
            if h >= 2:
                t.wait_ge(sem["arg"], at("arg", h - 1))
            mm(ps[:, unit(j), :], m.con[0:4, CON["ident"] + h:CON["ident"] + h + 1].to_broadcast([4, P]),
               m.ow[:, 5:7].rearrange("p k t -> p (k t)"), start=True, stop=True).then_inc(sem["bc"], 1)
            j += 1
            if h >= 1:
                head_out(h - 1)
        head_out(3)
        for h in range(4):
            if h % 2 == 0:
                t.wait_ge(sem["qkm"], at("qkm", 3 + h // 2))
            else:
                t.wait_ge(sem["arg"], at("arg", 3 + h // 2))
            t.wait_ge(sem["hsq"], at("hsq", h + 1))
            mm(ps[:, unit(j), 0:S], c2("mean128"), m.sq[:, h], start=True, stop=True).then_inc(sem["hvar"], 1)
            j += 1

        for b, src in enumerate((m.att, m.hm)):
            for q in range(4):
                i = E_BR + 12 * b + 3 * q
                k4 = 4 * b + q
                if k4 < 2:
                    t.wait_ge(sem["hsd"], at("hsd", 7 + 2 * k4))
                else:
                    t.wait_ge(sem["outsg"], at("outsg", k4 - 1))
                j = pair(i, j)
                if k4 >= 2:
                    t.wait_ge(sem["outm"], at("outm", k4 - 1))
                if b == 1 and q == 0:
                    t.wait_ge(sem["hm"], at("hm", 4))
                t.wait_ge(landed[(i + 2) % RING], landed_at(i + 2))
                for c in range(2):
                    for k in range(4):
                        last = mm(ps[:, unit(j), c * S:(c + 1) * S], chunk_tile(m, i + 2, 4 * c + k), src[:, k],
                                  start=k == 0, stop=k == 3)
                last.then_inc(done, 1)
                j += 1
        t.wait_ge(sem["outm"], at("outm", 8))
        for q in range(4):
            for c in range(2):
                i = E_OUT + 2 * q + c
                t.wait_ge(landed[i % RING], landed_at(i))
                for k in range(ND):
                    last = mm(ps[:, unit(j), c * S:(c + 1) * S], chunk_tile(m, i, k), m.merged[:, k],
                              start=k == 0, stop=k == ND - 1)
                last.then_inc(done, 1)
            j += 1

        rms(1)
        t.wait_ge(sem["u"], at("u", 2))
        for b in range(4):
            mm(ps[:, b, :], m.zero[:, 0:P], m.zero[:], start=True, stop=False, skip_group_check=True)

        def up(i, f, rounds=0):
            project(i, ps[:, 4 + f % 2, 0:S], rounds).then_inc(done, 1)

        def down(i, f, fk, rounds=0, last=False):
            t.wait_ge(landed[i % RING], landed_at(i, rounds))
            t.wait_ge(sem["hid"], at("hid", fk + 1))
            for n in range(ND):
                x = mm(ps[:, n // 2, (n % 2) * S:(n % 2 + 1) * S], chunk_tile(m, i, n), m.hid[:, f % 2],
                       start=False, stop=last, skip_group_check=True)
            x.then_inc(done, 1)

        up(E_FFN, 0)
        with t.Fori(0, 5) as it:
            for q in range(6):
                up(E_FFN + 1 + 2 * q, 1 + q, it)
                down(E_FFN + 2 + 2 * q, q, 6 * it + q, it)
        up(E_FFN + 61, 31)
        down(E_FFN + 62, 30, 30)
        down(E_FFN + 63, 31, 31, last=True)

    with t.Fori(0, DEPTH) as l:
        layer(l)


def scalar2(nc, a, m, sem, stream, par_source):
    ps, con = m.ps, m.con_of
    landed, done = stream.landed, stream.done
    act = nc.scalar.activation

    def layer(l):
        at = lambda name, k: l * SIGNALS2[name] + k
        landed_at = lambda i, rounds=0: stream.landed_value(l, i, rounds)
        done_at = lambda i, rounds=0: stream.done_value(l, i, rounds)
        par = lambda name, at=0, n=1: m.par[:, PAR2[name] + at:PAR2[name] + at + n]
        bank = lambda j: 4 + j % 4
        a.wait_ge(sem["layer_done"], at("layer_done", 1))
        a.dma_start(m.par[:, 0:PAR2["all"]], par_source[bass.ds(l, 1)].rearrange("a p n -> (a p) n"))\
            .then_inc(sem["par"], 16)

        def rms(k):
            for n in range(ND):
                if k == 1 and n % 2 == 0:
                    a.wait_ge(sem["xres"], at("xres", n // 2 + 1))
                act(m.sq[:, n], m.h[:, n], ACT.Square).then_inc(sem["usq"], 1)
            a.wait_ge(sem["uvar"], at("uvar", k + 1))
            act(m.sd, ps[:, 0, 0:S], ACT.Sqrt, bias=con("eps2", 1)).then_inc(sem["usd"], 1)

        rms(0)
        copied = sem["copied"]
        a.wait_ge(sem["par"], at("par", 16))
        j = 0
        for n in range(3):
            a.wait_ge(done, done_at(E_Q + 2 * n + 1 if n < 2 else E_K))
            for c in range(2 if n < 2 else 1):
                act(m.qk_raw[2 * n + c], ps[:, bank(j), c * S:(c + 1) * S], ACT.Copy)
                last = act(m.hsq[2 * n + c], ps[:, bank(j), c * S:(c + 1) * S], ACT.Square)
            last.then_inc(copied, 1)
            j += 1
        a.wait_ge(done, done_at(E_V))
        act(m.va, two(ps, bank(j), 0, P), ACT.Copy).then_inc(copied, 1)
        j += 1
        a.wait_ge(done, done_at(E_IF))
        act(m.ow[:, 0], ps[0:4, bank(j), 0:S], ACT.Identity, bias=par("ib")[0:4])
        act(m.ow[:, 1], ps[0:4, bank(j), S:2 * S], ACT.Identity, bias=par("fb")[0:4]).then_inc(copied, 1)
        j += 1
        for i, dst in ((E_QM, m.qm), (E_KM, m.km)):
            a.wait_ge(done, done_at(i + 1))
            act(dst, two(ps, bank(j)), ACT.Copy).then_inc(copied, 1)
            j += 1
        for q in range(2):
            a.wait_ge(done, done_at(E_VM + 2 * q + 1))
            act(m.vm[:, :, q * S:(q + 1) * S], two(ps, bank(j)), ACT.Copy).then_inc(copied, 1)
            j += 1
        for q in range(2):
            a.wait_ge(done, done_at(E_OM + 2 * q + 1))
            act(m.om[:, 2 * q:2 * q + 2], two(ps, bank(j)), ACT.Sigmoid).then_inc(copied, 1)
            j += 1
        act(m.ow[:, 2], m.ow[:, 1], ACT.Abs)
        a.drain()
        act(m.ow[:, 3], m.ow[:, 2], ACT.Exp, scale=-1.0).then_inc(sem["fexp"], 1)
        for n in range(5):
            a.wait_ge(sem["hvar"], at("hvar", n + 1))
            act(m.hsq[n], ps[:, bank(j), 0:S], ACT.Sqrt, bias=con("eps2", 1)).then_inc(sem["hsd"], 1)
            j += 1
        j += 5
        a.wait_ge(sem["dup"], at("dup", 1))
        act(m.ka, two(ps, bank(j)), ACT.Copy).then_inc(sem["dupc"], 1)

        def exps(i):
            a.wait_ge(sem["nmx"], at("nmx", i + 1))
            if i >= 2:
                a.wait_ge(sem["tr"], at("tr", i - 1))
            for r in range(4):
                act(m.e[:, i % 2, r, 0:P * (i % 2 + 1)], score_view(ps, i, i % 2)[:, r], ACT.Exp,
                    bias=m.nmx[:, i % 2, r:r + 1], accum_out=m.sums[:, i % 2, r:r + 1])
            act(m.esink[:, i % 2], m.esink[:, i % 2], ACT.Exp).then_inc(sem["ex"], 1)

        def turned(i):
            a.wait_ge(sem["tr"], at("tr", i + 1))
            k = i % 2
            act(m.ptt[:, i, 0:k + 1].rearrange("p k r q -> p k (r q)"), ps[:, 2:3 + k, :], ACT.Copy)\
                .then_inc(sem["ptt"], 1)

        def heads_out(g):
            a.wait_ge(sem["pv"], at("pv", 2 * g + 2))
            act(m.att[:, 2 * g:2 * g + 2], two(ps, g), ACT.Copy).then_inc(sem["oc"], 1)

        exps(0)
        for i in range(4):
            if i + 1 < 4:
                exps(i + 1)
            turned(i)
        heads_out(0)
        heads_out(1)

        def numerator_side(h):
            a.wait_ge(sem["num"], at("num", h + 1))
            act(m.den[:, h % 2], ps[:, h, S:2 * S], ACT.Abs).then_inc(sem["absd"], 1)
            a.wait_ge(sem["hh"], at("hh", h + 1))
            act(m.sq[:, h], m.hm[:, h], ACT.Square).then_inc(sem["hsq"], 1)

        j = 0
        for h in range(4):
            a.wait_ge(sem["bc"], at("bc", h + 1))
            act(m.em[:, h % 2], ps[:, bank(2 * h + 1), S:2 * S], ACT.Exp).then_inc(sem["me"], 1)
            a.wait_ge(sem["arg"], at("arg", h + 1))
            act(m.ee[:, h % 2], m.ee[:, h % 2], ACT.Exp).then_inc(sem["ee"], 1)
            if h >= 1:
                numerator_side(h - 1)
        numerator_side(3)
        j = 8
        for h in range(4):
            a.wait_ge(sem["hvar"], at("hvar", 5 + h + 1))
            if h >= 2:
                a.wait_ge(sem["hm"], at("hm", h - 1))
            act((m.sd, m.hsq[4])[h % 2], ps[:, bank(j), 0:S], ACT.Sqrt, bias=con("eps2", 1))\
                .then_inc(sem["hsd"], 1)
            j += 1

        for b in range(2):
            for q in range(4):
                k = 4 * b + q
                a.wait_ge(done, done_at(E_BR + 12 * b + 3 * q + 1))
                if k >= 2:
                    a.wait_ge(sem["outm"], at("outm", k - 1))
                act(m.sg[:, 2 * (q % 2):2 * (q % 2) + 2], two(ps, bank(j)), ACT.Sigmoid)\
                    .then_inc(sem["outsg"], 1)
                j += 2

        rms(1)

        def relu(i, f, rounds=0):
            a.wait_ge(done, done_at(i, rounds))
            act(m.silu[:, f % 2], ps[:, 4 + f % 2, 0:S], ACT.Relu).then_inc(sem["relu"], 1)
        relu(E_FFN, 0)
        with a.Fori(0, 5) as it:
            for q in range(6):
                relu(E_FFN + 1 + 2 * q, 1 + q, it)
        relu(E_FFN + 61, 31)

    with a.Fori(0, DEPTH) as l:
        layer(l)


def vector2(nc, v, m, sem, stream):
    ps, con = m.ps, m.con_of
    landed, done = stream.landed, stream.done
    tt, ts, stt = nc.vector.tensor_tensor, nc.vector.tensor_scalar, nc.vector.scalar_tensor_tensor

    def layer(l):
        at = lambda name, k: l * SIGNALS2[name] + k
        landed_at = lambda i, rounds=0: stream.landed_value(l, i, rounds)
        done_at = lambda i, rounds=0: stream.done_value(l, i, rounds)
        par = lambda name, at=0, n=1: m.par[:, PAR2[name] + at:PAR2[name] + at + n]
        c2 = lambda name, n=P, at=0: m.conb[:, CON2[name] + at:CON2[name] + at + n]
        bank = lambda j: 4 + j % 4

        def rms(k, gain):
            v.wait_ge(sem["par"], at("par", 16))
            v.wait_ge(sem["usd"], at("usd", k + 1))
            nc.vector.reciprocal(m.rs, m.sd)
            v.drain()
            for n in range(ND):
                last = stt(m.u[:, n], m.h[:, n], par(gain, n), m.rs, ALU.mult, ALU.mult)
            last.then_inc(sem["u"], 1)

        rms(0, "nmix")
        for n in range(5):
            v.wait_ge(sem["hsd"], at("hsd", n + 1))
            nc.vector.reciprocal(m.hsq[n], m.hsq[n])
            v.drain()
            stt(m.qk_raw[n], m.qk_raw[n], par("qn" if n < 4 else "kn"), m.hsq[n], ALU.mult, ALU.mult)\
                .then_inc(sem["qn"], 1)
        v.drain()
        for n in range(5):
            b = bank(16 + n)
            dst = m.qa[:, n] if n < 4 else m.kda
            v.wait_ge(sem["rotp"], at("rotp", n + 1))
            tt(m.tmp[n % 2], ps[:, b, 0:S], c2("sinq" if n < 4 else "sink", S), ALU.mult)
            tt(dst, m.qk_raw[n], c2("cosq" if n < 4 else "cosk", S), ALU.mult)
            v.drain()
            tt(dst, dst, m.tmp[n % 2], ALU.add).then_inc(sem["rope"], 1)

        w = lambda k: m.ow[:, k]
        v.wait_ge(sem["fexp"], at("fexp", 1))
        log1p(nc, v, w(3), w(2), w(4), w(5), w(6))
        ts(w(1), w(1), 0.0, None, ALU.min)
        v.drain()
        tt(w(1), w(1), w(5), ALU.subtract)
        v.drain()
        nc.vector.tensor_tensor_scan(w(2), w(7), w(1), 0.0, ALU.mult, ALU.add)
        v.drain()
        tt(w(3), w(0), w(2), ALU.subtract)
        v.drain()
        nc.vector.tensor_tensor_scan(w(4), w(3), w(3), 0.0, ALU.max, ALU.max)
        v.drain()
        ts(w(5), w(4), -1.0, None, ALU.mult)
        v.drain()
        tt(w(6), w(5), w(2), ALU.subtract).then_inc(sem["mt"], 1)
        v.wait_ge(sem["rt"], at("rt", 1))
        nc.vector.tensor_copy(m.rt, ps[:, bank(22), 0:8].rearrange("p (a h) -> p a h", a=2))\
            .then_inc(sem["mtc"], 1)

        def maxima(i):
            g, a = i // 2, i % 2
            mx, sink = m.mx[:, i % 2], par("sink", 4 * g, 4)
            v.wait_ge(sem["sc"], at("sc", i + 1))
            s = score_view(ps, i, a)
            mask = lambda t: t.rearrange("p (a t) -> p a t", a=1).to_broadcast([P, 4, P])
            tt(s[:, :, a * P:(a + 1) * P], s[:, :, a * P:(a + 1) * P], mask(con("neg")), ALU.add)
            if a == 1:
                tt(s[:, :, 0:P], s[:, :, 0:P], mask(c2("band")), ALU.add)
            v.drain()
            nc.vector.tensor_reduce(mx, s, AX, ALU.max)
            v.drain()
            tt(mx, mx, sink, ALU.max)
            v.drain()
            ts(m.nmx[:, i % 2], mx, -1.0, None, ALU.mult)
            tt(m.esink[:, i % 2], sink, mx, ALU.subtract)
            v.drain()
            v.nop().then_inc(sem["nmx"], 1)

        def weights(i):
            f = m.fac[:, i % 2]
            v.wait_ge(sem["ex"], at("ex", i + 1))
            tt(f, m.sums[:, i % 2], m.esink[:, i % 2], ALU.add)
            v.drain()
            nc.vector.reciprocal(f, f)
            v.drain()
            for r in range(4):
                p = m.e[:, i % 2, r, 0:P * (i % 2 + 1)]
                last = ts(p, p, f[:, r:r + 1], None, ALU.mult)
            last.then_inc(sem["pr"], 1)

        maxima(0)
        for i in range(4):
            if i + 1 < 4:
                maxima(i + 1)
            weights(i)

        def quotient(h):
            d = m.den[:, h % 2]
            v.wait_ge(sem["absd"], at("absd", h + 1))
            tt(d, d, m.em[:, h % 2], ALU.max)
            v.drain()
            nc.vector.reciprocal(d, d)
            v.drain()
            tt(m.hm[:, h], ps[:, h, 0:S], d, ALU.mult).then_inc(sem["hh"], 1)

        for h in range(4):
            b = bank(2 * h + 1)
            v.wait_ge(sem["qk"], at("qk", h + 1))
            tt(m.qkm[:, h % 2], ps[:, bank(2 * h), 0:384], c2("tri8", 384), ALU.mult).then_inc(sem["qkm"], 1)
            v.wait_ge(sem["me"], at("me", h + 1))
            ts(m.ee[:, h % 2, 0:S], ps[:, b, 0:S], m.rt[:, 0, h:h + 1], 0.0, ALU.add, ALU.min)
            ts(m.ee[:, h % 2, S:S + P], ps[:, b, P:S], m.rt[:, 1, h:h + 1], 0.0, ALU.add, ALU.min)\
                .then_inc(sem["arg"], 1)
            v.drain()
            if h >= 2:
                v.wait_ge(sem["num"], at("num", h - 1))
            v.wait_ge(sem["ee"], at("ee", h + 1))
            tt(m.mm[:, h % 2], m.ee[:, h % 2], m.qkm[:, h % 2], ALU.mult).then_inc(sem["mm"], 1)
            if h >= 1:
                quotient(h - 1)
        quotient(3)
        for h in range(4):
            v.wait_ge(sem["hsd"], at("hsd", 5 + h + 1))
            d = (m.sd, m.hsq[4])[h % 2]
            nc.vector.reciprocal(m.rs, d)
            v.drain()
            stt(m.hm[:, h], m.hm[:, h], par("hn", h), m.rs, ALU.mult, ALU.mult)
            v.drain()
            tt(m.hm[:, h], m.hm[:, h], m.om[:, h], ALU.mult).then_inc(sem["hm"], 1)

        j = 12
        for b in range(2):
            for q in range(4):
                v.wait_ge(sem["outsg"], at("outsg", 4 * b + q + 1))
                v.wait_ge(done, done_at(E_BR + 12 * b + 3 * q + 2))
                y, g, out = two(ps, bank(j + 1)), m.sg[:, 2 * (q % 2):2 * (q % 2) + 2], m.merged[:, 2 * q:2 * q + 2]
                if b == 0:
                    last = tt(out, y, g, ALU.mult)
                else:
                    tt(g, y, g, ALU.mult)
                    v.drain()
                    last = tt(out, out, g, ALU.add)
                last.then_inc(sem["outm"], 1)
                j += 2
        for q in range(4):
            v.wait_ge(done, done_at(E_OUT + 2 * q + 1))
            tt(m.h[:, 2 * q:2 * q + 2], two(ps, bank(j)), m.h[:, 2 * q:2 * q + 2], ALU.add)\
                .then_inc(sem["xres"], 1)
            j += 1
        v.drain()
        rms(1, "nffn")

        def square(f, fk):
            v.wait_ge(sem["relu"], at("relu", fk + 1))
            tt(m.hid[:, f % 2], m.silu[:, f % 2], m.silu[:, f % 2], ALU.mult).then_inc(sem["hid"], 1)
        square(0, 0)
        with v.Fori(0, 5) as it:
            for q in range(6):
                square(1 + q, 6 * it + 1 + q)
        square(31, 31)
        v.wait_ge(done, done_at(E_FFN + 63))
        for q in range(4):
            tt(m.h[:, 2 * q:2 * q + 2], two(ps, q), m.h[:, 2 * q:2 * q + 2], ALU.add).then_inc(sem["xres"], 1)
        v.drain()
        v.nop().then_inc(sem["layer_done"], 1)

    with v.Fori(0, DEPTH) as l:
        layer(l)


def build(nc, x, c, con, con1, con2, stream1, stream2, par1, par2, out):
    with ExitStack() as ctx:
        m = memory(nc, ctx)
        sem = lambda name: ctx.enter_context(nc.semaphore(name))
        sem1 = {name: sem("a_" + name) for name in SIGNALS1}
        first = Stream(N1, [sem(f"landed{s}") for s in range(RING)], sem("done"))
        sem2 = {name: sem("b_" + name) for name in SIGNALS2}
        second = Stream(N2, [sem(f"landed_b{s}") for s in range(RING)], sem("done_b"))
        inputs, ready, silu_c, stored, con_b = sem("inputs"), sem("ready"), sem("silu_c"), sem("stored"), sem("con_b")
        block = ctx.enter_context(nc.Block())

        @block.sync
        def _(sp):
            sp.dma_start(m.cvec[:, 8:16], c).then_inc(inputs, 16)
            sp.dma_start(m.h, x).then_inc(inputs, 16)
            sp.dma_start(m.con[:], con).then_inc(inputs, 16)
            sp.dma_start(m.conb[:, 0:CON1["all"]], con1).then_inc(inputs, 16)
            stream_weights(sp, m, stream1, first)
            stream_weights(sp, m, stream2, second, earlier=first)
            sp.wait_ge(sem2["layer_done"], 1 + DEPTH)
            sp.dma_start(out, m.h).then_inc(stored, 16)
            sp.wait_ge(stored, 16)

        @block.tensor
        def _(t):
            t.wait_ge(inputs, 64)
            t.wait_ge(ready, 2)
            t.nop().then_inc(first.done, RING)
            tensor1(nc, t, m, sem1, first)
            t.nop().then_inc(second.done, RING)
            t.wait_ge(con_b, 16)
            tensor2(nc, t, m, sem2, second)

        @block.scalar
        def _(a):
            a.wait_ge(inputs, 64)
            nc.scalar.activation(m.cvec[:, 0:8], m.cvec[:, 8:16], ACT.Silu).then_inc(silu_c, 1)
            scalar1(nc, a, m, sem1, first, par1)
            a.wait_ge(sem1["layer_done"], 1 + DEPTH)
            a.dma_start(m.conb[:, 0:CON2["all"]], con2).then_inc(con_b, 16)
            a.wait_ge(con_b, 16)
            scalar2(nc, a, m, sem2, second, par2)

        @block.vector
        def _(v):
            nc.vector.memset(m.zero[:], 0.0)
            nc.vector.memset(m.gr, 0.0)
            nc.vector.memset(m.vb, 0.0).then_inc(ready, 2)
            v.wait_ge(inputs, 64)
            v.wait_ge(silu_c, 1)
            v.nop().then_inc(sem1["layer_done"], 1)
            vector1(nc, v, m, sem1, first)
            v.wait_ge(con_b, 16)
            nc.vector.memset(m.ow[:, 7], 1.0)
            v.drain()
            v.nop().then_inc(sem2["layer_done"], 1)
            vector2(nc, v, m, sem2, second)



def by_column_tile(w):
    k, n = w.shape
    return w.reshape(k // P, P, n // P, P).transpose(2, 1, 0, 3).reshape(n // P, P, k)


def by_row_tile(w):
    return w.reshape(-1, P, 1024)


def columns(v):
    return v.reshape(-1, P).T


def interleave(a, b):
    return np.stack([a, b], 1).reshape(-1, *a.shape[1:])


def ffn_chunks(gate, up, down):
    gu, d = interleave(by_column_tile(gate), by_column_tile(up)), by_row_tile(down)
    parts = [gu[0:2]]
    for f in range(1, NF):
        parts += [gu[2 * f:2 * f + 2], d[f - 1:f]]
    return parts + [d[NF - 1:]]


def pack1(i):
    streams, pars = [], []
    for l in range(DEPTH):
        parts = [i["ada_w"][l].reshape(8, P, 9, 1024).transpose(2, 0, 1, 3).reshape(72, P, 1024)]
        parts += ffn_chunks(i["ffn_w_gate"][l, 0], i["ffn_w_up"][l, 0], i["ffn_w_down"][l, 0])
        w = i["w_in"][l]
        cut = lambda a, n: by_column_tile(w[:, a:a + n])
        parts += [interleave(cut(0, 1024), cut(1024, 1024)), cut(3072, 2048), cut(2048, 1024)]
        small = np.zeros((D, P), np.float32)
        small[:, 0:48] = w[:, 7696:7744]
        small[:, 64:80] = w[:, 5120:5136]
        parts += [by_column_tile(small), cut(5136, 1024), cut(6160, 256), cut(6416, 256), cut(6672, 256),
                  cut(7184, 256), cut(6928, 256), cut(7440, 256)]
        for name in ("cmp_k_w1", "cmp_v_w1"):
            parts.append(i[name][l].reshape(2, 8, P, P).transpose(0, 2, 1, 3).reshape(2, P, 1024))
        for b, name in enumerate(("w_a_out", "w_b_out", "w_c_out")):
            parts.append(interleave(cut(7744 + 1024 * b, 1024), by_column_tile(i[name][l])))
        parts.append(by_column_tile(i["w_o"][l]))
        parts += ffn_chunks(i["ffn_w_gate"][l, 1], i["ffn_w_up"][l, 1], i["ffn_w_down"][l, 1])
        streams.append(np.concatenate(parts))
        assert len(streams[-1]) == N1, (len(streams[-1]), N1)
        p = np.zeros((P, PAR1["all"]), np.float32)
        def put(name, v):
            p[0:v.shape[0], PAR1[name]:PAR1[name] + v.shape[1]] = v
        put("ada_b", columns(i["ada_b"][l]))
        put("ln_g", columns(i["ln_g"][l].reshape(-1)))
        put("ln_b", columns(i["ln_b"][l].reshape(-1)))
        put("aw", i["conv_a_w"][l].reshape(TAPS_A, ND, P).transpose(2, 1, 0).reshape(P, -1))
        put("ab", columns(i["conv_a_b"][l]))
        put("ag", columns(i["norm_a_g"][l]))
        put("abb", columns(i["norm_a_b"][l]))
        put("xw", i["ssm_conv_w"][l].reshape(TAPS_B, NXB, P).transpose(2, 1, 0).reshape(P, -1))
        put("xb", columns(i["ssm_conv_b"][l]))
        put("nw", columns(i["ssm_norm_w"][l]))
        put("dsk", columns(np.repeat(i["ssm_d"][l], 64)))
        put("dtb", i["ssm_dt_bias"][l][:, None])
        put("alog", i["ssm_a_log"][l][:, None])
        for name, src in (("pek", "cmp_pe_k"), ("pev", "cmp_pe_v")):
            put(name, i[src][l].reshape(16, P).T)
        put("w2k", np.tile(i["cmp_k_w2"][l], (1, 2)))
        put("w2v", i["cmp_v_w2"][l])
        pars.append(p)
    return np.concatenate(streams), np.stack(pars)


def pack2(i):
    i = {k[:-2]: v for k, v in i.items() if k.endswith("_2")}
    streams, pars = [], []
    for l in range(DEPTH):
        w = i["w_in"][l]
        cut = lambda a, n: by_column_tile(w[:, a:a + n])
        small = np.zeros((D, P), np.float32)
        small[:, 0:8] = w[:, 2304:2312]
        parts = [cut(0, 512), cut(512, 128), cut(640, 128), by_column_tile(small), cut(768, 256), cut(1024, 256),
                 cut(1280, 512), cut(1792, 512)]
        for name, at in (("w_att_branch", 2312), ("w_m_branch", 3336)):
            g = cut(at, 1024)
            br = by_column_tile(i[name][l]).reshape(4, 2, P, 512).transpose(0, 2, 1, 3).reshape(4, P, 1024)
            for q in range(4):
                parts += [g[2 * q:2 * q + 2], br[q:q + 1]]
        parts.append(by_column_tile(i["w_out"][l]))
        up, down = by_column_tile(i["w_ff1"][l]), by_row_tile(i["w_ff2"][l])
        parts += [up[0:1]] + [np.stack([up[f], down[f - 1]]) for f in range(1, NF2)] + [down[NF2 - 1:]]
        streams.append(np.concatenate(parts))
        assert len(streams[-1]) == N2
        p = np.zeros((P, PAR2["all"]), np.float32)
        def put(name, v):
            p[0:v.shape[0], PAR2[name]:PAR2[name] + v.shape[1]] = v
        put("nmix", columns(i["norm_mix"][l]))
        put("nffn", columns(i["norm_ffn"][l]))
        put("qn", np.tile(i["att_q_norm"][l], 2)[:, None])
        put("kn", np.tile(i["att_k_norm"][l], 2)[:, None])
        order = [4 * g + r for g in range(2) for r in (0, 2, 1, 3)]
        put("sink", np.tile(i["att_sinks"][l][order], (P, 1)))
        put("ib", i["m_gate_bias"][l][0:4, None])
        put("fb", i["m_gate_bias"][l][4:8, None])
        put("hn", columns(i["m_head_norm"][l]))
        pars.append(p)
    return np.concatenate(streams), np.stack(pars)


def kernel(**inputs):
    import concourse.bacc as bacc
    from concourse.bass_utils import run_bass_kernel_spmd

    i = {k: np.asarray(v) for k, v in inputs.items()}
    con, con1, con2 = constants()
    stream1, par1 = pack1(i)
    stream2, par2 = pack2(i)
    arrays = {
        "x_t": np.ascontiguousarray(i["x"][0].T.reshape(ND, P, S).transpose(1, 0, 2)),
        "c_t": np.ascontiguousarray(columns(i["c"][0])),
        "con": con, "con1": con1, "con2": con2,
        "stream1": stream1, "stream2": stream2, "par1": par1, "par2": par2,
    }
    nc = bacc.Bacc("TRN2", target_bir_lowering=False, num_devices=1)
    args = [nc.dram_tensor(k + "_dram", a.shape, F32, kind="ExternalInput").ap() for k, a in arrays.items()]
    out = nc.dram_tensor("out_t", (P, ND, S), F32, kind="ExternalOutput").ap()
    build(nc, *args, out)
    got = run_bass_kernel_spmd(nc, [{k + "_dram": a for k, a in arrays.items()}], core_ids=[0]).results[0]["out_t"]
    return np.ascontiguousarray(np.asarray(got).transpose(2, 1, 0)).reshape(1, S, D)
```

```python
from contextlib import ExitStack

import numpy as np

import concourse.bass as bass
from concourse import mybir

F32 = mybir.dt.float32
F32R = mybir.dt.float32r
BF16 = mybir.dt.bfloat16
ALU = mybir.AluOpType
ACT = mybir.ActivationFunctionType
AX = mybir.AxisListType.X

P = 128
S = 256
D = 1024
ND = D // P
DEPTH = 2
RING = 9
HIGH = 3
FF = 2816
NF = FF // P
FF2 = 4096
NF2 = FF2 // P
TAPS_A, TAPS_B = 31, 4
NXB = 16
CMP = 15
ALPHA = (2.0 * DEPTH) ** 0.25
NEG = -1e30

C_FFN0 = 0
C_MIX = C_FFN0 + 3 * NF
C_GLU = C_MIX
C_XBC = C_GLU + 16
C_Z = C_XBC + 16
C_SMALL = C_Z + 8
C_Q = C_SMALL + 1
C_KC = C_Q + 8
C_VC = C_KC + 2
C_KS = C_VC + 2
C_KW = C_KS + 2
C_VS = C_KW + 2
C_VW = C_VS + 2
C_CK = C_VW + 2
C_CV = C_CK + 2
C_OUT = C_CV + 2
C_WO = C_OUT + 48
C_FFN1 = C_WO + 8
N1 = C_FFN1 + 3 * NF

E_Q = 0
E_K = 4
E_V = 5
E_IF = 6
E_QM = 7
E_KM = 9
E_VM = 11
E_OM = 15
E_BR = 19
E_OUT = E_BR + 24
E_FFN = E_OUT + 8
N2 = E_FFN + 2 * NF2


def offsets(parts):
    at, out = 0, {}
    for name, n in parts:
        out[name] = at
        at += n
    out["all"] = at
    return out


PAR1 = offsets([("ada_b", 72), ("ln_g", 24), ("ln_b", 24), ("aw", ND * TAPS_A), ("ab", 8), ("ag", 8), ("abb", 8),
                ("xw", NXB * TAPS_B), ("xb", NXB), ("nw", 8), ("dsk", 8), ("dtb", 1), ("alog", 1),
                ("pek", 16), ("pev", 16), ("w2k", 128), ("w2v", 64)])
PAR2 = offsets([("nmix", 8), ("nffn", 8), ("qn", 1), ("kn", 1), ("sink", 8), ("ib", 1), ("fb", 1), ("hn", 4)])
CON = offsets([("ident", 128), ("mean", 128), ("ones", 128), ("neg", 128), ("tri", 384), ("eps", 1), ("eps2", 1),
               ("valid", 1)])
CON1 = offsets([("rot", 128), ("dup", 256), ("rdup", 256), ("cos", 256), ("sin", 256), ("cmask", 32)])
CON2 = offsets([("blk", 128), ("mean128", 128), ("rot", 128), ("dup", 256), ("band", 128), ("cosq", 256),
                ("sinq", 256), ("cosk", 256), ("sink", 256), ("tri8", 384)])


def constants():
    f = np.float32
    p = np.arange(P)
    con = np.zeros((P, CON["all"]), f)
    def put(a, off, name, v):
        a[:, off[name]:off[name] + v.shape[1]] = v
    put(con, CON, "ident", np.eye(P, dtype=f))
    put(con, CON, "mean", np.full((P, P), 1.0 / D, f))
    put(con, CON, "ones", np.ones((P, P), f))
    put(con, CON, "neg", np.where(p[None, :] > p[:, None], NEG, 0.0))
    tri = (p[:, None] <= p[None, :]).astype(f)
    tri3 = np.concatenate([tri, np.ones((P, P), f), tri], 1)
    put(con, CON, "tri", tri3)
    put(con, CON, "eps", np.full((P, 1), 1e-5, f))
    put(con, CON, "eps2", np.full((P, 1), 1e-6, f))
    put(con, CON, "valid", (p[:, None] >= 31).astype(f))

    con1 = np.zeros((P, CON1["all"]), f)
    rot = np.zeros((P, P), f)
    for m in range(P):
        d = m % 64
        rot[m + 32 if d < 32 else m - 32, m] = -1.0 if d < 32 else 1.0
    dup = np.zeros((2, P, P), f)
    for par in range(2):
        for m in range(P):
            dup[par, par * 64 + m % 64, m] = 1.0
    put(con1, CON1, "rot", rot)
    put(con1, CON1, "dup", np.concatenate([dup[0], dup[1]], 1))
    put(con1, CON1, "rdup", np.concatenate([rot @ dup[0], rot @ dup[1]], 1))
    half = 32
    inv = (10000.0 ** (-np.arange(half, dtype=f) / f(half))).astype(f)
    ang = np.arange(S, dtype=f)[:, None] * inv[None, :]
    put(con1, CON1, "cos", np.tile(np.cos(ang).T, (4, 1)).astype(f))
    put(con1, CON1, "sin", np.tile(np.sin(ang).T, (4, 1)).astype(f))
    t = np.arange(S).reshape(2, P)
    ends = np.arange(16) * 16 + 31
    cm = np.where(ends[None, None, :] <= t[:, :, None], 0.0, NEG)
    put(con1, CON1, "cmask", cm.transpose(1, 0, 2).reshape(P, 32))

    con2 = np.zeros((P, CON2["all"]), f)
    put(con2, CON2, "blk", np.kron(np.eye(2), np.full((64, 64), 1.0 / 64)))
    put(con2, CON2, "mean128", np.full((P, P), 1.0 / P, f))
    rot2 = np.zeros((P, P), f)
    for m in range(P):
        d = m % 64
        if d < 16:
            rot2[m + 8 if d < 8 else m - 8, m] = -1.0 if d < 8 else 1.0
    put(con2, CON2, "rot", rot2)
    put(con2, CON2, "dup", np.concatenate([dup[0], dup[1]], 1))
    put(con2, CON2, "band", np.where(p[None, :] <= p[:, None], NEG, 0.0))
    inv = (f(500000.0) ** (-np.arange(0, 16, 2, dtype=f) / f(16))).astype(f)
    ang = (np.arange(S, dtype=f)[:, None] * inv[None, :]).T
    cos, sin = np.ones((64, S), f), np.zeros((64, S), f)
    cos[0:8] = cos[8:16] = np.cos(ang)
    sin[0:8] = sin[8:16] = np.sin(ang)
    for name, tab, by in (("cosq", cos, 0.125), ("sinq", sin, 0.125), ("cosk", cos, 1.0), ("sink", sin, 1.0)):
        put(con2, CON2, name, np.tile(tab, (2, 1)) * f(by))
    put(con2, CON2, "tri8", tri3 * f(0.125))
    return con, con1, con2


class Modulation:

    def __init__(self, sem):
        self.landed = [sem(f"ada_landed{k}") for k in range(ND)]
        self.used, self.summed, self.columns = sem("ada_used"), sem("ada_summed"), sem("ada_columns")

    def group(self, l, q, it=0):
        return l * 9 + 3 + 6 * q + it


class Stream:

    def __init__(self, per_layer, landed, done, earlier=None):
        self.n, self.landed, self.done, self.earlier = per_layer, landed, done, earlier

    def landed_before(self, slot):
        return DEPTH * self.earlier.uses(slot) if self.earlier else 0

    def done_before(self):
        return DEPTH * self.earlier.n if self.earlier else 0

    def uses(self, slot):
        return (self.n - slot + RING - 1) // RING

    def landed_value(self, l, i, rounds=0):
        return 16 * (self.landed_before(i % RING) + l * self.uses(i % RING) + i // RING + 1 + rounds)

    def done_value(self, l, i, rounds=0):
        return self.done_before() + l * self.n + i + 1 + RING + rounds * RING

    def last(self, slot):
        return self.n - 1 - (self.n - 1 - slot) % RING


SIGNALS1 = dict(
    layer_done=1, par=16, u=1, umod=16, uhi=16, ulo=16, hi=6 * NF, lo=4 * NF, lo_down=2 * NF,
    silu=2 * NF, hid=2 * NF, hidhi=2 * NF, hidlo=2 * NF, scaled=24, resid=24, mu=4, cent=32,
    sq=40, var=5, sd=5, sg=8, glu=8, copied=23, aconv=8, xconv=16, xsilu=16, kpe=2, rotp=12, rope=12,
    gelu=1, kc1=1, kcr=1, kc2=1, kcmp=1, vb=1, vbc=1, anrs=8, anorm=8, pv=8, outsg=24, outm=24, dtexp=1, dtv=1,
    dtt=1, dttc=1, acs=1, acsc=1, xt=4, xdt=4, cb=4, cbm=4, bc=16, ee=16, arg=16, mm=16, yh=16, ysil=8, bnorm=8,
    cs=2, cmx=2, cex=2, cp=2, ct=2, ptc=2, sc=16, nmx=16, ex=16, pr=16, tr=16, ptt=16, oc=4)
SIGNALS2 = dict(
    layer_done=1, par=16, usq=16, uvar=2, usd=2, u=1, copied=11, hsq=4, hvar=9, hsd=9, qn=5, rotp=5, rope=5, dup=1,
    dupc=1, fexp=1, mt=1, rt=1, mtc=1, qk=4, qkm=4, bc=4, me=4, arg=4, ee=4, mm=4, num=4, absd=4, hh=4, hm=4,
    sc=4, nmx=4, ex=4, pr=4, tr=4, ptt=4, pv=4, oc=2, outsg=8, outm=8, relu=NF2, hid=NF2, hidhi=NF2, hidlo=NF2, xres=8,
    umod=8, uhi=8, ulo=8, hi=2 * NF2, lo=NF2, lo_down=NF2)


class Buffers:
    pass


def memory(nc, ctx):
    def sb(name, n, dt=F32):
        return ctx.enter_context(nc.sbuf_tensor(name, [P, n], dt))
    def typed_twice(name, n):
        with nc.sbuf_tensor(name, [P, n], F32) as whole:
            pass
        return whole, sb(name + "_parts", n, F32R)
    m = Buffers()
    def tiles(a, n):
        return a.rearrange("p (n t) -> p n t", n=n)
    m.ring, m.low = typed_twice("ring", RING * 1024)
    m.high = sb("high", HIGH * 1024, F32R)
    m.h = tiles(sb("h", ND * S)[:], ND)
    u, ulo = typed_twice("u", ND * S)
    m.u, m.ulo = tiles(u[:], ND), tiles(ulo[:], ND)
    eb = sb("eb", 2048)
    pt, ptr = typed_twice("pt", 4096)
    ap_ = sb("ap", ND * (S + TAPS_A - 1))
    ac, acr = typed_twice("ac", ND * S)
    xp = sb("xp", NXB * (S + TAPS_B - 1))
    xc = sb("xc", NXB * S)
    z = sb("z", ND * S)
    qr = sb("qr", ND * S)
    kv = sb("kv", 2048)
    kraw = sb("kraw", 1024)
    kr = sb("kr", 2048)
    vt = sb("vt", 1024)
    gr = sb("gr", 512)
    vb = sb("vb", 1024)
    small = sb("small", 512)
    sg = sb("sg", 1024)
    st = sb("st", 512)
    m.con = sb("con", CON["all"])
    m.con_of = lambda name, n=P, at=0: m.con[:, CON[name] + at:CON[name] + at + n]
    m.conb = sb("conb", max(CON1["all"], CON2["all"]))
    m.par = sb("par", PAR1["all"])
    m.cvec = sb("cvec", 16)
    m.mod = sb("mod", 72)
    m.sc1 = sb("sc1", 24)
    m.raw = sb("raw", 48)
    m.raw_moved = sb("raw_moved", 40)
    m.zero = sb("zero", 512, BF16)

    m.eb, m.pt = eb, pt
    m.ada = [buf[:, k * 1024:(k + 1) * 1024] for buf, n in ((xc, 4), (z, 2), (qr, 2)) for k in range(n)]
    m.ada_acc = eb[:, 0:1024]
    m.uhi = tiles(acr[:], ND)
    m.sq = tiles(eb[:], ND)
    m.silu = tiles(pt[:, 0:768], 3)
    m.hid, m.hidlo = tiles(pt[:, 768:1536], 3), tiles(ptr[:, 768:1536], 3)
    m.hidhi = tiles(ptr[:, 1536:2304], 3)
    m.apad = tiles(ap_[:], ND)
    m.merged = tiles(ap_[:, 0:ND * S], ND)
    m.ac = tiles(ac[:], ND)
    m.oT = m.ac
    m.xpad = tiles(xp[:], NXB)
    m.xdt = xp[:, 0:2048].rearrange("p (a f) -> p a f", a=2)
    m.yb = tiles(xp[:, 2048:4096], ND)
    m.xc = tiles(xc[:], NXB)
    m.pcmp = xc[:, 0:1024].rearrange("p (a h n) -> p a h n", a=2, h=16)
    m.ptc = xc[:, 1024:2048].rearrange("p (g t) -> p g t", g=4)
    m.z = tiles(z[:], ND)
    m.qr = tiles(qr[:], ND)
    m.kc = kv[:, 0:1024].rearrange("p (g t) -> p g t", g=4)
    m.vc = kv[:, 1024:2048].rearrange("p (g t) -> p g t", g=4)
    m.kp = [eb[:, 0:960].rearrange("p (j c) -> p j c", j=16), eb[:, 1024:1984].rearrange("p (j c) -> p j c", j=16)]
    m.kraw = kraw[:].rearrange("p (b n t) -> p b n t", b=2, n=2)
    m.kr = kr[:].rearrange("p (b g t) -> p b g t", b=2, g=4)
    m.vt = vt[:].rearrange("p (b a f) -> p b a f", b=2, a=2)
    m.gr = gr[:].rearrange("p (g r n) -> p g r n", g=4, r=4)
    m.vb = vb[:].rearrange("p (g i f) -> p g i f", g=4, i=2)
    m.gk = small[:, 0:60]
    m.kcr = small[:, 60:120]
    m.kcmp = small[:, 120:180]
    m.gates = small[:, 180:276].rearrange("p (a c) -> p a c", a=2)
    m.dtt = small[:, 276:340]
    m.nacs = small[:, 340:372]
    m.cst = small[:, 372:436].rearrange("p (k a h) -> p k a h", k=2, a=2)
    m.nmx = small[:, 436:444].rearrange("p (b r) -> p b r", b=2)
    m.sums = small[:, 444:452].rearrange("p (b r) -> p b r", b=2)
    m.fac = small[:, 452:460].rearrange("p (b r) -> p b r", b=2)
    m.esink = small[:, 460:468].rearrange("p (b r) -> p b r", b=2)
    m.aexp = small[:, 468:469]
    m.dtw = kv[0:16, 0:1280].rearrange("p (k t) -> p k t", k=5)
    m.cbm = kv[:, 1280:2048].rearrange("p (b t) -> p b t", b=2)
    m.dtraw = pt[0:16, 2048:2304]
    m.sg = tiles(sg[:], 4)
    m.sd, m.rs = st[:, 0:256], st[:, 256:512]
    m.ee = pt[:, 0:768].rearrange("p (b t) -> p b t", b=2)
    m.mm = pt[:, 768:1536].rearrange("p (b t) -> p b t", b=2)
    m.e = eb[:].rearrange("p (b r k) -> p b r k", b=2, r=4)
    m.ptt = pt[:].rearrange("p (b k r q) -> p b k r q", b=4, k=2, r=4)
    m.qk_raw = [ac[:, i * 256:(i + 1) * 256] for i in range(5)]
    m.hsq = [eb[:, i * 256:(i + 1) * 256] for i in range(5)]
    m.tmp = [sg[:, 0:256], sg[:, 256:512]]
    m.qa = tiles(qr[:, 0:1024], 4)
    m.qm = qr[:, 1024:1536].rearrange("p (n t) -> p n t", n=2)
    m.km = qr[:, 1536:2048].rearrange("p (n t) -> p n t", n=2)
    m.ka = kr[:, 0:512].rearrange("p (g t) -> p g t", g=2)
    m.kda = kr[:, 512:768]
    m.va = vt[:, 0:256].rearrange("p (a f) -> p a f", a=2)
    m.vm = xc[:, 0:1024].rearrange("p (a f) -> p a f", a=2)
    m.om = tiles(xc[:, 1024:2048], 4)
    m.ow = kv[0:4, 0:2048].rearrange("p (k t) -> p k t", k=8)
    m.att = tiles(z[:, 0:1024], 4)
    m.hm = tiles(z[:, 1024:2048], 4)
    m.rt = small[:, 0:8].rearrange("p (a h) -> p a h", a=2)
    m.qkm = xc[:, 2048:2816].rearrange("p (b t) -> p b t", b=2)
    m.em = xc[:, 2816:3328].rearrange("p (b t) -> p b t", b=2)
    m.den = xc[:, 3328:3840].rearrange("p (b t) -> p b t", b=2)
    m.mx = small[:, 8:16].rearrange("p (b r) -> p b r", b=2)
    m.ps = ctx.enter_context(nc.psum_tensor("ps", [P, 8, 512], F32))
    return m


def chunk_tile(m, i, k, a=0, b=P):
    at = (i % RING) * 1024 + k * P
    return m.ring[:, at + a:at + b]


def high_of(m, i):
    return m.high[:, (i % HIGH) * 1024:(i % HIGH + 1) * 1024]


def low_of(m, i):
    return m.low[:, (i % RING) * 1024:(i % RING + 1) * 1024]


def chunk_of(m, i):
    return m.ring[:, (i % RING) * 1024:(i % RING + 1) * 1024]


def product3(mm, out, m, i, k, xh, xl, start, stop, **kw):
    hi, lo = high_of(m, i)[:, k * P:(k + 1) * P], low_of(m, i)[:, k * P:(k + 1) * P]
    mm(out, hi, xh, start=start, stop=False, **kw)
    mm(out, hi, xl, start=False, stop=False, **kw)
    return mm(out, lo, xh, start=False, stop=stop, **kw)


def two(ps, bank, a=0, n=256):
    return ps[:, bank, a:a + 2 * n].rearrange("p (n t) -> p n t", n=2)



def stream_weights(sp, m, source, stream):
    def load(l, i, rounds=0):
        src = source[bass.ds(l * stream.n + i + rounds * RING, 1)].rearrange("a p n -> (a p) n")
        at = (i % RING) * 1024
        sp.dma_start(m.ring[:, at:at + 1024], src).then_inc(stream.landed[i % RING], 16)

    whole = stream.n // RING
    with sp.Fori(0, DEPTH) as l:
        for s in range(RING):
            if stream.earlier:
                sp.wait_ge(stream.done, stream.earlier.done_value(DEPTH - 1, stream.earlier.last(s)))
            sp.wait_ge(stream.done, stream.done_value(l, stream.last(s) - stream.n))
            load(l, s)
        with sp.Fori(0, whole - 1) as it:
            for s in range(RING):
                sp.wait_ge(stream.done, stream.done_value(l, s, it))
                load(l, RING + s, it)
        for i in range(whole * RING, stream.n):
            sp.wait_ge(stream.done, stream.done_value(l, i - RING))
            load(l, i)



def column_sums(t, mm, m, ada, g):
    t.wait_ge(ada.summed, g + 1)
    for j in range(8):
        last = mm(m.ps[:, 7, j:j + 1], m.ada_acc[:, j * P:(j + 1) * P], m.con_of("ones", 1), start=True, stop=True)
    last.then_inc(ada.columns, 1)


def tensor1(nc, t, m, sem, stream, ada):
    ps, con = m.ps, m.con_of
    landed, done = stream.landed, stream.done
    mm = nc.tensor.matmul

    def layer(l):
        at = lambda name, k: l * SIGNALS1[name] + k
        landed_at = lambda i, rounds=0: stream.landed_value(l, i, rounds)
        done_at = lambda i, rounds=0: stream.done_value(l, i, rounds)
        c1 = lambda name, n=P, at=0: m.conb[:, CON1[name] + at:CON1[name] + at + n]

        def project(i, out, k0=0, rounds=0, cols=(0, P)):
            t.wait_ge(landed[i % RING], landed_at(i, rounds))
            for k in range(ND):
                last = mm(out, chunk_tile(m, i, k, *cols), m.u[:, k], start=k == 0, stop=k == ND - 1)
            return last

        def accumulate_ones(bank, src, signal, k0, ones):
            for n in range(ND):
                t.wait_ge(sem[signal], at(signal, k0 + n + 1))
                last = mm(ps[:, bank, 0:S], ones, src[:, n], start=n == 0, stop=n == ND - 1)
            return last

        def layer_norm(at, src, sq, mu_bank, var_bank, resid_k):
            accumulate_ones(mu_bank, src, resid_k[0], resid_k[1], con("mean")).then_inc(sem["mu"], 1)
            rms(at[0], sq, var_bank)

        def rms(k, sq, bank):
            accumulate_ones(bank, sq, "sq", 8 * k, con("mean")).then_inc(sem["var"], 1)

        def ffn(q, cb, per):
            if q == 1:
                t.wait_ge(sem["sd"], at("sd", 4))
            for b in range(4):
                mm(ps[:, b, :], m.zero[:, 0:P], m.zero[:], start=True, stop=False, skip_group_check=True)

            def up(i, f, fk, rounds=0):
                for c in range(2):
                    t.wait_ge(sem["lo"], at("lo", 2 * NF * q + 2 * fk + c + 1))
                    for k in range(ND):
                        if f == 0 and c == 0:
                            t.wait_ge(sem["ulo"], at("ulo", 8 * q + k + 1))
                        last = product3(mm, ps[:, 4 + f % 3, c * S:(c + 1) * S], m, i + c, k, m.uhi[:, k], m.ulo[:, k],
                                        start=k == 0, stop=k == ND - 1)
                    last.then_inc(done, 1)

            def down(i, f, fk, rounds=0, last=False):
                t.wait_ge(sem["lo_down"], at("lo_down", q * NF + fk + 1))
                t.wait_ge(sem["hidlo"], at("hidlo", q * NF + fk + 1))
                for n in range(ND):
                    x = product3(mm, ps[:, n // 2, (n % 2) * S:(n % 2 + 1) * S], m, i, n, m.hidhi[:, f % 3],
                                 m.hidlo[:, f % 3], start=False, stop=last, skip_group_check=True)
                x.then_inc(done, 1)

            up(cb, 0, 0)
            with t.Fori(0, 18 // per) as it:
                for j in range(per):
                    up(cb + 2 + 3 * j, 1 + j, per * it + 1 + j)
                    if j == per - 1:
                        column_sums(t, mm, m, ada, ada.group(l, q, it))
                    down(cb + 4 + 3 * j, j, per * it + j)
            for f in range(19, NF):
                up(cb + 3 * f - 1, f, f)
                down(cb + 3 * f + 1, f - 1, f - 1)
            down(cb + 65, 21, 21, last=True)

        ffn(0, C_FFN0, 3)
        layer_norm((0,), m.h, m.u, 4, 5, ("resid", 0))

        t.wait_ge(sem["u"], at("u", 1))
        unit = lambda j: 4 + j % 4
        j = 0
        for n in range(8):
            if n >= 4:
                t.wait_ge(sem["glu"], at("glu", n - 3))
            project(C_GLU + 2 * n, ps[:, unit(j), 0:S]).then_inc(done, 1)
            project(C_GLU + 2 * n + 1, ps[:, unit(j), S:2 * S]).then_inc(done, 1)
            j += 1
        for n in range(12):
            if n < 4:
                t.wait_ge(sem["glu"], at("glu", n + 5))
            else:
                t.wait_ge(sem["copied"], at("copied", n - 3))
            project(C_XBC + 2 * n, ps[:, unit(j), 0:S]).then_inc(done, 1)
            project(C_XBC + 2 * n + 1, ps[:, unit(j), S:2 * S]).then_inc(done, 1)
            j += 1
        t.wait_ge(sem["copied"], at("copied", 9))
        t.wait_ge(landed[C_SMALL % RING], landed_at(C_SMALL))
        for a in range(2):
            for k in range(ND):
                mm(ps[:, unit(j), a * 48:a * 48 + 48], m.u[:, k, a * P:(a + 1) * P],
                   chunk_tile(m, C_SMALL, k, 0, 48), start=k == 0, stop=k == ND - 1)
        for k in range(ND):
            last = mm(ps[0:16, unit(j), S:2 * S], chunk_tile(m, C_SMALL, k, 64, 80), m.u[:, k],
                      start=k == 0, stop=k == ND - 1)
        last.then_inc(done, 1)
        j += 1
        for n in range(8):
            t.wait_ge(sem["copied"], at("copied", 10 + n))
            project(C_Q + 2 * n, ps[:, unit(j), 0:S]).then_inc(done, 1)
            project(C_Q + 2 * n + 1, ps[:, unit(j), S:2 * S]).then_inc(done, 1)
            j += 1
        for b in range(2):
            t.wait_ge(sem["copied"], at("copied", 18 + b))
            for c in range(2):
                i = C_VS + 2 * b + c
                t.wait_ge(landed[i % RING], landed_at(i))
                for a in range(2):
                    for k in range(ND):
                        last = mm(ps[:, unit(j), a * S + c * P:a * S + (c + 1) * P], m.u[:, k, a * P:(a + 1) * P],
                                  chunk_tile(m, i, k), start=k == 0, stop=k == ND - 1)
                last.then_inc(done, 1)
            j += 1
        for n in range(4):
            t.wait_ge(sem["copied"], at("copied", 20 + n))
            for c in range(2):
                last = mm(ps[:, unit(j), c * S:(c + 1) * S], c1("rot"), m.qr[:, 2 * n + c], start=True, stop=True)
            last.then_inc(sem["rotp"], 1)
            j += 1
        for b in range(2):
            for g in range(4):
                t.wait_ge(sem["rope"], at("rope", 4 * b + g + 1))
                src = m.kraw[:, b, g // 2]
                mm(ps[:, unit(j), 0:S], c1("dup", P, (g % 2) * P), src, start=True, stop=True)
                mm(ps[:, unit(j), S:2 * S], c1("rdup", P, (g % 2) * P), src, start=True, stop=True)\
                    .then_inc(sem["rotp"], 1)
                j += 1
        t.wait_ge(sem["rope"], at("rope", 9))
        for b in range(2):
            t.wait_ge(sem["kpe"], at("kpe", b + 1))
            for c in range(2):
                i = C_CK + 2 * b + c
                t.wait_ge(landed[i % RING], landed_at(i))
                for k in range(8):
                    last = mm(ps[:, unit(j), b * 64:b * 64 + 60], chunk_tile(m, i, k), m.kp[b][:, 8 * c + k],
                              start=c == 0 and k == 0, stop=c == 1 and k == 7)
                last.then_inc(done, 1)
        j += 1
        t.wait_ge(sem["rope"], at("rope", 10))
        t.wait_ge(sem["gelu"], at("gelu", 1))
        mm(ps[:, unit(j), 0:60], m.par[:, PAR1["w2k"]:PAR1["w2k"] + P], m.gk, start=True, stop=True)\
            .then_inc(sem["kc1"], 1)
        j += 1
        t.wait_ge(sem["rope"], at("rope", 11))
        t.wait_ge(sem["kcr"], at("kcr", 1))
        mm(ps[:, unit(j), 0:60], c1("rot"), m.kcr, start=True, stop=True).then_inc(sem["kc2"], 1)
        j += 1
        t.wait_ge(sem["rope"], at("rope", 12))
        for g in range(4):
            last = mm(ps[:, unit(j), g * 64:(g + 1) * 64], m.gr[:, g].rearrange("p r n -> p (r n)"),
                      m.par[:, PAR1["w2v"]:PAR1["w2v"] + 64], start=True, stop=True)
        last.then_inc(sem["vb"], 1)
        j += 1

        layer_norm((1,), m.ac, m.sq, 0, 1, ("aconv", 0))

        def out_tile(branch, src, n, j):
            i = C_OUT + 16 * branch + 2 * n
            project(i, ps[:, unit(j), 0:S]).then_inc(done, 1)
            if n == 0 and branch == 0:
                t.wait_ge(sem["anorm"], at("anorm", 8))
            if n == 0 and branch == 1:
                t.wait_ge(sem["bnorm"], at("bnorm", 8))
            if n == 0 and branch == 2:
                t.wait_ge(sem["oc"], at("oc", 4))
            t.wait_ge(landed[(i + 1) % RING], landed_at(i + 1))
            for k in range(ND):
                last = mm(ps[:, unit(j), S:2 * S], chunk_tile(m, i + 1, k), src[:, k], start=k == 0, stop=k == 7)
            last.then_inc(done, 1)
            return j + 1

        t.wait_ge(sem["gelu"], at("gelu", 1))
        j = out_tile(0, m.ac, 0, j)
        t.wait_ge(sem["kcr"], at("kcr", 1))
        j = out_tile(0, m.ac, 1, j)
        t.wait_ge(sem["kcmp"], at("kcmp", 1))
        j = out_tile(0, m.ac, 2, j)
        t.wait_ge(sem["vbc"], at("vbc", 1))
        j = out_tile(0, m.ac, 3, j)
        for n in range(4, 8):
            t.wait_ge(sem["outm"], at("outm", n - 3))
            j = out_tile(0, m.ac, n, j)

        ident16 = m.con[0:16, CON["ident"]:CON["ident"] + 16]
        t.wait_ge(sem["outm"], at("outm", 5))
        t.wait_ge(sem["dtv"], at("dtv", 1))
        for k in range(4):
            last = mm(ps[:, unit(j), 16 * k:16 * k + 16], m.dtw[:, 3 + k // 2, (k % 2) * P:(k % 2 + 1) * P],
                      ident16, start=True, stop=True)
        last.then_inc(sem["dtt"], 1)
        j += 1
        t.wait_ge(sem["outm"], at("outm", 6))
        t.wait_ge(sem["dttc"], at("dttc", 1))
        tri, ones = con("tri"), con("ones")
        adt = [m.dtt[:, 32:48], m.dtt[:, 48:64]]
        b = unit(j)
        mm(ps[:, b, 0:16], tri, adt[0], start=True, stop=True)
        mm(ps[:, b, 16:32], ones, adt[0], start=True, stop=False)
        mm(ps[:, b, 16:32], tri, adt[1], start=False, stop=True)
        mm(ps[0:16, b, 256:512], adt[0], con("tri", 256), start=True, stop=False)
        mm(ps[0:16, b, 384:512], adt[1], tri, start=False, stop=True).then_inc(sem["acs"], 1)
        j += 1
        for h in range(4):
            if h < 2:
                t.wait_ge(sem["outm"], at("outm", 7 + h))
            elif h == 2:
                t.wait_ge(sem["dttc"], at("dttc", 1))
            else:
                t.wait_ge(sem["acsc"], at("acsc", 1))
            t.wait_ge(sem["xsilu"], at("xsilu", 8))
            for n in range(4):
                f = 4 * (h % 2) + n
                last = nc.tensor.transpose(ps[:, unit(j), n * P:(n + 1) * P],
                                           m.xc[:, f, (h // 2) * P:(h // 2 + 1) * P], con("ident"))
            last.then_inc(sem["xt"], 1)
            j += 1
        def ssm_head(h):
            t.wait_ge(sem["mm"], at("mm", h + 1))
            out = ps[64 * (h % 2):64 * (h % 2) + 64, h // 4, ((h // 2) % 2) * S:((h // 2) % 2 + 1) * S]
            x = m.xdt[:, :, 64 * h:64 * h + 64]
            mm(out, x[:, 0], m.mm[:, h % 2, 0:S], start=True, stop=False)
            mm(out[:, P:S], x[:, 1], m.mm[:, h % 2, S:S + P], start=False, stop=True).then_inc(sem["yh"], 1)

        t.wait_ge(sem["xsilu"], at("xsilu", 16))
        t.wait_ge(sem["acsc"], at("acsc", 1))
        for g in range(4):
            if g == 0:
                t.wait_ge(sem["xdt"], at("xdt", 1))
            else:
                t.wait_ge(sem["arg"], at("arg", 4 * g - 3))
            B, C = m.xc[:, 8 + g], m.xc[:, 12 + g]
            mm(ps[:, unit(j), 0:256], B[:, 0:P], C, start=True, stop=True)
            mm(ps[:, unit(j), 256:384], B[:, P:S], C[:, P:S], start=True, stop=True).then_inc(sem["cb"], 1)
            j += 1
            for r in range(4):
                h = 4 * g + r
                if r == 3:
                    t.wait_ge(sem["cbm"], at("cbm", g + 1))
                elif g == 0:
                    t.wait_ge(sem["xdt"], at("xdt", r + 2))
                else:
                    t.wait_ge(sem["arg"], at("arg", 4 * g - 2 + r))
                mm(ps[:, unit(j), 0:S], m.con[0:16, CON["ident"] + h:CON["ident"] + h + 1].to_broadcast([16, P]),
                   m.dtw[:, 2], start=True, stop=True).then_inc(sem["bc"], 1)
                j += 1
                if h >= 1:
                    ssm_head(h - 1)
        ssm_head(15)
        rms(2, m.sq, 4)
        for n in range(8):
            if n < 4:
                t.wait_ge(sem["arg"], at("arg", 13 + n))
            else:
                t.wait_ge(sem["outm"], at("outm", 5 + n))
            j = out_tile(1, m.yb, n, j)

        kcmp = m.kcmp.rearrange("p (g n) -> p g n", g=4)
        for a in range(2):
            t.wait_ge(sem["outm"], at("outm", 14 + 2 * a))
            for h in range(16):
                lo = 64 * (h % 2)
                o = (h // 2) * 16
                last = mm(ps[:, unit(j + h % 2), o:o + CMP], m.qr[lo:lo + 64, h // 2, a * P:(a + 1) * P],
                          kcmp[lo:lo + 64, h // 4], start=True, stop=True)
            last.then_inc(sem["cs"], 1)
            j += 2
        for k in range(2):
            t.wait_ge(sem["cmx"], at("cmx", 1))
            t.wait_ge(sem["cp"], at("cp", 2))
            for g in (2 * k, 2 * k + 1):
                for a in range(2):
                    last = nc.tensor.transpose(ps[:, unit(j), (g % 2) * S + a * P:(g % 2) * S + (a + 1) * P],
                                               m.pcmp[:, a, 4 * g:4 * g + 4].rearrange("p r n -> p (r n)"),
                                               con("ident"))
            last.then_inc(sem["ct"], 1)
            j += 1

        def scores(i):
            g, a, b = i // 4, (i // 2) % 2, i % 2
            kl = P * (a + 1)
            if i >= 2:
                t.wait_ge(sem["ex"], at("ex", i - 1))
            for r in range(4):
                h = 4 * g + r
                lo = 64 * (h % 2)
                last = mm(score_view(ps, i, a)[:, place_of(r)], m.qr[lo:lo + 64, h // 2, a * P:(a + 1) * P],
                          m.kr[lo:lo + 64, b, g, 0:kl], start=True, stop=True)
            last.then_inc(sem["sc"], 1)

        def turn(i):
            a = (i // 2) % 2
            t.wait_ge(sem["pr"], at("pr", i + 1))
            if i >= 1:
                t.wait_ge(sem["ptt"], at("ptt", i))
            for k in range(a + 1):
                for r in range(4):
                    last = nc.tensor.transpose(ps[:, 2 + k, r * P:(r + 1) * P], m.e[:, i % 2, r, k * P:(k + 1) * P],
                                               con("ident"))
            last.then_inc(sem["tr"], 1)

        def values(i2):
            g, a = i2 // 2, i2 % 2
            o = ps[:, g % 2, :].rearrange("p (i t) -> p i t", i=2)
            if a == 0:
                if g >= 2:
                    t.wait_ge(sem["oc"], at("oc", g - 1))
                for i in range(2):
                    mm(o[:, i], m.vb[:, g, i], m.ptc[:, g], start=i == 0, stop=False, skip_group_check=True)
            t.wait_ge(sem["ptt"], at("ptt", 2 * i2 + 2))
            for b in range(2):
                for k in range(a + 1):
                    for par in range(2):
                        last = mm(o[64 * par:64 * par + 64, :, a * P:(a + 1) * P],
                                  m.vt[:, b, k, g * 64:(g + 1) * 64],
                                  m.ptt[:, (2 * i2 + b) % 4, k, 2 * par:2 * par + 2], start=False, stop=a == 1 and b == 1 and k == 1,
                                  skip_group_check=True)
            last.then_inc(sem["pv"], 1)

        t.wait_ge(sem["ptc"], at("ptc", 2))
        scores(0)
        for i in range(16):
            if i + 1 < 16:
                scores(i + 1)
            turn(i)
            if i >= 2 and i % 2 == 0:
                values(i // 2 - 1)
        values(7)
        for n in range(8):
            if n < 4:
                t.wait_ge(sem["ptc"], at("ptc", 2))
            else:
                t.wait_ge(sem["outm"], at("outm", 13 + n))
            j = out_tile(2, m.oT, n, j)

        t.wait_ge(sem["outm"], at("outm", 24))
        for n in range(8):
            if n >= 4:
                t.wait_ge(sem["scaled"], at("scaled", 5 + n))
            t.wait_ge(landed[(C_WO + n) % RING], landed_at(C_WO + n))
            for k in range(ND):
                last = mm(ps[:, unit(j), 0:S], chunk_tile(m, C_WO + n, k), m.merged[:, k], start=k == 0, stop=k == 7)
            last.then_inc(done, 1)
            j += 1
        layer_norm((3,), m.h, m.u, 0, 1, ("resid", 8))

        ffn(1, C_FFN1, 6)
        layer_norm((4,), m.h, m.u, 4, 5, ("resid", 16))

    for g in range(3):
        column_sums(t, mm, m, ada, g)
    with t.Fori(0, DEPTH) as l:
        layer(l)


def place_of(r):
    return (r % 2) * 2 + r // 2


def score_view(ps, i, a):
    b = 4 + 2 * (i % 2)
    return ps[:, b:b + 2, :].rearrange("p b (r k) -> p (b r) k", r=2)[:, :, 0:P * (a + 1)]





def scalar1(nc, a, m, sem, stream, par_source):
    ps, con = m.ps, m.con_of
    landed, done = stream.landed, stream.done
    act = nc.scalar.activation

    def layer(l):
        at = lambda name, k: l * SIGNALS1[name] + k
        landed_at = lambda i, rounds=0: stream.landed_value(l, i, rounds)
        done_at = lambda i, rounds=0: stream.done_value(l, i, rounds)
        par = lambda name, at=0, n=1: m.par[:, PAR1[name] + at:PAR1[name] + at + n]
        gate = lambda i, n: m.mod[:, (3 * i + 2) * 8 + n:(3 * i + 2) * 8 + n + 1]
        bank = lambda j: 4 + j % 4

        a.wait_ge(sem["layer_done"], at("layer_done", 1))
        a.dma_start(m.par[:], par_source[bass.ds(l, 1)].rearrange("a p n -> (a p) n")).then_inc(sem["par"], 16)

        def high(i, rounds=0):
            act(high_of(m, i), chunk_of(m, i), ACT.Copy).then_inc(sem["hi"], 1)

        def first_highs(cb):
            for i in range(cb, cb + HIGH):
                a.wait_ge(landed[i % RING], landed_at(i))
                high(i)

        def later_high(i, rounds=0):
            a.wait_ge(landed[i % RING], landed_at(i, rounds))
            a.wait_ge(done, done_at(i - HIGH, rounds))
            high(i)

        def ffn(q, cb, per):
            for n in range(ND):
                a.wait_ge(sem["umod"], at("umod", 8 * q + n + 1))
                act(m.uhi[:, n], m.u[:, n], ACT.Copy).then_inc(sem["uhi"], 1)

            def silu(i, f, rounds=0):
                a.wait_ge(done, done_at(i, rounds))
                act(m.silu[:, f % 3], ps[:, 4 + f % 3, 0:S], ACT.Silu).then_inc(sem["silu"], 1)

            def hidden_high(f, fk):
                a.wait_ge(sem["hid"], at("hid", q * NF + fk + 1))
                act(m.hidhi[:, f % 3], m.hid[:, f % 3], ACT.Copy).then_inc(sem["hidhi"], 1)

            def step(i, f, fk, rounds=0):
                silu(i, f, rounds)
                later_high(i + 3, rounds)
                hidden_high(f, fk)
                later_high(i + 4, rounds)
                later_high(i + 5, rounds)

            later_high(cb + 3)
            silu(cb + 1, 0)
            later_high(cb + 4)
            hidden_high(0, 0)
            later_high(cb + 5)
            with a.Fori(0, 18 // per) as it:
                for j in range(per):
                    step(cb + 3 + 3 * j, 1 + j, per * it + 1 + j, it * (per // 3))
            for f in range(19, 21):
                step(cb + 3 * f, f, f)
            silu(cb + 63, 21)
            hidden_high(21, 21)
            a.wait_ge(done, done_at(cb + 65))
            for n in range(ND):
                act(m.u[:, n], ps[:, n // 2, (n % 2) * S:(n % 2 + 1) * S], ACT.Identity, scale=gate(2 * q, n))\
                    .then_inc(sem["scaled"], 1)

        def squares(k, src, dst, signal, k0, var_bank):
            for n in range(ND):
                a.wait_ge(sem[signal], at(signal, k0 + n + 1))
                act(dst[:, n], src[:, n], ACT.Square).then_inc(sem["sq"], 1)
            a.wait_ge(sem["var"], at("var", k + 1))
            act(m.sd, ps[:, var_bank, 0:S], ACT.Sqrt, bias=con("eps", 1)).then_inc(sem["sd"], 1)

        first_highs(C_FFN0)
        ffn(0, C_FFN0, 3)
        squares(0, m.h, m.u, "cent", 0, 5)

        j = 0
        for n in range(8):
            a.wait_ge(done, done_at(C_GLU + 2 * n + 1))
            if n >= 4:
                a.wait_ge(sem["glu"], at("glu", n - 3))
            act(m.sg[:, n % 4], ps[:, bank(j), S:2 * S], ACT.Sigmoid).then_inc(sem["sg"], 1)
            j += 1
        copied = sem["copied"]
        for n in range(8):
            a.wait_ge(done, done_at(C_XBC + 2 * n + 1))
            act(m.xpad[:, 2 * n:2 * n + 2, TAPS_B - 1:], two(ps, bank(j)), ACT.Copy).then_inc(copied, 1)
            j += 1
        for n in range(4):
            a.wait_ge(done, done_at(C_Z + 2 * n + 1))
            act(m.z[:, 2 * n:2 * n + 2], two(ps, bank(j)), ACT.Silu).then_inc(copied, 1)
            j += 1
        a.wait_ge(done, done_at(C_SMALL))
        act(m.gates, two(ps, bank(j), 0, 48), ACT.Sigmoid)
        act(m.dtraw, ps[0:16, bank(j), S:2 * S], ACT.Identity, bias=par("dtb")[0:16]).then_inc(copied, 1)
        j += 1
        for n in range(4):
            a.wait_ge(done, done_at(C_Q + 2 * n + 1))
            act(m.qr[:, 2 * n:2 * n + 2], two(ps, bank(j)), ACT.Copy, scale=0.125).then_inc(copied, 1)
            j += 1
        for b, dst in enumerate((m.kc, m.vc)):
            a.wait_ge(done, done_at(C_KC + 2 * b + 1))
            for par_ in range(2):
                for nxt in range(2):
                    last = act(dst[64 * nxt:64 * nxt + 64, par_::2, 0:S - nxt],
                               two(ps[64 * par_:64 * par_ + 64], bank(j))[:, :, nxt:S], ACT.Copy)
            last.then_inc(copied, 1)
            j += 1
        for b in range(2):
            a.wait_ge(done, done_at(C_KS + 2 * b + 1))
            act(m.kraw[:, b], two(ps, bank(j)), ACT.Copy).then_inc(copied, 1)
            j += 1
        for b in range(2):
            a.wait_ge(done, done_at(C_VS + 2 * b + 1))
            act(m.vt[:, b], two(ps, bank(j)), ACT.Copy).then_inc(copied, 1)
            j += 1
        for n in range(NXB):
            a.wait_ge(sem["xconv"], at("xconv", n + 1))
            act(m.xc[:, n], m.xc[:, n], ACT.Silu).then_inc(sem["xsilu"], 1)
        j += 12
        a.wait_ge(done, done_at(C_CV + 1))
        act(m.gk, ps[:, bank(j), 0:60], ACT.Gelu_apprx_tanh)
        for r in range(4):
            last = act(m.gr[:, :, r, 0:CMP], ps[:, bank(j), 64:124].rearrange("p (g n) -> p g n", g=4),
                       ACT.Gelu_apprx_tanh)
        last.then_inc(sem["gelu"], 1)
        j += 1
        a.wait_ge(sem["kc1"], at("kc1", 1))
        act(m.kcr, ps[:, bank(j), 0:60], ACT.Copy).then_inc(sem["kcr"], 1)
        j += 3

        act(m.dtw[:, 0], m.dtraw, ACT.Abs)
        act(m.aexp[0:16], par("alog")[0:16], ACT.Exp)
        a.drain()
        act(m.dtw[:, 1], m.dtw[:, 0], ACT.Exp, scale=-1.0).then_inc(sem["dtexp"], 1)

        squares(1, m.ac, m.sq, "cent", 8, 1)
        for n in range(ND):
            a.wait_ge(sem["anrs"], at("anrs", n + 1))
            act(m.ac[:, n], m.ac[:, n], ACT.Silu, scale=par("ag", n), bias=par("abb", n)).then_inc(sem["anorm"], 1)

        def out_gates(branch, j):
            for n in range(8):
                a.wait_ge(done, done_at(C_OUT + 16 * branch + 2 * n + 1))
                k = 8 * branch + n
                if k >= 4:
                    a.wait_ge(sem["outm"], at("outm", k - 3))
                act(m.sg[:, n % 4], ps[:, bank(j), 0:S], ACT.Sigmoid).then_inc(sem["outsg"], 1)
                j += 1
            return j

        j = out_gates(0, j)

        j += 1
        a.wait_ge(sem["acs"], at("acs", 1))
        act(m.nacs, ps[:, bank(j), 0:32], ACT.Copy, scale=-1.0)
        act(m.dtw[:, 2], ps[0:16, bank(j), S:2 * S], ACT.Copy).then_inc(sem["acsc"], 1)
        j += 5
        for h in range(16):
            a.wait_ge(sem["arg"], at("arg", h + 1))
            act(m.ee[:, h % 2], m.ee[:, h % 2], ACT.Exp).then_inc(sem["ee"], 1)
        j += 20
        squares(2, m.yb, m.sq, "ysil", 0, 4)
        j = out_gates(1, j)

        for k in range(2):
            a.wait_ge(sem["cmx"], at("cmx", k + 1))
            act(m.pcmp[:, k, :, 0:CMP], m.pcmp[:, k, :, 0:CMP], ACT.Exp).then_inc(sem["cex"], 1)
        j += 4
        for k in range(2):
            a.wait_ge(sem["ct"], at("ct", k + 1))
            act(m.ptc[:, 2 * k:2 * k + 2], two(ps, bank(j)), ACT.Copy).then_inc(sem["ptc"], 1)
            j += 1

        def exps(i):
            k = (i // 2) % 2
            a.wait_ge(sem["nmx"], at("nmx", i + 1))
            if i >= 2:
                a.wait_ge(sem["tr"], at("tr", i - 1))
            for r in range(4):
                last = act(m.e[:, i % 2, r, 0:P * (k + 1)], score_view(ps, i, k)[:, r], ACT.Exp,
                           bias=m.nmx[:, i % 2, r:r + 1], accum_out=m.sums[:, i % 2, r:r + 1])
            last.then_inc(sem["ex"], 1)

        def turned(i):
            k = (i // 2) % 2
            a.wait_ge(sem["tr"], at("tr", i + 1))
            if i >= 4:
                a.wait_ge(sem["pv"], at("pv", (i - 4) // 2 + 1))
            act(m.ptt[:, i % 4, 0:k + 1].rearrange("p k r q -> p k (r q)"), ps[:, 2:3 + k, :], ACT.Copy)\
                .then_inc(sem["ptt"], 1)

        def heads_out(g):
            a.wait_ge(sem["pv"], at("pv", 2 * g + 2))
            act(m.oT[:, 2 * g:2 * g + 2], two(ps, g % 2), ACT.Copy).then_inc(sem["oc"], 1)

        exps(0)
        for i in range(16):
            if i + 1 < 16:
                exps(i + 1)
            turned(i)
            if i % 4 == 0 and i:
                heads_out(i // 4 - 1)
        heads_out(3)
        j = out_gates(2, j)

        for n in range(ND):
            a.wait_ge(done, done_at(C_WO + n))
            act(m.u[:, n], ps[:, bank(j), 0:S], ACT.Identity, scale=gate(1, n)).then_inc(sem["scaled"], 1)
            j += 1
        first_highs(C_FFN1)
        squares(3, m.h, m.u, "cent", 16, 1)
        ffn(1, C_FFN1, 6)
        squares(4, m.h, m.u, "cent", 24, 5)

    with a.Fori(0, DEPTH) as l:
        layer(l)



def add_modulation(nc, v, m, ada, g, k):
    v.wait_ge(ada.landed[k], 16 * (g + 1))
    c = m.cvec[:, k:k + 1]
    if k == 0:
        last = nc.vector.tensor_scalar(m.ada_acc, m.ada[k], c, None, ALU.mult)
    else:
        last = nc.vector.scalar_tensor_tensor(m.ada_acc, m.ada[k], c, m.ada_acc, ALU.mult, ALU.add)
    last.then_inc(ada.used, 1)
    v.drain()
    if k == ND - 1:
        v.nop().then_inc(ada.summed, 1)


def keep_columns(nc, v, m, ada, g):
    v.wait_ge(ada.columns, g + 1)
    nc.vector.tensor_copy(m.raw_moved[:], m.raw[:, 8:48])
    v.drain()
    nc.vector.tensor_copy(m.raw[:, 0:40], m.raw_moved[:])
    nc.vector.tensor_copy(m.raw[:, 40:48], m.ps[:, 7, 0:8])
    v.drain()


def vector1(nc, v, m, sem, stream, ada):
    ps, con = m.ps, m.con_of
    landed, done = stream.landed, stream.done
    tt, ts, stt = nc.vector.tensor_tensor, nc.vector.tensor_scalar, nc.vector.scalar_tensor_tensor

    def layer(l):
        at = lambda name, k: l * SIGNALS1[name] + k
        landed_at = lambda i, rounds=0: stream.landed_value(l, i, rounds)
        done_at = lambda i, rounds=0: stream.done_value(l, i, rounds)
        par = lambda name, at=0, n=1: m.par[:, PAR1[name] + at:PAR1[name] + at + n]
        c1 = lambda name, n=P, at=0: m.conb[:, CON1[name] + at:CON1[name] + at + n]
        bank = lambda j: 4 + j % 4

        def low(i, count):
            v.wait_ge(sem["hi"], at("hi", count))
            tt(low_of(m, i), chunk_of(m, i), high_of(m, i), ALU.subtract).then_inc(sem["lo"], 1)

        def scale_and_gate(i):
            ts(m.sc1[:, 8 * i:8 * i + 8], m.mod[:, (3 * i + 1) * 8:(3 * i + 2) * 8], 1.0, None, ALU.add)
            if i != 1:
                g = m.mod[:, (3 * i + 2) * 8:(3 * i + 3) * 8]
                ts(g, g, 0.5, None, ALU.mult)

        v.wait_ge(sem["par"], at("par", 16))
        tt(m.mod[:, 0:24], m.raw[:, 24:48], par("ada_b", 0, 24), ALU.add)
        v.drain()
        scale_and_gate(0)
        v.drain()

        def modulate(i):
            for n in range(ND):
                last = ts(m.u[:, n], m.h[:, n], m.sc1[:, 8 * i + n:8 * i + n + 1],
                          m.mod[:, 24 * i + n:24 * i + n + 1], ALU.mult, ALU.add)
                if i != 1:
                    last.then_inc(sem["umod"], 1)
            if i == 1:
                last.then_inc(sem["u"], 1)

        def residual(k0):
            for n in range(ND):
                v.wait_ge(sem["scaled"], at("scaled", k0 + n + 1))
                stt(m.h[:, n], m.h[:, n], ALPHA, m.u[:, n], ALU.mult, ALU.add).then_inc(sem["resid"], 1)

        def centre(k, src, bank_, k0):
            v.wait_ge(sem["mu"], at("mu", k + 1))
            for n in range(ND):
                tt(src[:, n], src[:, n], ps[:, bank_, 0:S], ALU.subtract).then_inc(sem["cent"], 1)

        def inverse_root(k):
            v.wait_ge(sem["sd"], at("sd", k + 1))
            nc.vector.reciprocal(m.rs, m.sd)
            v.drain()

        def norm(i, at, bank_):
            centre(at[0], m.h, bank_, 0)
            if i == 1:
                first_lows(1, C_FFN1)
            inverse_root(at[1])
            for n in range(ND):
                tt(m.h[:, n], m.h[:, n], m.rs, ALU.mult)
            v.drain()
            for n in range(ND):
                last = ts(m.h[:, n], m.h[:, n], par("ln_g", 8 * i + n), par("ln_b", 8 * i + n), ALU.mult, ALU.add)
            v.drain()
            return last

        def first_lows(q, cb):
            for c in range(3):
                low(cb + c, 3 * NF * q + c + 1)

        def ffn(q, cb, per):
            for n in range(ND):
                v.wait_ge(sem["uhi"], at("uhi", 8 * q + n + 1))
                tt(m.ulo[:, n], m.u[:, n], m.uhi[:, n], ALU.subtract)\
                    .then_inc(sem["ulo"], 1)

            def hidden(f, fk):
                v.wait_ge(sem["silu"], at("silu", q * NF + fk + 1))
                tt(m.hid[:, f % 3], ps[:, 4 + f % 3, S:2 * S], m.silu[:, f % 3], ALU.mult)\
                    .then_inc(sem["hid"], 1)

            def hidden_low(f, fk):
                v.wait_ge(sem["hidhi"], at("hidhi", q * NF + fk + 1))
                tt(m.hidlo[:, f % 3], m.hid[:, f % 3], m.hidhi[:, f % 3], ALU.subtract)\
                    .then_inc(sem["hidlo"], 1)

            low(cb + 3, 3 * NF * q + 4)
            hidden(0, 0)
            hidden_low(0, 0)
            low(cb + 5, 3 * NF * q + 6)
            each = 8 // (2 * per // 3)
            with v.Fori(0, 18 // per) as it:
                g = ada.group(l, q, it)
                for j in range(per):
                    i, f, fk = cb + 3 + 3 * j, 1 + j, per * it + 1 + j
                    hidden(f, fk)
                    low(i + 3, 3 * NF * q + 3 * fk + 4)
                    hidden_low(f, fk)
                    if j < 8 // each:
                        for k in range(each * j, each * j + each):
                            add_modulation(nc, v, m, ada, g, k)
                    low(i + 5, 3 * NF * q + 3 * fk + 6)
                    if j == per - 1:
                        keep_columns(nc, v, m, ada, g)
            for f in range(19, 21):
                hidden(f, f)
                low(cb + 3 * f + 3, 3 * NF * q + 3 * f + 4)
                hidden_low(f, f)
                if f == 19:
                    low(cb + 3 * f + 5, 3 * NF * q + 3 * f + 6)
            hidden(21, 21)
            hidden_low(21, 21)
            residual(16 * q)

        modulate(0)
        first_lows(0, C_FFN0)
        ffn(0, C_FFN0, 3)
        tt(m.mod[:, 24:72], m.raw[:], par("ada_b", 24, 48), ALU.add)
        v.drain()
        scale_and_gate(1)
        scale_and_gate(2)
        norm(0, (0, 0), 4)
        modulate(1)

        nc.vector.memset(m.apad[:, :, 0:TAPS_A - 1], 0.0)
        nc.vector.memset(m.xpad[:, :, 0:TAPS_B - 1], 0.0)
        j = 0
        for n in range(8):
            v.wait_ge(sem["sg"], at("sg", n + 1))
            tt(m.apad[:, n, TAPS_A - 1:], ps[:, bank(j), 0:S], m.sg[:, n % 4], ALU.mult).then_inc(sem["glu"], 1)
            j += 1
        v.drain()

        def conv(dst, src, w, b, taps, lo, hi, signal):
            for k in range(taps):
                for n in range(lo, hi):
                    if k == 0:
                        ts(dst[:, n], src[:, n, 0:S], par(w, n * taps), par(b, n), ALU.mult, ALU.add)
                    else:
                        last = stt(dst[:, n], src[:, n, k:k + S], par(w, n * taps + k), dst[:, n], ALU.mult, ALU.add)
                        if k == taps - 1:
                            last.then_inc(sem[signal], 1)
                v.drain()

        conv(m.ac, m.apad, "aw", "ab", TAPS_A, 0, ND, "aconv")
        for q in range(2):
            v.wait_ge(sem["copied"], at("copied", 4 * q + 4))
            conv(m.xc, m.xpad, "xw", "xb", TAPS_B, 8 * q, 8 * q + 8, "xconv")
        for b, (src, pe) in enumerate(((m.kc, "pek"), (m.vc, "pev"))):
            v.wait_ge(sem["copied"], at("copied", 18 + b))
            for q in range(16):
                last = ts(m.kp[b][:, q].rearrange("p (g n) -> p g n", g=4), src[:, :, 2 * q:2 * q + 225:16],
                          par(pe, q), None, ALU.add)
            last.then_inc(sem["kpe"], 1)
        j = 31

        def both(t, n=2, k=S):
            return t.rearrange("p (a t) -> p a t", a=1).to_broadcast([P, n, k])
        cos, sin = c1("cos", S), c1("sin", S)
        for n in range(4):
            v.wait_ge(sem["rotp"], at("rotp", n + 1))
            q, tmp = m.qr[:, 2 * n:2 * n + 2], m.sg[:, 2 * (n % 2):2 * (n % 2) + 2]
            tt(tmp, two(ps, bank(j)), both(sin), ALU.mult)
            tt(q, q, both(cos), ALU.mult)
            v.drain()
            tt(q, q, tmp, ALU.add).then_inc(sem["rope"], 1)
            j += 1
        for n in range(8):
            v.wait_ge(sem["rotp"], at("rotp", 5 + n))
            k, tmp = m.kr[:, n // 4, n % 4], m.sg[:, n % 4]
            tt(tmp, ps[:, bank(j), S:2 * S], sin, ALU.mult)
            tt(k, ps[:, bank(j), 0:S], cos, ALU.mult)
            v.drain()
            tt(k, k, tmp, ALU.add).then_inc(sem["rope"], 1)
            j += 1
        j += 2
        v.drain()
        v.wait_ge(sem["kc2"], at("kc2", 1))
        g4 = lambda t: t.rearrange("p (g n) -> p g n", g=4)
        ends = lambda t: both(t[:, 31:S:16], 4, CMP)
        tmp = m.sg[:, 0, 0:60]
        tt(g4(tmp), g4(ps[:, bank(j), 0:60]), ends(sin), ALU.mult)
        tt(g4(m.kcmp), g4(m.kcr), ends(cos), ALU.mult)
        v.drain()
        tt(m.kcmp, m.kcmp, tmp, ALU.add).then_inc(sem["kcmp"], 1)
        j += 1
        v.wait_ge(sem["vb"], at("vb", 1))
        for r in range(4):
            last = nc.vector.tensor_copy(m.vb[32 * r:32 * r + 32, :, r // 2, (r % 2) * 64:(r % 2) * 64 + 64],
                                         ps[32 * r:32 * r + 32, bank(j), 0:256].rearrange("p (g d) -> p g d", g=4))
        last.then_inc(sem["vbc"], 1)
        j += 1

        v.wait_ge(sem["dtexp"], at("dtexp", 1))
        log1p(nc, v, m.dtw[:, 1], m.dtw[:, 0], m.dtw[:, 2], m.dtw[:, 3], m.dtw[:, 4])
        ts(m.dtw[:, 0], m.dtraw, 0.0, None, ALU.max)
        v.drain()
        tt(m.dtw[:, 3], m.dtw[:, 3], m.dtw[:, 0], ALU.add)
        v.drain()
        ts(m.dtw[:, 4], m.dtw[:, 3], m.aexp[0:16], -1.0, ALU.mult, ALU.mult).then_inc(sem["dtv"], 1)

        centre(1, m.ac, 0, 8)
        inverse_root(1)
        for n in range(ND):
            tt(m.ac[:, n], m.ac[:, n], m.rs, ALU.mult).then_inc(sem["anrs"], 1)

        def merge(branch, j):
            for n in range(8):
                v.wait_ge(sem["outsg"], at("outsg", 8 * branch + n + 1))
                y, g = ps[:, bank(j), S:2 * S], m.sg[:, n % 4]
                if branch == 0:
                    last = tt(m.merged[:, n], y, g, ALU.mult)
                else:
                    tt(g, y, g, ALU.mult)
                    v.drain()
                    last = tt(m.merged[:, n], m.merged[:, n], g, ALU.add)
                last.then_inc(sem["outm"], 1)
                j += 1
            return j

        j = merge(0, j)

        v.wait_ge(sem["dtt"], at("dtt", 1))
        nc.vector.tensor_copy(m.dtt, ps[:, bank(j), 0:64]).then_inc(sem["dttc"], 1)
        v.drain()
        j += 2
        for h in range(4):
            v.wait_ge(sem["xt"], at("xt", h + 1))
            a, o = h // 2, h % 2
            dt = m.dtt[:, 16 * a + 8 * o:16 * a + 8 * o + 8].rearrange("p (h d) -> p h d", d=1).to_broadcast([P, 8, 64])
            tt(m.xdt[:, a, 512 * o:512 * o + 512].rearrange("p (h d) -> p h d", h=8),
               ps[:, bank(j), :].rearrange("p (h d) -> p h d", h=8), dt, ALU.mult).then_inc(sem["xdt"], 1)
            j += 1
        def exponent(h, j):
            if h % 4 == 0:
                v.wait_ge(sem["cb"], at("cb", h // 4 + 1))
                tt(m.cbm[:, (h // 4) % 2], ps[:, bank(j), 0:384], con("tri", 384), ALU.mult)\
                    .then_inc(sem["cbm"], 1)
                j += 1
            v.wait_ge(sem["bc"], at("bc", h + 1))
            ts(m.ee[:, h % 2, 0:S], ps[:, bank(j), 0:S], m.nacs[:, h:h + 1], 0.0, ALU.add, ALU.min)
            ts(m.ee[:, h % 2, S:S + P], ps[:, bank(j), P:S], m.nacs[:, 16 + h:17 + h], 0.0, ALU.add, ALU.min)\
                .then_inc(sem["arg"], 1)
            return j + 1

        j = exponent(0, j)
        for h in range(16):
            v.drain()
            v.wait_ge(sem["ee"], at("ee", h + 1))
            if h >= 2:
                v.wait_ge(sem["yh"], at("yh", h - 1))
            tt(m.mm[:, h % 2], m.ee[:, h % 2], m.cbm[:, (h // 4) % 2], ALU.mult).then_inc(sem["mm"], 1)
            if h + 1 < 16:
                j = exponent(h + 1, j)
        for n in range(ND):
            v.wait_ge(sem["yh"], at("yh", 4 * (n // 2) + 4))
            stt(m.yb[:, n], m.xc[:, n], par("dsk", n), ps[:, n // 2, (n % 2) * S:(n % 2 + 1) * S], ALU.mult, ALU.add)
        v.drain()
        for n in range(ND):
            tt(m.yb[:, n], m.yb[:, n], m.z[:, n], ALU.mult).then_inc(sem["ysil"], 1)
        inverse_root(2)
        for n in range(ND):
            stt(m.yb[:, n], m.yb[:, n], par("nw", n), m.rs, ALU.mult, ALU.mult).then_inc(sem["bnorm"], 1)
        j = merge(1, j)

        nc.vector.memset(m.pcmp, 0.0)
        v.drain()
        wide = lambda t, n, k: t.rearrange("p (h d) -> p h d", d=1).to_broadcast([P, n, k])
        for a in range(2):
            v.wait_ge(sem["cs"], at("cs", a + 1))
            p = m.pcmp[:, a, :, 0:CMP]
            for odd in range(2):
                s = ps[:, bank(j + odd), 0:128].rearrange("p (h n) -> p h n", h=8)[:, :, 0:CMP]
                tt(p[:, odd::2], s, both(c1("cmask", CMP, 16 * a), 8, CMP), ALU.add)
            v.drain()
            nc.vector.tensor_reduce(m.cst[:, 0, a], p, AX, ALU.max)
            v.drain()
            tt(p, p, wide(m.cst[:, 0, a], 16, CMP), ALU.subtract).then_inc(sem["cmx"], 1)
            j += 2
        for a in range(2):
            p, f = m.pcmp[:, a, :, 0:CMP], m.cst[:, 1, a]
            v.wait_ge(sem["cex"], at("cex", a + 1))
            nc.vector.tensor_reduce(f, p, AX, ALU.add)
            v.drain()
            nc.vector.reciprocal(f, f)
            v.drain()
            tt(f, f, m.gates[:, a, 0:48:3], ALU.mult)
            v.drain()
            if a == 0:
                ts(f, f, con("valid", 1), None, ALU.mult)
                v.drain()
            tt(p, p, wide(f, 16, CMP), ALU.mult).then_inc(sem["cp"], 1)
        j += 2

        def maxima(i):
            a = (i // 2) % 2
            v.wait_ge(sem["sc"], at("sc", i + 1))
            s = score_view(ps, i, a)
            diag = s[:, :, a * P:(a + 1) * P]
            tt(diag, diag, both(con("neg"), 4, P), ALU.add)
            v.drain()
            nc.vector.tensor_reduce(m.nmx[:, i % 2], s, AX, ALU.max, negate=True).then_inc(sem["nmx"], 1)

        def weights(i):
            g, a, b = i // 4, (i // 2) % 2, i % 2
            f = m.fac[:, i % 2]
            v.wait_ge(sem["ex"], at("ex", i + 1))
            nc.vector.reciprocal(f, m.sums[:, i % 2])
            v.drain()
            gate = m.gates[:, a, 12 * g:12 * g + 12].rearrange("p (i q c) -> p q i c", i=2, q=2)[:, :, :, 1 + b]
            ff = f.rearrange("p (q i) -> p q i", q=2)
            tt(ff, ff, gate, ALU.mult)
            v.drain()
            for r in range(4):
                p = m.e[:, i % 2, r, 0:P * (a + 1)]
                last = ts(p, p, f[:, r:r + 1], None, ALU.mult)
            last.then_inc(sem["pr"], 1)

        maxima(0)
        for i in range(16):
            if i + 1 < 16:
                maxima(i + 1)
            weights(i)
        j = merge(2, j)

        residual(8)
        norm(1, (2, 3), 0)
        modulate(2)
        ffn(1, C_FFN1, 6)
        last = norm(2, (3, 4), 4)
        v.nop().then_inc(sem["layer_done"], 1)

    for g in range(3):
        for k in range(ND):
            add_modulation(nc, v, m, ada, g, k)
        keep_columns(nc, v, m, ada, g)
    with v.Fori(0, DEPTH) as l:
        layer(l)



def gpsimd1(nc, g, m, sem, stream, ada, ada_source):
    def load(group, k):
        g.dma_start(m.ada[k], ada_source[bass.ds(group * ND + k, 1)].rearrange("a p n -> (a p) n"))\
            .then_inc(ada.landed[k], 16)

    def load_later(group, k):
        g.wait_ge(ada.used, (group - 1) * ND + k + 1)
        load(group, k)

    for k in range(ND):
        g.dma_start(m.ada[k], ada_source[k]).then_inc(ada.landed[k], 16)
    for group in range(1, 3):
        for k in range(ND):
            g.wait_ge(ada.used, (group - 1) * ND + k + 1)
            g.dma_start(m.ada[k], ada_source[group * ND + k]).then_inc(ada.landed[k], 16)

    def layer(l):
        at = lambda name, k: l * SIGNALS1[name] + k

        def low_down(i, q, fk):
            g.wait_ge(sem["hi"], at("hi", 3 * NF * q + i_of(fk)))
            nc.gpsimd.tensor_tensor(low_of(m, i), chunk_of(m, i), high_of(m, i), ALU.subtract)\
                .then_inc(sem["lo_down"], 1)
        i_of = lambda fk: 3 * fk + 5

        def ffn(q, cb, per):
            each = 8 // (2 * per // 3)
            g.wait_ge(sem["umod"], at("umod", 8 * q + 1))
            for k in range(ND):
                load_later(ada.group(l, q), k)
            low_down(cb + 4, q, 0)

            def steps(it, more):
                for j in range(per):
                    low_down(cb + 7 + 3 * j, q, per * it + 1 + j)
                    if more and j < 8 // each:
                        for k in range(each * j, each * j + each):
                            load_later(ada.group(l, q, it + 1), k)

            with g.Fori(0, 18 // per - 1) as it:
                steps(it, True)
            steps(18 // per - 1, False)
            for f in range(19, 21):
                low_down(cb + 3 * f + 4, q, f)
            g.wait_ge(sem["hi"], at("hi", 3 * NF * (q + 1)))
            nc.gpsimd.tensor_tensor(low_of(m, cb + 65), chunk_of(m, cb + 65), high_of(m, cb + 65),
                                    ALU.subtract).then_inc(sem["lo_down"], 1)

        ffn(0, C_FFN0, 3)
        ffn(1, C_FFN1, 6)

    with g.Fori(0, DEPTH) as l:
        layer(l)


def log1p(nc, v, y, z, z2, out, p):
    tt, ts, stt = nc.vector.tensor_tensor, nc.vector.tensor_scalar, nc.vector.scalar_tensor_tensor
    ts(z, y, 2.0, None, ALU.add)
    v.drain()
    nc.vector.reciprocal(z, z)
    v.drain()
    tt(z, z, y, ALU.mult)
    v.drain()
    tt(z2, z, z, ALU.mult)
    v.drain()
    ts(p, z2, 1.0 / 15, None, ALU.mult)
    v.drain()
    for c in (13, 11, 9, 7, 5, 3):
        stt(p, p, 1.0 / c, z2, ALU.add, ALU.mult)
        v.drain()
    stt(out, p, 1.0, z, ALU.add, ALU.mult)
    v.drain()
    ts(out, out, 2.0, None, ALU.mult)
    v.drain()



def tensor2(nc, t, m, sem, stream):
    ps, con = m.ps, m.con_of
    landed, done = stream.landed, stream.done
    mm = nc.tensor.matmul

    def layer(l):
        at = lambda name, k: l * SIGNALS2[name] + k
        landed_at = lambda i, rounds=0: stream.landed_value(l, i, rounds)
        done_at = lambda i, rounds=0: stream.done_value(l, i, rounds)
        c2 = lambda name, n=P, at=0: m.conb[:, CON2[name] + at:CON2[name] + at + n]
        unit = lambda j: 4 + j % 4

        def project(i, out, rounds=0, cols=(0, P)):
            t.wait_ge(landed[i % RING], landed_at(i, rounds))
            for k in range(ND):
                last = mm(out, chunk_tile(m, i, k, *cols), m.u[:, k], start=k == 0, stop=k == ND - 1)
            return last

        def token_major(i, bank, width, at):
            t.wait_ge(landed[i % RING], landed_at(i))
            for a in range(2):
                for k in range(ND):
                    last = mm(ps[:, bank, a * width + at:a * width + at + P], m.u[:, k, a * P:(a + 1) * P],
                              chunk_tile(m, i, k), start=k == 0, stop=k == ND - 1)
            return last

        def rms(k):
            for n in range(ND):
                t.wait_ge(sem["usq"], at("usq", 8 * k + n + 1))
                last = mm(ps[:, 0, 0:S], con("mean"), m.sq[:, n], start=n == 0, stop=n == ND - 1)
            last.then_inc(sem["uvar"], 1)

        rms(0)
        t.wait_ge(sem["u"], at("u", 1))
        j = 0
        def pair(i, j):
            project(i, ps[:, unit(j), 0:S]).then_inc(done, 1)
            project(i + 1, ps[:, unit(j), S:2 * S]).then_inc(done, 1)
            return j + 1
        j = pair(E_Q, j)
        j = pair(E_Q + 2, j)
        project(E_K, ps[:, unit(j), 0:S]).then_inc(done, 1)
        j += 1
        token_major(E_V, unit(j), P, 0).then_inc(done, 1)
        j += 1
        t.wait_ge(sem["copied"], at("copied", 1))
        project(E_IF, ps[0:4, unit(j), 0:S], cols=(0, 4))
        project(E_IF, ps[0:4, unit(j), S:2 * S], cols=(4, 8)).then_inc(done, 1)
        j += 1
        t.wait_ge(sem["copied"], at("copied", 2))
        j = pair(E_QM, j)
        t.wait_ge(sem["copied"], at("copied", 3))
        j = pair(E_KM, j)
        for q in range(2):
            t.wait_ge(sem["copied"], at("copied", 4 + q))
            for c in range(2):
                token_major(E_VM + 2 * q + c, unit(j), S, c * P).then_inc(done, 1)
            j += 1
        t.wait_ge(sem["copied"], at("copied", 6))
        j = pair(E_OM, j)
        t.wait_ge(sem["copied"], at("copied", 7))
        j = pair(E_OM + 2, j)
        for n in range(5):
            if n < 4:
                t.wait_ge(sem["copied"], at("copied", 8 + n))
            else:
                t.wait_ge(sem["hsd"], at("hsd", 1))
            mm(ps[:, unit(j), 0:S], c2("blk"), m.hsq[n], start=True, stop=True).then_inc(sem["hvar"], 1)
            j += 1
        for n in range(5):
            if n < 4:
                t.wait_ge(sem["hsd"], at("hsd", 2 + n))
            else:
                t.wait_ge(sem["rope"], at("rope", 1))
            t.wait_ge(sem["qn"], at("qn", n + 1))
            mm(ps[:, unit(j), 0:S], c2("rot"), m.qk_raw[n], start=True, stop=True).then_inc(sem["rotp"], 1)
            j += 1
        t.wait_ge(sem["rope"], at("rope", 5))
        mm(ps[:, unit(j), 0:S], c2("dup"), m.kda, start=True, stop=True)
        mm(ps[:, unit(j), S:2 * S], c2("dup", P, P), m.kda, start=True, stop=True).then_inc(sem["dup"], 1)
        j += 1
        t.wait_ge(sem["mt"], at("mt", 1))
        for a in range(2):
            last = mm(ps[:, unit(j), 4 * a:4 * a + 4], m.ow[:, 3, a * P:(a + 1) * P],
                      m.con[0:4, CON["ident"]:CON["ident"] + 4], start=True, stop=True)
        last.then_inc(sem["rt"], 1)

        def scores(i):
            g, a = i // 2, i % 2
            if i >= 2:
                t.wait_ge(sem["ex"], at("ex", i - 1))
            for r in range(4):
                lo = 64 * (r % 2)
                last = mm(score_view(ps, i, a)[:, place_of(r)], m.qa[lo:lo + 64, 2 * g + r // 2, a * P:(a + 1) * P],
                          m.ka[lo:lo + 64, g, 0:P * (a + 1)], start=True, stop=True)
            last.then_inc(sem["sc"], 1)

        def turn(i):
            t.wait_ge(sem["pr"], at("pr", i + 1))
            if i >= 1:
                t.wait_ge(sem["ptt"], at("ptt", i))
            for k in range(i % 2 + 1):
                for r in range(4):
                    last = nc.tensor.transpose(ps[:, 2 + k, r * P:(r + 1) * P], m.e[:, i % 2, r, k * P:(k + 1) * P],
                                               con("ident"))
            last.then_inc(sem["tr"], 1)

        def values(i):
            g, a = i // 2, i % 2
            o = ps[:, g, :].rearrange("p (i t) -> p i t", i=2)
            t.wait_ge(sem["ptt"], at("ptt", i + 1))
            for k in range(a + 1):
                for q in range(2):
                    last = mm(o[64 * q:64 * q + 64, :, a * P:(a + 1) * P], m.va[:, k, g * 64:(g + 1) * 64],
                              m.ptt[:, i, k, 2 * q:2 * q + 2], start=a == 0, stop=a == 1 and k == 1,
                              skip_group_check=True)
            last.then_inc(sem["pv"], 1)

        t.wait_ge(sem["dupc"], at("dupc", 1))
        t.wait_ge(sem["mtc"], at("mtc", 1))
        scores(0)
        for i in range(4):
            if i + 1 < 4:
                scores(i + 1)
            turn(i)
            if i >= 1:
                values(i - 1)
        values(3)

        t.wait_ge(sem["oc"], at("oc", 2))
        j = 0

        def head_out(h):
            t.wait_ge(sem["mm"], at("mm", h + 1))
            for a, lhs in enumerate((m.vm, None)):
                o = ps[:, h, a * S:(a + 1) * S]
                left = lambda s: con("ones") if lhs is None else m.vm[:, s, h * P:(h + 1) * P]
                mm(o, left(0), m.mm[:, h % 2, 0:S], start=True, stop=False)
                last = mm(o[:, P:S], left(1), m.mm[:, h % 2, S:S + P], start=False, stop=True)
            last.then_inc(sem["num"], 1)

        for h in range(4):
            lo = 64 * (h % 2)
            if h >= 2:
                t.wait_ge(sem["qkm"], at("qkm", h - 1))
            q, k = m.qm[lo:lo + 64, h // 2], m.km[lo:lo + 64, h // 2]
            mm(ps[:, unit(j), 0:S], k[:, 0:P], q, start=True, stop=True)
            mm(ps[:, unit(j), S:S + P], k[:, P:S], q[:, P:S], start=True, stop=True).then_inc(sem["qk"], 1)
            j += 1
            if h >= 2:
                t.wait_ge(sem["arg"], at("arg", h - 1))
            mm(ps[:, unit(j), :], m.con[0:4, CON["ident"] + h:CON["ident"] + h + 1].to_broadcast([4, P]),
               m.ow[:, 5:7].rearrange("p k t -> p (k t)"), start=True, stop=True).then_inc(sem["bc"], 1)
            j += 1
            if h >= 1:
                head_out(h - 1)
        head_out(3)
        for h in range(4):
            if h % 2 == 0:
                t.wait_ge(sem["qkm"], at("qkm", 3 + h // 2))
            else:
                t.wait_ge(sem["arg"], at("arg", 3 + h // 2))
            t.wait_ge(sem["hsq"], at("hsq", h + 1))
            mm(ps[:, unit(j), 0:S], c2("mean128"), m.sq[:, h], start=True, stop=True).then_inc(sem["hvar"], 1)
            j += 1

        for b, src in enumerate((m.att, m.hm)):
            for q in range(4):
                i = E_BR + 12 * b + 3 * q
                k4 = 4 * b + q
                if k4 < 2:
                    t.wait_ge(sem["hsd"], at("hsd", 7 + 2 * k4))
                else:
                    t.wait_ge(sem["outsg"], at("outsg", k4 - 1))
                j = pair(i, j)
                if k4 >= 2:
                    t.wait_ge(sem["outm"], at("outm", k4 - 1))
                if b == 1 and q == 0:
                    t.wait_ge(sem["hm"], at("hm", 4))
                t.wait_ge(landed[(i + 2) % RING], landed_at(i + 2))
                for c in range(2):
                    for k in range(4):
                        last = mm(ps[:, unit(j), c * S:(c + 1) * S], chunk_tile(m, i + 2, 4 * c + k), src[:, k],
                                  start=k == 0, stop=k == 3)
                last.then_inc(done, 1)
                j += 1
        t.wait_ge(sem["outm"], at("outm", 8))
        for q in range(4):
            for c in range(2):
                i = E_OUT + 2 * q + c
                t.wait_ge(landed[i % RING], landed_at(i))
                for k in range(ND):
                    last = mm(ps[:, unit(j), c * S:(c + 1) * S], chunk_tile(m, i, k), m.merged[:, k],
                              start=k == 0, stop=k == ND - 1)
                last.then_inc(done, 1)
            j += 1

        rms(1)
        t.wait_ge(sem["usd"], at("usd", 2))
        for b in range(4):
            mm(ps[:, b, :], m.zero[:, 0:P], m.zero[:], start=True, stop=False, skip_group_check=True)

        def up(i, f, fk):
            t.wait_ge(sem["lo"], at("lo", fk + 1))
            for k in range(ND):
                if f == 0:
                    t.wait_ge(sem["ulo"], at("ulo", k + 1))
                last = product3(mm, ps[:, 4 + f % 3, 0:S], m, i, k, m.uhi[:, k], m.ulo[:, k],
                                start=k == 0, stop=k == ND - 1)
            last.then_inc(done, 1)

        def down(i, f, fk, last=False):
            t.wait_ge(sem["lo_down"], at("lo_down", fk + 1))
            t.wait_ge(sem["hidlo"], at("hidlo", fk + 1))
            for n in range(ND):
                x = product3(mm, ps[:, n // 2, (n % 2) * S:(n % 2 + 1) * S], m, i, n, m.hidhi[:, f % 3],
                             m.hidlo[:, f % 3], start=False, stop=last, skip_group_check=True)
            x.then_inc(done, 1)

        up(E_FFN, 0, 0)
        with t.Fori(0, 3) as it:
            for q in range(9):
                up(E_FFN + 1 + 2 * q, 1 + q, 9 * it + 1 + q)
                down(E_FFN + 2 + 2 * q, q, 9 * it + q)
        for f in range(28, NF2):
            up(E_FFN + 2 * f - 1, f, f)
            down(E_FFN + 2 * f, f - 1, f - 1)
        down(E_FFN + 63, 31, 31, last=True)

    with t.Fori(0, DEPTH) as l:
        layer(l)


def scalar2(nc, a, m, sem, stream, par_source):
    ps, con = m.ps, m.con_of
    landed, done = stream.landed, stream.done
    act = nc.scalar.activation

    def layer(l):
        at = lambda name, k: l * SIGNALS2[name] + k
        landed_at = lambda i, rounds=0: stream.landed_value(l, i, rounds)
        done_at = lambda i, rounds=0: stream.done_value(l, i, rounds)
        par = lambda name, at=0, n=1: m.par[:, PAR2[name] + at:PAR2[name] + at + n]
        bank = lambda j: 4 + j % 4
        a.wait_ge(sem["layer_done"], at("layer_done", 1))
        a.dma_start(m.par[:, 0:PAR2["all"]], par_source[bass.ds(l, 1)].rearrange("a p n -> (a p) n"))\
            .then_inc(sem["par"], 16)

        def rms(k):
            for n in range(ND):
                if k == 1 and n % 2 == 0:
                    a.wait_ge(sem["xres"], at("xres", n // 2 + 1))
                act(m.sq[:, n], m.h[:, n], ACT.Square).then_inc(sem["usq"], 1)
            a.wait_ge(sem["uvar"], at("uvar", k + 1))
            act(m.sd, ps[:, 0, 0:S], ACT.Sqrt, bias=con("eps2", 1)).then_inc(sem["usd"], 1)

        rms(0)
        copied = sem["copied"]
        a.wait_ge(sem["par"], at("par", 16))
        j = 0
        for n in range(3):
            a.wait_ge(done, done_at(E_Q + 2 * n + 1 if n < 2 else E_K))
            for c in range(2 if n < 2 else 1):
                act(m.qk_raw[2 * n + c], ps[:, bank(j), c * S:(c + 1) * S], ACT.Copy)
                last = act(m.hsq[2 * n + c], ps[:, bank(j), c * S:(c + 1) * S], ACT.Square)
            last.then_inc(copied, 1)
            j += 1
        a.wait_ge(done, done_at(E_V))
        act(m.va, two(ps, bank(j), 0, P), ACT.Copy).then_inc(copied, 1)
        j += 1
        a.wait_ge(done, done_at(E_IF))
        act(m.ow[:, 0], ps[0:4, bank(j), 0:S], ACT.Identity, bias=par("ib")[0:4])
        act(m.ow[:, 1], ps[0:4, bank(j), S:2 * S], ACT.Identity, bias=par("fb")[0:4]).then_inc(copied, 1)
        j += 1
        for i, dst in ((E_QM, m.qm), (E_KM, m.km)):
            a.wait_ge(done, done_at(i + 1))
            act(dst, two(ps, bank(j)), ACT.Copy).then_inc(copied, 1)
            j += 1
        for q in range(2):
            a.wait_ge(done, done_at(E_VM + 2 * q + 1))
            act(m.vm[:, :, q * S:(q + 1) * S], two(ps, bank(j)), ACT.Copy).then_inc(copied, 1)
            j += 1
        for q in range(2):
            a.wait_ge(done, done_at(E_OM + 2 * q + 1))
            act(m.om[:, 2 * q:2 * q + 2], two(ps, bank(j)), ACT.Sigmoid).then_inc(copied, 1)
            j += 1
        act(m.ow[:, 2], m.ow[:, 1], ACT.Abs)
        a.drain()
        act(m.ow[:, 3], m.ow[:, 2], ACT.Exp, scale=-1.0).then_inc(sem["fexp"], 1)
        for n in range(5):
            a.wait_ge(sem["hvar"], at("hvar", n + 1))
            act(m.hsq[n], ps[:, bank(j), 0:S], ACT.Sqrt, bias=con("eps2", 1)).then_inc(sem["hsd"], 1)
            j += 1
        j += 5
        a.wait_ge(sem["dup"], at("dup", 1))
        act(m.ka, two(ps, bank(j)), ACT.Copy).then_inc(sem["dupc"], 1)

        def exps(i):
            a.wait_ge(sem["nmx"], at("nmx", i + 1))
            if i >= 2:
                a.wait_ge(sem["tr"], at("tr", i - 1))
            for r in range(4):
                act(m.e[:, i % 2, r, 0:P * (i % 2 + 1)], score_view(ps, i, i % 2)[:, r], ACT.Exp,
                    bias=m.nmx[:, i % 2, r:r + 1], accum_out=m.sums[:, i % 2, r:r + 1])
            act(m.esink[:, i % 2], m.esink[:, i % 2], ACT.Exp).then_inc(sem["ex"], 1)

        def turned(i):
            a.wait_ge(sem["tr"], at("tr", i + 1))
            k = i % 2
            act(m.ptt[:, i, 0:k + 1].rearrange("p k r q -> p k (r q)"), ps[:, 2:3 + k, :], ACT.Copy)\
                .then_inc(sem["ptt"], 1)

        def heads_out(g):
            a.wait_ge(sem["pv"], at("pv", 2 * g + 2))
            act(m.att[:, 2 * g:2 * g + 2], two(ps, g), ACT.Copy).then_inc(sem["oc"], 1)

        exps(0)
        for i in range(4):
            if i + 1 < 4:
                exps(i + 1)
            turned(i)
        heads_out(0)
        heads_out(1)

        def numerator_side(h):
            a.wait_ge(sem["num"], at("num", h + 1))
            act(m.den[:, h % 2], ps[:, h, S:2 * S], ACT.Abs).then_inc(sem["absd"], 1)
            a.wait_ge(sem["hh"], at("hh", h + 1))
            act(m.sq[:, h], m.hm[:, h], ACT.Square).then_inc(sem["hsq"], 1)

        j = 0
        for h in range(4):
            a.wait_ge(sem["bc"], at("bc", h + 1))
            act(m.em[:, h % 2], ps[:, bank(2 * h + 1), S:2 * S], ACT.Exp).then_inc(sem["me"], 1)
            a.wait_ge(sem["arg"], at("arg", h + 1))
            act(m.ee[:, h % 2], m.ee[:, h % 2], ACT.Exp).then_inc(sem["ee"], 1)
            if h >= 1:
                numerator_side(h - 1)
        numerator_side(3)
        j = 8
        for h in range(4):
            a.wait_ge(sem["hvar"], at("hvar", 5 + h + 1))
            if h >= 2:
                a.wait_ge(sem["hm"], at("hm", h - 1))
            act((m.sd, m.hsq[4])[h % 2], ps[:, bank(j), 0:S], ACT.Sqrt, bias=con("eps2", 1))\
                .then_inc(sem["hsd"], 1)
            j += 1

        for b in range(2):
            for q in range(4):
                k = 4 * b + q
                a.wait_ge(done, done_at(E_BR + 12 * b + 3 * q + 1))
                if k >= 2:
                    a.wait_ge(sem["outm"], at("outm", k - 1))
                act(m.sg[:, 2 * (q % 2):2 * (q % 2) + 2], two(ps, bank(j)), ACT.Sigmoid)\
                    .then_inc(sem["outsg"], 1)
                j += 2

        def high(i):
            act(high_of(m, i), chunk_of(m, i), ACT.Copy).then_inc(sem["hi"], 1)

        def later_high(i, rounds=0):
            a.wait_ge(landed[i % RING], landed_at(i, rounds))
            a.wait_ge(done, done_at(i - HIGH, rounds))
            high(i)

        for i in range(E_FFN, E_FFN + HIGH):
            a.wait_ge(landed[i % RING], landed_at(i))
            high(i)
        rms(1)
        for n in range(ND):
            a.wait_ge(sem["umod"], at("umod", n + 1))
            act(m.uhi[:, n], m.u[:, n], ACT.Copy).then_inc(sem["uhi"], 1)

        def relu(i, f, rounds=0):
            a.wait_ge(done, done_at(i, rounds))
            act(m.silu[:, f % 3], ps[:, 4 + f % 3, 0:S], ACT.Relu).then_inc(sem["relu"], 1)

        def hidden_high(f, fk):
            a.wait_ge(sem["hid"], at("hid", fk + 1))
            act(m.hidhi[:, f % 3], m.hid[:, f % 3], ACT.Copy).then_inc(sem["hidhi"], 1)

        def step(i, f, fk, rounds=0):
            relu(i, f, rounds)
            later_high(i + 3, rounds)
            hidden_high(f, fk)
            later_high(i + 4, rounds)

        relu(E_FFN, 0)
        later_high(E_FFN + 3)
        hidden_high(0, 0)
        with a.Fori(0, 3) as it:
            for q in range(9):
                step(E_FFN + 1 + 2 * q, 1 + q, 9 * it + 1 + q, 2 * it)
        for f in range(28, 31):
            step(E_FFN + 2 * f - 1, f, f)
        relu(E_FFN + 61, 31)
        hidden_high(31, 31)

    with a.Fori(0, DEPTH) as l:
        layer(l)


def vector2(nc, v, m, sem, stream):
    ps, con = m.ps, m.con_of
    landed, done = stream.landed, stream.done
    tt, ts, stt = nc.vector.tensor_tensor, nc.vector.tensor_scalar, nc.vector.scalar_tensor_tensor

    def layer(l):
        at = lambda name, k: l * SIGNALS2[name] + k
        landed_at = lambda i, rounds=0: stream.landed_value(l, i, rounds)
        done_at = lambda i, rounds=0: stream.done_value(l, i, rounds)
        par = lambda name, at=0, n=1: m.par[:, PAR2[name] + at:PAR2[name] + at + n]
        c2 = lambda name, n=P, at=0: m.conb[:, CON2[name] + at:CON2[name] + at + n]
        bank = lambda j: 4 + j % 4

        def rms(k, gain):
            v.wait_ge(sem["par"], at("par", 16))
            v.wait_ge(sem["usd"], at("usd", k + 1))
            nc.vector.reciprocal(m.rs, m.sd)
            v.drain()
            for n in range(ND):
                last = stt(m.u[:, n], m.h[:, n], par(gain, n), m.rs, ALU.mult, ALU.mult)
                if k == 1:
                    last.then_inc(sem["umod"], 1)
            if k == 0:
                last.then_inc(sem["u"], 1)

        rms(0, "nmix")
        for n in range(5):
            v.wait_ge(sem["hsd"], at("hsd", n + 1))
            nc.vector.reciprocal(m.hsq[n], m.hsq[n])
            v.drain()
            stt(m.qk_raw[n], m.qk_raw[n], par("qn" if n < 4 else "kn"), m.hsq[n], ALU.mult, ALU.mult)\
                .then_inc(sem["qn"], 1)
        v.drain()
        for n in range(5):
            b = bank(16 + n)
            dst = m.qa[:, n] if n < 4 else m.kda
            v.wait_ge(sem["rotp"], at("rotp", n + 1))
            tt(m.tmp[n % 2], ps[:, b, 0:S], c2("sinq" if n < 4 else "sink", S), ALU.mult)
            tt(dst, m.qk_raw[n], c2("cosq" if n < 4 else "cosk", S), ALU.mult)
            v.drain()
            tt(dst, dst, m.tmp[n % 2], ALU.add).then_inc(sem["rope"], 1)

        w = lambda k: m.ow[:, k]
        v.wait_ge(sem["fexp"], at("fexp", 1))
        log1p(nc, v, w(3), w(2), w(4), w(5), w(6))
        ts(w(1), w(1), 0.0, None, ALU.min)
        v.drain()
        tt(w(1), w(1), w(5), ALU.subtract)
        v.drain()
        nc.vector.tensor_tensor_scan(w(2), w(7), w(1), 0.0, ALU.mult, ALU.add)
        v.drain()
        tt(w(3), w(0), w(2), ALU.subtract)
        v.drain()
        nc.vector.tensor_tensor_scan(w(4), w(3), w(3), 0.0, ALU.max, ALU.max)
        v.drain()
        ts(w(5), w(4), -1.0, None, ALU.mult)
        v.drain()
        tt(w(6), w(5), w(2), ALU.subtract).then_inc(sem["mt"], 1)
        v.wait_ge(sem["rt"], at("rt", 1))
        nc.vector.tensor_copy(m.rt, ps[:, bank(22), 0:8].rearrange("p (a h) -> p a h", a=2))\
            .then_inc(sem["mtc"], 1)

        def maxima(i):
            g, a = i // 2, i % 2
            mx, sink = m.mx[:, i % 2], par("sink", 4 * g, 4)
            v.wait_ge(sem["sc"], at("sc", i + 1))
            s = score_view(ps, i, a)
            mask = lambda t: t.rearrange("p (a t) -> p a t", a=1).to_broadcast([P, 4, P])
            tt(s[:, :, a * P:(a + 1) * P], s[:, :, a * P:(a + 1) * P], mask(con("neg")), ALU.add)
            if a == 1:
                tt(s[:, :, 0:P], s[:, :, 0:P], mask(c2("band")), ALU.add)
            v.drain()
            nc.vector.tensor_reduce(mx, s, AX, ALU.max)
            v.drain()
            tt(mx, mx, sink, ALU.max)
            v.drain()
            ts(m.nmx[:, i % 2], mx, -1.0, None, ALU.mult)
            tt(m.esink[:, i % 2], sink, mx, ALU.subtract)
            v.drain()
            v.nop().then_inc(sem["nmx"], 1)

        def weights(i):
            f = m.fac[:, i % 2]
            v.wait_ge(sem["ex"], at("ex", i + 1))
            tt(f, m.sums[:, i % 2], m.esink[:, i % 2], ALU.add)
            v.drain()
            nc.vector.reciprocal(f, f)
            v.drain()
            for r in range(4):
                p = m.e[:, i % 2, r, 0:P * (i % 2 + 1)]
                last = ts(p, p, f[:, r:r + 1], None, ALU.mult)
            last.then_inc(sem["pr"], 1)

        maxima(0)
        for i in range(4):
            if i + 1 < 4:
                maxima(i + 1)
            weights(i)

        def quotient(h):
            d = m.den[:, h % 2]
            v.wait_ge(sem["absd"], at("absd", h + 1))
            tt(d, d, m.em[:, h % 2], ALU.max)
            v.drain()
            nc.vector.reciprocal(d, d)
            v.drain()
            tt(m.hm[:, h], ps[:, h, 0:S], d, ALU.mult).then_inc(sem["hh"], 1)

        for h in range(4):
            b = bank(2 * h + 1)
            v.wait_ge(sem["qk"], at("qk", h + 1))
            tt(m.qkm[:, h % 2], ps[:, bank(2 * h), 0:384], c2("tri8", 384), ALU.mult).then_inc(sem["qkm"], 1)
            v.wait_ge(sem["me"], at("me", h + 1))
            ts(m.ee[:, h % 2, 0:S], ps[:, b, 0:S], m.rt[:, 0, h:h + 1], 0.0, ALU.add, ALU.min)
            ts(m.ee[:, h % 2, S:S + P], ps[:, b, P:S], m.rt[:, 1, h:h + 1], 0.0, ALU.add, ALU.min)\
                .then_inc(sem["arg"], 1)
            v.drain()
            if h >= 2:
                v.wait_ge(sem["num"], at("num", h - 1))
            v.wait_ge(sem["ee"], at("ee", h + 1))
            tt(m.mm[:, h % 2], m.ee[:, h % 2], m.qkm[:, h % 2], ALU.mult).then_inc(sem["mm"], 1)
            if h >= 1:
                quotient(h - 1)
        quotient(3)
        for h in range(4):
            v.wait_ge(sem["hsd"], at("hsd", 5 + h + 1))
            d = (m.sd, m.hsq[4])[h % 2]
            nc.vector.reciprocal(m.rs, d)
            v.drain()
            stt(m.hm[:, h], m.hm[:, h], par("hn", h), m.rs, ALU.mult, ALU.mult)
            v.drain()
            tt(m.hm[:, h], m.hm[:, h], m.om[:, h], ALU.mult).then_inc(sem["hm"], 1)

        j = 12
        for b in range(2):
            for q in range(4):
                v.wait_ge(sem["outsg"], at("outsg", 4 * b + q + 1))
                v.wait_ge(done, done_at(E_BR + 12 * b + 3 * q + 2))
                y, g, out = two(ps, bank(j + 1)), m.sg[:, 2 * (q % 2):2 * (q % 2) + 2], m.merged[:, 2 * q:2 * q + 2]
                if b == 0:
                    last = tt(out, y, g, ALU.mult)
                else:
                    tt(g, y, g, ALU.mult)
                    v.drain()
                    last = tt(out, out, g, ALU.add)
                last.then_inc(sem["outm"], 1)
                j += 2
        for q in range(4):
            v.wait_ge(done, done_at(E_OUT + 2 * q + 1))
            tt(m.h[:, 2 * q:2 * q + 2], two(ps, bank(j)), m.h[:, 2 * q:2 * q + 2], ALU.add)\
                .then_inc(sem["xres"], 1)
            j += 1
        v.drain()
        def low(i, count):
            v.wait_ge(sem["hi"], at("hi", count))
            tt(low_of(m, i), chunk_of(m, i), high_of(m, i), ALU.subtract).then_inc(sem["lo"], 1)

        low(E_FFN, 1)
        low(E_FFN + 1, 2)
        rms(1, "nffn")
        for n in range(ND):
            v.wait_ge(sem["uhi"], at("uhi", n + 1))
            tt(m.ulo[:, n], m.u[:, n], m.uhi[:, n], ALU.subtract).then_inc(sem["ulo"], 1)

        def hidden(f, fk):
            v.wait_ge(sem["relu"], at("relu", fk + 1))
            tt(m.hid[:, f % 3], m.silu[:, f % 3], m.silu[:, f % 3], ALU.mult).then_inc(sem["hid"], 1)

        def hidden_low(f, fk):
            v.wait_ge(sem["hidhi"], at("hidhi", fk + 1))
            tt(m.hidlo[:, f % 3], m.hid[:, f % 3], m.hidhi[:, f % 3], ALU.subtract)\
                .then_inc(sem["hidlo"], 1)

        def step(f, fk):
            hidden(f, fk)
            hidden_low(f, fk)
            if not isinstance(fk, int) or fk < 30:
                low(E_FFN + 2 * f + 3, 2 * fk + 4)

        step(0, 0)
        with v.Fori(0, 3) as it:
            for q in range(9):
                step(1 + q, 9 * it + 1 + q)
        for f in range(28, NF2):
            step(f, f)
        v.wait_ge(done, done_at(E_FFN + 63))
        for q in range(4):
            tt(m.h[:, 2 * q:2 * q + 2], two(ps, q), m.h[:, 2 * q:2 * q + 2], ALU.add).then_inc(sem["xres"], 1)
        v.drain()
        v.nop().then_inc(sem["layer_done"], 1)

    with v.Fori(0, DEPTH) as l:
        layer(l)


def gpsimd2(nc, g, m, sem):
    def layer(l):
        at = lambda name, k: l * SIGNALS2[name] + k

        def low_down(i, count):
            g.wait_ge(sem["hi"], at("hi", count))
            nc.gpsimd.tensor_tensor(low_of(m, i), chunk_of(m, i), high_of(m, i), ALU.subtract)\
                .then_inc(sem["lo_down"], 1)

        low_down(E_FFN + 2, 3)
        with g.Fori(0, 3) as it:
            for q in range(9):
                low_down(E_FFN + 4 + 2 * q, 2 * (9 * it + 1 + q) + 3)
        for f in range(28, 31):
            low_down(E_FFN + 2 * f + 2, 2 * f + 3)
        low_down(E_FFN + 63, 64)

    with g.Fori(0, DEPTH) as l:
        layer(l)


def build(nc, x, c, con, con1, con2, stream1, ada_w, stream2, par1, par2, out):
    with ExitStack() as ctx:
        m = memory(nc, ctx)
        sem = lambda name: ctx.enter_context(nc.semaphore(name))
        sem1 = {name: sem("a_" + name) for name in SIGNALS1}
        first = Stream(N1, [sem(f"landed{s}") for s in range(RING)], sem("done"))
        sem2 = {name: sem("b_" + name) for name in SIGNALS2}
        second = Stream(N2, first.landed, first.done, first)
        ada = Modulation(sem)
        inputs, ready, silu_c, stored, con_b = sem("inputs"), sem("ready"), sem("silu_c"), sem("stored"), sem("con_b")
        block = ctx.enter_context(nc.Block())

        @block.sync
        def _(sp):
            sp.dma_start(m.cvec[:, 8:16], c).then_inc(inputs, 16)
            sp.dma_start(m.h, x).then_inc(inputs, 16)
            sp.dma_start(m.con[:], con).then_inc(inputs, 16)
            sp.dma_start(m.conb[:, 0:CON1["all"]], con1).then_inc(inputs, 16)
            stream_weights(sp, m, stream1, first)
            stream_weights(sp, m, stream2, second)
            sp.wait_ge(sem2["layer_done"], 1 + DEPTH)
            sp.dma_start(out, m.h).then_inc(stored, 16)
            sp.wait_ge(stored, 16)

        @block.tensor
        def _(t):
            t.wait_ge(inputs, 64)
            t.wait_ge(ready, 2)
            t.nop().then_inc(first.done, RING)
            tensor1(nc, t, m, sem1, first, ada)
            t.wait_ge(con_b, 16)
            tensor2(nc, t, m, sem2, second)

        @block.scalar
        def _(a):
            a.wait_ge(inputs, 64)
            nc.scalar.activation(m.cvec[:, 0:8], m.cvec[:, 8:16], ACT.Silu).then_inc(silu_c, 1)
            scalar1(nc, a, m, sem1, first, par1)
            a.wait_ge(sem1["layer_done"], 1 + DEPTH)
            a.dma_start(m.conb[:, 0:CON2["all"]], con2).then_inc(con_b, 16)
            a.wait_ge(con_b, 16)
            scalar2(nc, a, m, sem2, second, par2)

        @block.vector
        def _(v):
            nc.vector.memset(m.zero[:], 0.0)
            nc.vector.memset(m.gr, 0.0)
            nc.vector.memset(m.raw[:], 0.0)
            nc.vector.memset(m.vb, 0.0).then_inc(ready, 2)
            v.wait_ge(inputs, 64)
            v.wait_ge(silu_c, 1)
            v.nop().then_inc(sem1["layer_done"], 1)
            vector1(nc, v, m, sem1, first, ada)
            v.wait_ge(con_b, 16)
            nc.vector.memset(m.ow[:, 7], 1.0)
            v.drain()
            v.nop().then_inc(sem2["layer_done"], 1)
            vector2(nc, v, m, sem2, second)

        @block.gpsimd
        def _(g):
            gpsimd1(nc, g, m, sem1, first, ada, ada_w)
            gpsimd2(nc, g, m, sem2)



def by_column_tile(w):
    k, n = w.shape
    return w.reshape(k // P, P, n // P, P).transpose(2, 1, 0, 3).reshape(n // P, P, k)


def by_row_tile(w):
    return w.reshape(-1, P, 1024)


def columns(v):
    return v.reshape(-1, P).T


def interleave(a, b):
    return np.stack([a, b], 1).reshape(-1, *a.shape[1:])


def ffn_chunks(gate, up, down):
    gu, d = interleave(by_column_tile(gate), by_column_tile(up)), by_row_tile(down)
    parts = [gu[0:2]]
    for f in range(1, NF):
        parts += [gu[2 * f:2 * f + 2], d[f - 1:f]]
    return parts + [d[NF - 1:]]


def pack1(i):
    streams, pars = [], []
    for l in range(DEPTH):
        parts = ffn_chunks(i["ffn_w_gate"][l, 0], i["ffn_w_up"][l, 0], i["ffn_w_down"][l, 0])
        w = i["w_in"][l]
        cut = lambda a, n: by_column_tile(w[:, a:a + n])
        parts += [interleave(cut(0, 1024), cut(1024, 1024)), cut(3072, 2048), cut(2048, 1024)]
        small = np.zeros((D, P), np.float32)
        small[:, 0:48] = w[:, 7696:7744]
        small[:, 64:80] = w[:, 5120:5136]
        parts += [by_column_tile(small), cut(5136, 1024), cut(6160, 256), cut(6416, 256), cut(6672, 256),
                  cut(7184, 256), cut(6928, 256), cut(7440, 256)]
        for name in ("cmp_k_w1", "cmp_v_w1"):
            parts.append(i[name][l].reshape(2, 8, P, P).transpose(0, 2, 1, 3).reshape(2, P, 1024))
        for b, name in enumerate(("w_a_out", "w_b_out", "w_c_out")):
            parts.append(interleave(cut(7744 + 1024 * b, 1024), by_column_tile(i[name][l])))
        parts.append(by_column_tile(i["w_o"][l]))
        parts += ffn_chunks(i["ffn_w_gate"][l, 1], i["ffn_w_up"][l, 1], i["ffn_w_down"][l, 1])
        streams.append(np.concatenate(parts))
        assert len(streams[-1]) == N1, (len(streams[-1]), N1)
        p = np.zeros((P, PAR1["all"]), np.float32)
        def put(name, v):
            p[0:v.shape[0], PAR1[name]:PAR1[name] + v.shape[1]] = v
        put("ada_b", columns(i["ada_b"][l]))
        put("ln_g", columns(i["ln_g"][l].reshape(-1)))
        put("ln_b", columns(i["ln_b"][l].reshape(-1)))
        put("aw", i["conv_a_w"][l].reshape(TAPS_A, ND, P).transpose(2, 1, 0).reshape(P, -1))
        put("ab", columns(i["conv_a_b"][l]))
        put("ag", columns(i["norm_a_g"][l]))
        put("abb", columns(i["norm_a_b"][l]))
        put("xw", i["ssm_conv_w"][l].reshape(TAPS_B, NXB, P).transpose(2, 1, 0).reshape(P, -1))
        put("xb", columns(i["ssm_conv_b"][l]))
        put("nw", columns(i["ssm_norm_w"][l]))
        put("dsk", columns(np.repeat(i["ssm_d"][l], 64)))
        put("dtb", i["ssm_dt_bias"][l][:, None])
        put("alog", i["ssm_a_log"][l][:, None])
        for name, src in (("pek", "cmp_pe_k"), ("pev", "cmp_pe_v")):
            put(name, i[src][l].reshape(16, P).T)
        put("w2k", np.tile(i["cmp_k_w2"][l], (1, 2)))
        put("w2v", i["cmp_v_w2"][l])
        pars.append(p)
    return np.concatenate(streams), np.stack(pars)


def pack_modulation(i):
    w = [i["ada_w"][l].reshape(8, P, 9, 1024).transpose(2, 0, 1, 3).reshape(9 * 8, P, 1024) for l in range(DEPTH)]
    parts = [w[0][0:24]]
    for l in range(DEPTH):
        parts += [w[l][24:72], w[(l + 1) % DEPTH][0:24]]
    return np.concatenate(parts)


def pack2(i):
    i = {k[:-2]: v for k, v in i.items() if k.endswith("_2")}
    streams, pars = [], []
    for l in range(DEPTH):
        w = i["w_in"][l]
        cut = lambda a, n: by_column_tile(w[:, a:a + n])
        small = np.zeros((D, P), np.float32)
        small[:, 0:8] = w[:, 2304:2312]
        parts = [cut(0, 512), cut(512, 128), cut(640, 128), by_column_tile(small), cut(768, 256), cut(1024, 256),
                 cut(1280, 512), cut(1792, 512)]
        for name, at in (("w_att_branch", 2312), ("w_m_branch", 3336)):
            g = cut(at, 1024)
            br = by_column_tile(i[name][l]).reshape(4, 2, P, 512).transpose(0, 2, 1, 3).reshape(4, P, 1024)
            for q in range(4):
                parts += [g[2 * q:2 * q + 2], br[q:q + 1]]
        parts.append(by_column_tile(i["w_out"][l]))
        up, down = by_column_tile(i["w_ff1"][l]), by_row_tile(i["w_ff2"][l])
        parts += [up[0:1]] + [np.stack([up[f], down[f - 1]]) for f in range(1, NF2)] + [down[NF2 - 1:]]
        streams.append(np.concatenate(parts))
        assert len(streams[-1]) == N2
        p = np.zeros((P, PAR2["all"]), np.float32)
        def put(name, v):
            p[0:v.shape[0], PAR2[name]:PAR2[name] + v.shape[1]] = v
        put("nmix", columns(i["norm_mix"][l]))
        put("nffn", columns(i["norm_ffn"][l]))
        put("qn", np.tile(i["att_q_norm"][l], 2)[:, None])
        put("kn", np.tile(i["att_k_norm"][l], 2)[:, None])
        order = [4 * g + r for g in range(2) for r in (0, 2, 1, 3)]
        put("sink", np.tile(i["att_sinks"][l][order], (P, 1)))
        put("ib", i["m_gate_bias"][l][0:4, None])
        put("fb", i["m_gate_bias"][l][4:8, None])
        put("hn", columns(i["m_head_norm"][l]))
        pars.append(p)
    return np.concatenate(streams), np.stack(pars)


def kernel(**inputs):
    import concourse.bacc as bacc
    from concourse.bass_utils import run_bass_kernel_spmd

    i = {k: np.asarray(v) for k, v in inputs.items()}
    con, con1, con2 = constants()
    stream1, par1 = pack1(i)
    stream2, par2 = pack2(i)
    arrays = {
        "x_t": np.ascontiguousarray(i["x"][0].T.reshape(ND, P, S).transpose(1, 0, 2)),
        "c_t": np.ascontiguousarray(columns(i["c"][0])),
        "con": con, "con1": con1, "con2": con2,
        "stream1": stream1, "ada": pack_modulation(i), "stream2": stream2, "par1": par1, "par2": par2,
    }
    nc = bacc.Bacc("TRN2", target_bir_lowering=False, num_devices=1)
    args = [nc.dram_tensor(k + "_dram", a.shape, F32, kind="ExternalInput").ap() for k, a in arrays.items()]
    out = nc.dram_tensor("out_t", (P, ND, S), F32, kind="ExternalOutput").ap()
    build(nc, *args, out)
    got = run_bass_kernel_spmd(nc, [{k + "_dram": a for k, a in arrays.items()}], core_ids=[0]).results[0]["out_t"]
    return np.ascontiguousarray(np.asarray(got).transpose(2, 1, 0)).reshape(1, S, D)
```

```python
from contextlib import ExitStack

import numpy as np

import concourse.bass as bass
from concourse import mybir

F32 = mybir.dt.float32
F32R = mybir.dt.float32r
BF16 = mybir.dt.bfloat16
ALU = mybir.AluOpType
ACT = mybir.ActivationFunctionType
AX = mybir.AxisListType.X

P = 128
S = 256
D = 1024
ND = D // P
DEPTH = 2
RING = 9
HIGH = 3
FF = 2816
NF = FF // P
FF2 = 4096
NF2 = FF2 // P
TAPS_A, TAPS_B = 31, 4
NXB = 16
CMP = 15
ALPHA = (2.0 * DEPTH) ** 0.25
NEG = -1e30

C_FFN0 = 0
C_MIX = C_FFN0 + 3 * NF
C_GLU = C_MIX
C_XBC = C_GLU + 16
C_Z = C_XBC + 16
C_SMALL = C_Z + 8
C_Q = C_SMALL + 1
C_KC = C_Q + 8
C_VC = C_KC + 2
C_KS = C_VC + 2
C_KW = C_KS + 2
C_VS = C_KW + 2
C_VW = C_VS + 2
C_GA = C_VW + 2
C_CK = C_GA + 8
C_CV = C_CK + 2
C_PA = C_CV + 2
C_SSM = C_PA + 4
C_ATT = C_SSM + 12
C_PC = C_ATT + 16
C_WO = C_PC + 8
C_FFN1 = C_WO + 8
N1 = C_FFN1 + 3 * NF

E_Q = 0
E_K = 4
E_V = 5
E_IF = 6
E_QM = 7
E_KM = 9
E_VM = 11
E_OM = 15
E_GATE = 19
E_BR = E_GATE + 16
E_OUT = E_BR + 8
E_FFN = E_OUT + 8
N2 = E_FFN + 2 * NF2


def mix1(i):
    if i < C_CK:
        return i - C_MIX
    if i < C_ATT:
        return C_CK - C_MIX + [gate_b(n) for n in range(8)].index(i)
    return C_CK - C_MIX + 8 + (i - C_ATT) // 2


def gate_b(n):
    return C_SSM + 3 * (n // 2) + 2 * (n % 2)


MIX1 = C_CK - C_MIX + 16
MIX2 = E_BR


def offsets(parts):
    at, out = 0, {}
    for name, n in parts:
        out[name] = at
        at += n
    out["all"] = at
    return out


PAR1 = offsets([("ada_b", 72), ("ln_g", 24), ("ln_b", 24), ("aw", ND * TAPS_A), ("ab", 8), ("ag", 8), ("abb", 8),
                ("xw", NXB * TAPS_B), ("xb", NXB), ("nw", 8), ("dsk", 8), ("dtb", 1), ("alog", 1),
                ("pek", 16), ("pev", 16), ("w2k", 128), ("w2v", 64)])
PAR2 = offsets([("nmix", 8), ("nffn", 8), ("qn", 1), ("kn", 1), ("sink", 8), ("ib", 1), ("fb", 1), ("hn", 4)])
CON = offsets([("ident", 128), ("mean", 128), ("ones", 128), ("neg", 128), ("tri", 384), ("eps", 1), ("eps2", 1),
               ("valid", 1)])
CON1 = offsets([("rot", 128), ("dup", 256), ("rdup", 256), ("cos", 256), ("sin", 256), ("cmask", 32)])
CON2 = offsets([("blk", 128), ("mean128", 128), ("rot", 128), ("dup", 256), ("band", 128), ("cosq", 256),
                ("sinq", 256), ("cosk", 256), ("sink", 256), ("tri8", 384)])


def constants():
    f = np.float32
    p = np.arange(P)
    con = np.zeros((P, CON["all"]), f)
    def put(a, off, name, v):
        a[:, off[name]:off[name] + v.shape[1]] = v
    put(con, CON, "ident", np.eye(P, dtype=f))
    put(con, CON, "mean", np.full((P, P), 1.0 / D, f))
    put(con, CON, "ones", np.ones((P, P), f))
    put(con, CON, "neg", np.where(p[None, :] > p[:, None], NEG, 0.0))
    tri = (p[:, None] <= p[None, :]).astype(f)
    tri3 = np.concatenate([tri, np.ones((P, P), f), tri], 1)
    put(con, CON, "tri", tri3)
    put(con, CON, "eps", np.full((P, 1), 1e-5, f))
    put(con, CON, "eps2", np.full((P, 1), 1e-6, f))
    put(con, CON, "valid", (p[:, None] >= 31).astype(f))

    con1 = np.zeros((P, CON1["all"]), f)
    rot = np.zeros((P, P), f)
    for m in range(P):
        d = m % 64
        rot[m + 32 if d < 32 else m - 32, m] = -1.0 if d < 32 else 1.0
    dup = np.zeros((2, P, P), f)
    for par in range(2):
        for m in range(P):
            dup[par, par * 64 + m % 64, m] = 1.0
    put(con1, CON1, "rot", rot)
    put(con1, CON1, "dup", np.concatenate([dup[0], dup[1]], 1))
    put(con1, CON1, "rdup", np.concatenate([rot @ dup[0], rot @ dup[1]], 1))
    half = 32
    inv = (10000.0 ** (-np.arange(half, dtype=f) / f(half))).astype(f)
    ang = np.arange(S, dtype=f)[:, None] * inv[None, :]
    put(con1, CON1, "cos", np.tile(np.cos(ang).T, (4, 1)).astype(f))
    put(con1, CON1, "sin", np.tile(np.sin(ang).T, (4, 1)).astype(f))
    t = np.arange(S).reshape(2, P)
    ends = np.arange(16) * 16 + 31
    cm = np.where(ends[None, None, :] <= t[:, :, None], 0.0, NEG)
    put(con1, CON1, "cmask", cm.transpose(1, 0, 2).reshape(P, 32))

    con2 = np.zeros((P, CON2["all"]), f)
    put(con2, CON2, "blk", np.kron(np.eye(2), np.full((64, 64), 1.0 / 64)))
    put(con2, CON2, "mean128", np.full((P, P), 1.0 / P, f))
    rot2 = np.zeros((P, P), f)
    for m in range(P):
        d = m % 64
        if d < 16:
            rot2[m + 8 if d < 8 else m - 8, m] = -1.0 if d < 8 else 1.0
    put(con2, CON2, "rot", rot2)
    put(con2, CON2, "dup", np.concatenate([dup[0], dup[1]], 1))
    put(con2, CON2, "band", np.where(p[None, :] <= p[:, None], NEG, 0.0))
    inv = (f(500000.0) ** (-np.arange(0, 16, 2, dtype=f) / f(16))).astype(f)
    ang = (np.arange(S, dtype=f)[:, None] * inv[None, :]).T
    cos, sin = np.ones((64, S), f), np.zeros((64, S), f)
    cos[0:8] = cos[8:16] = np.cos(ang)
    sin[0:8] = sin[8:16] = np.sin(ang)
    for name, tab, by in (("cosq", cos, 0.125), ("sinq", sin, 0.125), ("cosk", cos, 1.0), ("sink", sin, 1.0)):
        put(con2, CON2, name, np.tile(tab, (2, 1)) * f(by))
    put(con2, CON2, "tri8", tri3 * f(0.125))
    return con, con1, con2


class Modulation:

    def __init__(self, sem):
        self.landed = [sem(f"ada_landed{k}") for k in range(ND)]
        self.used, self.summed, self.columns = sem("ada_used"), sem("ada_summed"), sem("ada_columns")

    def group(self, l, q, it=0):
        return l * 9 + 3 + 6 * q + it


class Stream:

    def __init__(self, per_layer, landed, done, earlier=None):
        self.n, self.landed, self.done, self.earlier = per_layer, landed, done, earlier

    def landed_before(self, slot):
        return DEPTH * self.earlier.uses(slot) if self.earlier else 0

    def done_before(self):
        return DEPTH * self.earlier.n if self.earlier else 0

    def uses(self, slot):
        return (self.n - slot + RING - 1) // RING

    def landed_value(self, l, i, rounds=0):
        return 16 * (self.landed_before(i % RING) + l * self.uses(i % RING) + i // RING + 1 + rounds)

    def done_value(self, l, i, rounds=0):
        return self.done_before() + l * self.n + i + 1 + RING + rounds * RING

    def last(self, slot):
        return self.n - 1 - (self.n - 1 - slot) % RING


SIGNALS1 = dict(
    layer_done=1, par=16, umod=24, uhi=24, ulo=24, hi=6 * NF + MIX1, lo=4 * NF, lo_g=2 * NF + MIX1,
    normed=1, aside=16, back=16, silu=2 * NF, hid=2 * NF, hidhi=2 * NF, hidlo=2 * NF, scaled=24, resid=24, mu=4, cent=32,
    sq=40, var=5, sd=5, sg=8, glu=8, copied=23, aconv=8, xconv=16, xsilu=16, kpe=2, rotp=12, rope=12,
    gelu=1, kc1=1, kcr=1, kc2=1, kcmp=1, vb=1, vbc=1, anrs=8, anorm=8, pv=8, outsg=3, gcopy=24, outm=24, dtexp=1, dtv=1,
    dtt=1, dttc=1, acs=1, acsc=1, xt=4, xdt=4, cb=4, cbm=4, bc=16, ee=16, arg=16, mm=16, yh=16, ysil=8, bnorm=8,
    cs=2, cmx=2, cex=2, cp=2, ct=2, ptc=2, sc=16, nmx=16, ex=16, pr=16, tr=16, ptt=16, oc=4)
SIGNALS2 = dict(
    layer_done=1, par=16, usq=16, uvar=2, usd=2, copied=11, hsq=4, hvar=9, hsd=9, qn=5, rotp=5, rope=5, dup=1,
    dupc=1, fexp=1, mt=1, rt=1, mtc=1, qk=4, qkm=4, bc=4, me=4, arg=4, ee=4, mm=4, num=4, absd=4, hh=4, hm=4,
    sc=4, nmx=4, ex=4, pr=4, tr=4, ptt=4, pv=4, oc=2, gcopy=8, outsg=1, outm=8, relu=NF2, hid=NF2, hidhi=NF2, hidlo=NF2, xres=8,
    umod=16, uhi=16, ulo=16, hi=2 * NF2 + MIX2, lo=NF2, lo_g=NF2 + MIX2, aside=16, back=16)


class Buffers:
    pass


def memory(nc, ctx):
    def sb(name, n, dt=F32):
        return ctx.enter_context(nc.sbuf_tensor(name, [P, n], dt))
    def typed_twice(name, n):
        with nc.sbuf_tensor(name, [P, n], F32) as whole:
            pass
        return whole, sb(name + "_parts", n, F32R)
    m = Buffers()
    def tiles(a, n):
        return a.rearrange("p (n t) -> p n t", n=n)
    m.ring, m.low = typed_twice("ring", RING * 1024)
    m.high = sb("high", HIGH * 1024, F32R)
    h, hparts = typed_twice("h", ND * S)
    m.h, m.uhi = tiles(h[:], ND), tiles(hparts[:], ND)
    u, ulo = typed_twice("u", ND * S)
    m.u, m.ulo = tiles(u[:], ND), tiles(ulo[:], ND)
    eb = sb("eb", 2048)
    pt, ptr = typed_twice("pt", 4096)
    ap_ = sb("ap", ND * (S + TAPS_A - 1))
    ac, acr = typed_twice("ac", ND * S)
    xp = sb("xp", NXB * (S + TAPS_B - 1))
    xc = sb("xc", NXB * S)
    z = sb("z", ND * S)
    qr = sb("qr", ND * S)
    kv = sb("kv", 2048)
    kraw = sb("kraw", 1024)
    kr = sb("kr", 2048)
    vt = sb("vt", 1024)
    gr = sb("gr", 512)
    vb = sb("vb", 1024)
    small = sb("small", 512)
    sg = sb("sg", 1024)
    st = sb("st", 512)
    m.con = sb("con", CON["all"])
    m.con_of = lambda name, n=P, at=0: m.con[:, CON[name] + at:CON[name] + at + n]
    m.conb = sb("conb", max(CON1["all"], CON2["all"]))
    m.par = sb("par", PAR1["all"])
    m.cvec = sb("cvec", 16)
    m.mod = sb("mod", 72)
    m.sc1 = sb("sc1", 24)
    m.raw = sb("raw", 48)
    m.raw_moved = sb("raw_moved", 40)
    m.zero = sb("zero", 512, BF16)

    m.eb, m.pt = eb, pt
    m.ada = [buf[:, k * 1024:(k + 1) * 1024] for buf, n in ((xc, 4), (z, 2), (qr, 2)) for k in range(n)]
    m.ada_acc = eb[:, 0:1024]
    m.uhi_ffn = tiles(acr[:], ND)
    m.sq = tiles(eb[:], ND)
    m.silu = tiles(pt[:, 0:768], 3)
    m.hid, m.hidlo = tiles(pt[:, 768:1536], 3), tiles(ptr[:, 768:1536], 3)
    m.hidhi = tiles(ptr[:, 1536:2304], 3)
    m.apad = tiles(ap_[:], ND)
    m.merged = tiles(ap_[:, 0:ND * S], ND)
    m.ac = tiles(ac[:], ND)
    m.oT = m.ac
    m.xpad = tiles(xp[:], NXB)
    m.xdt = xp[:, 0:2048].rearrange("p (a f) -> p a f", a=2)
    m.yb = tiles(xp[:, 2048:4096], ND)
    m.xc = tiles(xc[:], NXB)
    m.pcmp = xc[:, 0:1024].rearrange("p (a h n) -> p a h n", a=2, h=16)
    m.ptc = xc[:, 1024:2048].rearrange("p (g t) -> p g t", g=4)
    m.z = tiles(z[:], ND)
    m.qr = tiles(qr[:], ND)
    m.kc = kv[:, 0:1024].rearrange("p (g t) -> p g t", g=4)
    m.vc = kv[:, 1024:2048].rearrange("p (g t) -> p g t", g=4)
    m.kp = [eb[:, 0:960].rearrange("p (j c) -> p j c", j=16), eb[:, 1024:1984].rearrange("p (j c) -> p j c", j=16)]
    m.kraw = kraw[:].rearrange("p (b n t) -> p b n t", b=2, n=2)
    m.kr = kr[:].rearrange("p (b g t) -> p b g t", b=2, g=4)
    m.vt = vt[:].rearrange("p (b a f) -> p b a f", b=2, a=2)
    m.gr = gr[:].rearrange("p (g r n) -> p g r n", g=4, r=4)
    m.vb = vb[:].rearrange("p (g i f) -> p g i f", g=4, i=2)
    m.gk = small[:, 0:60]
    m.kcr = small[:, 60:120]
    m.kcmp = small[:, 120:180]
    m.gates = small[:, 180:276].rearrange("p (a c) -> p a c", a=2)
    m.dtt = small[:, 276:340]
    m.nacs = small[:, 340:372]
    m.cst = small[:, 372:436].rearrange("p (k a h) -> p k a h", k=2, a=2)
    m.nmx = small[:, 436:444].rearrange("p (b r) -> p b r", b=2)
    m.sums = small[:, 444:452].rearrange("p (b r) -> p b r", b=2)
    m.fac = small[:, 452:460].rearrange("p (b r) -> p b r", b=2)
    m.esink = small[:, 460:468].rearrange("p (b r) -> p b r", b=2)
    m.aexp = small[:, 468:469]
    m.dtw = kv[0:16, 0:1280].rearrange("p (k t) -> p k t", k=5)
    m.cbm = kv[:, 1280:2048].rearrange("p (b t) -> p b t", b=2)
    m.gate_a = tiles(pt[:, 2048:4096], ND)
    m.sq_a = m.gate_a
    m.gate_b_raw = [(kraw, sg)[n // 4][:, (n % 4) * S:(n % 4 + 1) * S] for n in range(8)]
    m.gate_b = tiles(xc[:, 2048:4096], ND)
    m.gate_c = m.z
    m.gate2 = tiles(xp[:, 0:4096], 16)
    m.dtraw = pt[0:16, 1536:1792]
    m.sg = tiles(sg[:], 4)
    m.sd, m.rs = st[:, 0:256], st[:, 256:512]
    m.ee = pt[:, 0:768].rearrange("p (b t) -> p b t", b=2)
    m.mm = pt[:, 768:1536].rearrange("p (b t) -> p b t", b=2)
    m.e = eb[:].rearrange("p (b r k) -> p b r k", b=2, r=4)
    m.ptt = pt[:].rearrange("p (b k r q) -> p b k r q", b=4, k=2, r=4)
    m.qk_raw = [ac[:, i * 256:(i + 1) * 256] for i in range(5)]
    m.hsq = [eb[:, i * 256:(i + 1) * 256] for i in range(5)]
    m.tmp = [sg[:, 0:256], sg[:, 256:512]]
    m.qa = tiles(qr[:, 0:1024], 4)
    m.qm = qr[:, 1024:1536].rearrange("p (n t) -> p n t", n=2)
    m.km = qr[:, 1536:2048].rearrange("p (n t) -> p n t", n=2)
    m.ka = kr[:, 0:512].rearrange("p (g t) -> p g t", g=2)
    m.kda = kr[:, 512:768]
    m.va = vt[:, 0:256].rearrange("p (a f) -> p a f", a=2)
    m.vm = xc[:, 0:1024].rearrange("p (a f) -> p a f", a=2)
    m.om = tiles(xc[:, 1024:2048], 4)
    m.ow = kv[0:4, 0:2048].rearrange("p (k t) -> p k t", k=8)
    m.att = tiles(z[:, 0:1024], 4)
    m.hm = tiles(z[:, 1024:2048], 4)
    m.rt = small[:, 0:8].rearrange("p (a h) -> p a h", a=2)
    m.qkm = xc[:, 2048:2816].rearrange("p (b t) -> p b t", b=2)
    m.em = xc[:, 2816:3328].rearrange("p (b t) -> p b t", b=2)
    m.den = xc[:, 3328:3840].rearrange("p (b t) -> p b t", b=2)
    m.mx = small[:, 8:16].rearrange("p (b r) -> p b r", b=2)
    m.ps = ctx.enter_context(nc.psum_tensor("ps", [P, 8, 512], F32))
    return m


def chunk_tile(m, i, k, a=0, b=P):
    at = (i % RING) * 1024 + k * P
    return m.ring[:, at + a:at + b]


def high_of(m, i):
    return m.high[:, (i % HIGH) * 1024:(i % HIGH + 1) * 1024]


def low_of(m, i):
    return m.low[:, (i % RING) * 1024:(i % RING + 1) * 1024]


def chunk_of(m, i):
    return m.ring[:, (i % RING) * 1024:(i % RING + 1) * 1024]


def product3(mm, out, m, i, k, xh, xl, start, stop, cols=(0, P), **kw):
    a, b = k * P + cols[0], k * P + cols[1]
    hi, lo = high_of(m, i)[:, a:b], low_of(m, i)[:, a:b]
    mm(out, hi, xh, start=start, stop=False, **kw)
    mm(out, hi, xl, start=False, stop=False, **kw)
    return mm(out, lo, xh, start=False, stop=stop, **kw)


def product3_tokens(mm, out, m, i, k, xh, xl, start, stop, cols=(0, P)):
    a, b = k * P + cols[0], k * P + cols[1]
    hi, lo = high_of(m, i)[:, a:b], low_of(m, i)[:, a:b]
    mm(out, xh, hi, start=start, stop=False)
    mm(out, xl, hi, start=False, stop=False)
    return mm(out, xh, lo, start=False, stop=stop)


def two(ps, bank, a=0, n=256):
    return ps[:, bank, a:a + 2 * n].rearrange("p (n t) -> p n t", n=2)



def stream_weights(sp, m, source, stream):
    def load(l, i, rounds=0):
        src = source[bass.ds(l * stream.n + i + rounds * RING, 1)].rearrange("a p n -> (a p) n")
        at = (i % RING) * 1024
        sp.dma_start(m.ring[:, at:at + 1024], src).then_inc(stream.landed[i % RING], 16)

    whole = stream.n // RING
    with sp.Fori(0, DEPTH) as l:
        for s in range(RING):
            if stream.earlier:
                sp.wait_ge(stream.done, stream.earlier.done_value(DEPTH - 1, stream.earlier.last(s)))
            sp.wait_ge(stream.done, stream.done_value(l, stream.last(s) - stream.n))
            load(l, s)
        with sp.Fori(0, whole - 1) as it:
            for s in range(RING):
                sp.wait_ge(stream.done, stream.done_value(l, s, it))
                load(l, RING + s, it)
        for i in range(whole * RING, stream.n):
            sp.wait_ge(stream.done, stream.done_value(l, i - RING))
            load(l, i)



def column_sums(t, mm, m, ada, g):
    t.wait_ge(ada.summed, g + 1)
    for j in range(8):
        last = mm(m.ps[:, 7, j:j + 1], m.ada_acc[:, j * P:(j + 1) * P], m.con_of("ones", 1), start=True, stop=True)
    last.then_inc(ada.columns, 1)


def tensor1(nc, t, m, sem, stream, ada):
    ps, con = m.ps, m.con_of
    landed, done = stream.landed, stream.done
    mm = nc.tensor.matmul

    def layer(l):
        at = lambda name, k: l * SIGNALS1[name] + k
        landed_at = lambda i, rounds=0: stream.landed_value(l, i, rounds)
        done_at = lambda i, rounds=0: stream.done_value(l, i, rounds)
        c1 = lambda name, n=P, at=0: m.conb[:, CON1[name] + at:CON1[name] + at + n]

        def project(i, out):
            t.wait_ge(sem["lo_g"], at("lo_g", NF + mix1(i) + 1))
            for k in range(ND):
                if i == C_MIX:
                    t.wait_ge(sem["ulo"], at("ulo", 8 + k + 1))
                last = product3(mm, out, m, i, k, m.uhi[:, k], m.ulo[:, k], start=k == 0, stop=k == ND - 1)
            return last

        def accumulate_ones(bank, src, signal, k0, ones):
            for n in range(ND):
                t.wait_ge(sem[signal], at(signal, k0 + n + 1))
                last = mm(ps[:, bank, 0:S], ones, src[:, n], start=n == 0, stop=n == ND - 1)
            return last

        def layer_norm(at, src, sq, mu_bank, var_bank, resid_k):
            accumulate_ones(mu_bank, src, resid_k[0], resid_k[1], con("mean")).then_inc(sem["mu"], 1)
            rms(at[0], sq, var_bank)

        def rms(k, sq, bank):
            accumulate_ones(bank, sq, "sq", 8 * k, con("mean")).then_inc(sem["var"], 1)

        def ffn(q, cb, per):
            if q == 1:
                t.wait_ge(sem["sd"], at("sd", 4))
            for b in range(4):
                mm(ps[:, b, :], m.zero[:, 0:P], m.zero[:], start=True, stop=False, skip_group_check=True)

            def up(i, f, fk, rounds=0):
                for c in range(2):
                    t.wait_ge(sem["lo"], at("lo", 2 * NF * q + 2 * fk + c + 1))
                    for k in range(ND):
                        if f == 0 and c == 0:
                            t.wait_ge(sem["ulo"], at("ulo", 16 * q + k + 1))
                        last = product3(mm, ps[:, 4 + f % 3, c * S:(c + 1) * S], m, i + c, k, m.uhi_ffn[:, k], m.ulo[:, k],
                                        start=k == 0, stop=k == ND - 1)
                    last.then_inc(done, 1)

            def down(i, f, fk, rounds=0, last=False):
                t.wait_ge(sem["lo_g"], at("lo_g", q * (NF + MIX1) + fk + 1))
                t.wait_ge(sem["hidlo"], at("hidlo", q * NF + fk + 1))
                for n in range(ND):
                    x = product3(mm, ps[:, n // 2, (n % 2) * S:(n % 2 + 1) * S], m, i, n, m.hidhi[:, f % 3],
                                 m.hidlo[:, f % 3], start=False, stop=last, skip_group_check=True)
                x.then_inc(done, 1)

            up(cb, 0, 0)
            with t.Fori(0, 18 // per) as it:
                for j in range(per):
                    up(cb + 2 + 3 * j, 1 + j, per * it + 1 + j)
                    if j == per - 1:
                        column_sums(t, mm, m, ada, ada.group(l, q, it))
                    down(cb + 4 + 3 * j, j, per * it + j)
            for f in range(19, NF):
                up(cb + 3 * f - 1, f, f)
                down(cb + 3 * f + 1, f - 1, f - 1)
            down(cb + 65, 21, 21, last=True)

        ffn(0, C_FFN0, 3)
        layer_norm((0,), m.h, m.u, 4, 5, ("resid", 0))

        unit = lambda j: 4 + j % 4
        j = 0
        for n in range(8):
            if n >= 4:
                t.wait_ge(sem["glu"], at("glu", n - 3))
            project(C_GLU + 2 * n, ps[:, unit(j), 0:S]).then_inc(done, 1)
            project(C_GLU + 2 * n + 1, ps[:, unit(j), S:2 * S]).then_inc(done, 1)
            j += 1
        for n in range(12):
            if n < 4:
                t.wait_ge(sem["glu"], at("glu", n + 5))
            else:
                t.wait_ge(sem["copied"], at("copied", n - 3))
            project(C_XBC + 2 * n, ps[:, unit(j), 0:S]).then_inc(done, 1)
            project(C_XBC + 2 * n + 1, ps[:, unit(j), S:2 * S]).then_inc(done, 1)
            j += 1
        t.wait_ge(sem["copied"], at("copied", 9))
        t.wait_ge(sem["lo_g"], at("lo_g", NF + mix1(C_SMALL) + 1))
        for a in range(2):
            for k in range(ND):
                product3_tokens(mm, ps[:, unit(j), a * 48:a * 48 + 48], m, C_SMALL, k, m.uhi[:, k, a * P:(a + 1) * P],
                                m.ulo[:, k, a * P:(a + 1) * P], start=k == 0, stop=k == ND - 1, cols=(0, 48))
        for k in range(ND):
            last = product3(mm, ps[0:16, unit(j), S:2 * S], m, C_SMALL, k, m.uhi[:, k], m.ulo[:, k],
                            start=k == 0, stop=k == ND - 1, cols=(64, 80))
        last.then_inc(done, 1)
        j += 1
        for n in range(8):
            t.wait_ge(sem["copied"], at("copied", 10 + n))
            project(C_Q + 2 * n, ps[:, unit(j), 0:S]).then_inc(done, 1)
            project(C_Q + 2 * n + 1, ps[:, unit(j), S:2 * S]).then_inc(done, 1)
            j += 1
        accumulate_ones(0, m.ac, "aconv", 0, con("mean")).then_inc(sem["mu"], 1)
        for b in range(2):
            t.wait_ge(sem["copied"], at("copied", 18 + b))
            for c in range(2):
                i = C_VS + 2 * b + c
                t.wait_ge(sem["lo_g"], at("lo_g", NF + mix1(i) + 1))
                for a in range(2):
                    for k in range(ND):
                        last = product3_tokens(mm, ps[:, unit(j), a * S + c * P:a * S + (c + 1) * P], m, i, k,
                                               m.uhi[:, k, a * P:(a + 1) * P], m.ulo[:, k, a * P:(a + 1) * P],
                                               start=k == 0, stop=k == ND - 1)
                last.then_inc(done, 1)
            j += 1
            if b == 0:
                rms(1, m.sq_a, 1)
        for n in range(4):
            t.wait_ge(sem["copied"], at("copied", 20 + n))
            for c in range(2):
                last = mm(ps[:, unit(j), c * S:(c + 1) * S], c1("rot"), m.qr[:, 2 * n + c], start=True, stop=True)
            last.then_inc(sem["rotp"], 1)
            j += 1
        for n in range(8):
            if n >= 2:
                t.wait_ge(sem["gcopy"], at("gcopy", n - 1))
            project(C_GA + n, ps[:, 2 + n % 2, 0:S]).then_inc(done, 1)

        def out_product(i, out, src):
            t.wait_ge(landed[i % RING], landed_at(i))
            for k in range(ND):
                last = mm(out, chunk_tile(m, i, k), src[:, k], start=k == 0, stop=k == 7)
            last.then_inc(done, 1)

        def project_a(n):
            if n == 0:
                t.wait_ge(sem["gcopy"], at("gcopy", 8))
                t.wait_ge(sem["anorm"], at("anorm", 8))
            out_product(C_PA + n, ps[:, n, 0:S], m.ac)

        for b in range(2):
            for g in range(4):
                t.wait_ge(sem["rope"], at("rope", 4 * b + g + 1))
                src = m.kraw[:, b, g // 2]
                mm(ps[:, unit(j), 0:S], c1("dup", P, (g % 2) * P), src, start=True, stop=True)
                mm(ps[:, unit(j), S:2 * S], c1("rdup", P, (g % 2) * P), src, start=True, stop=True)\
                    .then_inc(sem["rotp"], 1)
                j += 1
        t.wait_ge(sem["rope"], at("rope", 9))
        for b in range(2):
            t.wait_ge(sem["kpe"], at("kpe", b + 1))
            for c in range(2):
                i = C_CK + 2 * b + c
                t.wait_ge(landed[i % RING], landed_at(i))
                for k in range(8):
                    last = mm(ps[:, unit(j), b * 64:b * 64 + 60], chunk_tile(m, i, k), m.kp[b][:, 8 * c + k],
                              start=c == 0 and k == 0, stop=c == 1 and k == 7)
                last.then_inc(done, 1)
        j += 1
        project_a(0)
        t.wait_ge(sem["rope"], at("rope", 10))
        t.wait_ge(sem["gelu"], at("gelu", 1))
        mm(ps[:, unit(j), 0:60], m.par[:, PAR1["w2k"]:PAR1["w2k"] + P], m.gk, start=True, stop=True)\
            .then_inc(sem["kc1"], 1)
        j += 1
        project_a(1)
        t.wait_ge(sem["rope"], at("rope", 11))
        t.wait_ge(sem["kcr"], at("kcr", 1))
        mm(ps[:, unit(j), 0:60], c1("rot"), m.kcr, start=True, stop=True).then_inc(sem["kc2"], 1)
        j += 1
        project_a(2)
        t.wait_ge(sem["rope"], at("rope", 12))
        for g in range(4):
            last = mm(ps[:, unit(j), g * 64:(g + 1) * 64], m.gr[:, g].rearrange("p r n -> p (r n)"),
                      m.par[:, PAR1["w2v"]:PAR1["w2v"] + 64], start=True, stop=True)
        last.then_inc(sem["vb"], 1)
        j += 1
        project_a(3)

        ident16 = m.con[0:16, CON["ident"]:CON["ident"] + 16]
        t.wait_ge(sem["gelu"], at("gelu", 1))
        t.wait_ge(sem["dtv"], at("dtv", 1))
        for k in range(4):
            last = mm(ps[:, unit(j), 16 * k:16 * k + 16], m.dtw[:, 3 + k // 2, (k % 2) * P:(k % 2 + 1) * P],
                      ident16, start=True, stop=True)
        last.then_inc(sem["dtt"], 1)
        j += 1
        t.wait_ge(sem["kcr"], at("kcr", 1))
        t.wait_ge(sem["dttc"], at("dttc", 1))
        tri, ones = con("tri"), con("ones")
        adt = [m.dtt[:, 32:48], m.dtt[:, 48:64]]
        b = unit(j)
        mm(ps[:, b, 0:16], tri, adt[0], start=True, stop=True)
        mm(ps[:, b, 16:32], ones, adt[0], start=True, stop=False)
        mm(ps[:, b, 16:32], tri, adt[1], start=False, stop=True)
        mm(ps[0:16, b, 256:512], adt[0], con("tri", 256), start=True, stop=False)
        mm(ps[0:16, b, 384:512], adt[1], tri, start=False, stop=True).then_inc(sem["acs"], 1)
        j += 1
        for h in range(4):
            if h == 0:
                t.wait_ge(sem["kcmp"], at("kcmp", 1))
            elif h == 1:
                t.wait_ge(sem["vbc"], at("vbc", 1))
            elif h == 2:
                t.wait_ge(sem["dttc"], at("dttc", 1))
            else:
                t.wait_ge(sem["acsc"], at("acsc", 1))
            t.wait_ge(sem["xsilu"], at("xsilu", 8))
            for n in range(4):
                f = 4 * (h % 2) + n
                last = nc.tensor.transpose(ps[:, unit(j), n * P:(n + 1) * P],
                                           m.xc[:, f, (h // 2) * P:(h // 2 + 1) * P], con("ident"))
            last.then_inc(sem["xt"], 1)
            j += 1
        def ssm_head(h):
            t.wait_ge(sem["mm"], at("mm", h + 1))
            out = ps[64 * (h % 2):64 * (h % 2) + 64, h // 4, ((h // 2) % 2) * S:((h // 2) % 2 + 1) * S]
            x = m.xdt[:, :, 64 * h:64 * h + 64]
            mm(out, x[:, 0], m.mm[:, h % 2, 0:S], start=True, stop=False)
            mm(out[:, P:S], x[:, 1], m.mm[:, h % 2, S:S + P], start=False, stop=True).then_inc(sem["yh"], 1)

        t.wait_ge(sem["outm"], at("outm", 4))
        t.wait_ge(sem["xsilu"], at("xsilu", 16))
        t.wait_ge(sem["acsc"], at("acsc", 1))
        for g in range(4):
            if g == 0:
                t.wait_ge(sem["xdt"], at("xdt", 1))
            else:
                t.wait_ge(sem["arg"], at("arg", 4 * g - 1))
            B, C = m.xc[:, 8 + g], m.xc[:, 12 + g]
            mm(ps[:, unit(j), 0:256], B[:, 0:P], C, start=True, stop=True)
            mm(ps[:, unit(j), 256:384], B[:, P:S], C[:, P:S], start=True, stop=True).then_inc(sem["cb"], 1)
            j += 1
            for r in range(4):
                h = 4 * g + r
                if r == 2:
                    t.wait_ge(sem["cbm"], at("cbm", g + 1))
                elif r == 3:
                    t.wait_ge(sem["arg"], at("arg", 4 * g + 2))
                elif g == 0:
                    t.wait_ge(sem["xdt"], at("xdt", r + 2))
                elif r == 0:
                    t.wait_ge(sem["outm"], at("outm", 4 + g))
                else:
                    t.wait_ge(sem["arg"], at("arg", 4 * g))
                mm(ps[:, unit(j), 0:S], m.con[0:16, CON["ident"] + h:CON["ident"] + h + 1].to_broadcast([16, P]),
                   m.dtw[:, 2], start=True, stop=True).then_inc(sem["bc"], 1)
                j += 1
                if h >= 1:
                    ssm_head(h - 1)
                if r == 1:
                    if g == 0:
                        t.wait_ge(sem["xdt"], at("xdt", 4))
                    else:
                        t.wait_ge(sem["gcopy"], at("gcopy", 8 + 2 * g))
                    project(gate_b(2 * g), ps[:, unit(j), 0:S]).then_inc(done, 1)
                    j += 1
                elif r == 2:
                    t.wait_ge(sem["arg"], at("arg", 4 * g + 1))
                    out_product(C_SSM + 3 * g + 1, ps[:, unit(j), 0:S], m.ac)
                    j += 1
                elif r == 3:
                    t.wait_ge(sem["gcopy"], at("gcopy", 9 + 2 * g))
                    project(gate_b(2 * g + 1), ps[:, unit(j), 0:S]).then_inc(done, 1)
                    j += 1
        ssm_head(15)
        rms(2, m.sq, 0)

        kcmp = m.kcmp.rearrange("p (g n) -> p g n", g=4)
        for a in range(2):
            if a == 0:
                t.wait_ge(sem["arg"], at("arg", 15))
                t.wait_ge(sem["outm"], at("outm", 8))
            else:
                t.wait_ge(sem["arg"], at("arg", 16))
                t.wait_ge(sem["gcopy"], at("gcopy", 16))
            for h in range(16):
                lo = 64 * (h % 2)
                o = (h // 2) * 16
                last = mm(ps[:, unit(j + h % 2), o:o + CMP], m.qr[lo:lo + 64, h // 2, a * P:(a + 1) * P],
                          kcmp[lo:lo + 64, h // 4], start=True, stop=True)
            last.then_inc(sem["cs"], 1)
            j += 2
        for k in range(2):
            t.wait_ge(sem["cmx"], at("cmx", 1))
            t.wait_ge(sem["cp"], at("cp", 2))
            for g in (2 * k, 2 * k + 1):
                for a in range(2):
                    last = nc.tensor.transpose(ps[:, unit(j), (g % 2) * S + a * P:(g % 2) * S + (a + 1) * P],
                                               m.pcmp[:, a, 4 * g:4 * g + 4].rearrange("p r n -> p (r n)"),
                                               con("ident"))
            last.then_inc(sem["ct"], 1)
            j += 1

        def scores(i):
            g, a, b = i // 4, (i // 2) % 2, i % 2
            kl = P * (a + 1)
            if i >= 2:
                t.wait_ge(sem["ex"], at("ex", i - 1))
            for r in range(4):
                h = 4 * g + r
                lo = 64 * (h % 2)
                last = mm(score_view(ps, i, a)[:, place_of(r)], m.qr[lo:lo + 64, h // 2, a * P:(a + 1) * P],
                          m.kr[lo:lo + 64, b, g, 0:kl], start=True, stop=True)
            last.then_inc(sem["sc"], 1)

        def turn(i):
            a = (i // 2) % 2
            t.wait_ge(sem["pr"], at("pr", i + 1))
            if i >= 1:
                t.wait_ge(sem["ptt"], at("ptt", i))
            for k in range(a + 1):
                for r in range(4):
                    last = nc.tensor.transpose(ps[:, 2 + k, r * P:(r + 1) * P], m.e[:, i % 2, r, k * P:(k + 1) * P],
                                               con("ident"))
            last.then_inc(sem["tr"], 1)

        def values(i2):
            g, a = i2 // 2, i2 % 2
            o = ps[:, 0, :].rearrange("p (i t) -> p i t", i=2)
            if a == 0:
                if g >= 1:
                    t.wait_ge(sem["oc"], at("oc", g))
                for i in range(2):
                    mm(o[:, i], m.vb[:, g, i], m.ptc[:, g], start=i == 0, stop=False, skip_group_check=True)
            t.wait_ge(sem["ptt"], at("ptt", 2 * i2 + 2))
            for b in range(2):
                for k in range(a + 1):
                    for par in range(2):
                        last = mm(o[64 * par:64 * par + 64, :, a * P:(a + 1) * P],
                                  m.vt[:, b, k, g * 64:(g + 1) * 64],
                                  m.ptt[:, (2 * i2 + b) % 4, k, 2 * par:2 * par + 2], start=False, stop=a == 1 and b == 1 and k == 1,
                                  skip_group_check=True)
            last.then_inc(sem["pv"], 1)

        t.wait_ge(sem["ptc"], at("ptc", 2))
        scores(0)
        scores(1)
        for i in range(16):
            if i + 2 < 16:
                scores(i + 2)
            turn(i)
            if i >= 2 and i % 2 == 0:
                values(i // 2 - 1)
            if i % 2 == 0:
                if i >= 2:
                    t.wait_ge(sem["outm"], at("outm", 8 + i // 2))
                project(C_ATT + i, ps[:, 1, 0:S]).then_inc(done, 1)
            else:
                t.wait_ge(sem["gcopy"], at("gcopy", 17 + i // 2))
                if i == 1:
                    t.wait_ge(sem["bnorm"], at("bnorm", 8))
                out_product(C_ATT + i, ps[:, 1, 0:S], m.yb)
        values(7)
        for n in range(8):
            if n < 4:
                t.wait_ge(sem["ptc"], at("ptc", 2))
            else:
                t.wait_ge(sem["outm"], at("outm", 13 + n))
            if n == 0:
                t.wait_ge(sem["oc"], at("oc", 4))
            out_product(C_PC + n, ps[:, unit(j), 0:S], m.oT)
            j += 1

        t.wait_ge(sem["outm"], at("outm", 24))
        for n in range(8):
            if n >= 4:
                t.wait_ge(sem["scaled"], at("scaled", 5 + n))
            t.wait_ge(landed[(C_WO + n) % RING], landed_at(C_WO + n))
            for k in range(ND):
                last = mm(ps[:, unit(j), 0:S], chunk_tile(m, C_WO + n, k), m.merged[:, k], start=k == 0, stop=k == 7)
            last.then_inc(done, 1)
            j += 1
        layer_norm((3,), m.h, m.u, 0, 1, ("resid", 8))

        ffn(1, C_FFN1, 6)
        layer_norm((4,), m.h, m.u, 4, 5, ("resid", 16))

    for g in range(3):
        column_sums(t, mm, m, ada, g)
    with t.Fori(0, DEPTH) as l:
        layer(l)


def place_of(r):
    return (r % 2) * 2 + r // 2


def score_view(ps, i, a):
    b = 4 + 2 * (i % 2)
    return ps[:, b:b + 2, :].rearrange("p b (r k) -> p (b r) k", r=2)[:, :, 0:P * (a + 1)]





def scalar1(nc, a, m, sem, stream, par_source, aside):
    ps, con = m.ps, m.con_of
    landed, done = stream.landed, stream.done
    act = nc.scalar.activation

    def layer(l):
        at = lambda name, k: l * SIGNALS1[name] + k
        landed_at = lambda i, rounds=0: stream.landed_value(l, i, rounds)
        done_at = lambda i, rounds=0: stream.done_value(l, i, rounds)
        par = lambda name, at=0, n=1: m.par[:, PAR1[name] + at:PAR1[name] + at + n]
        gate = lambda i, n: m.mod[:, (3 * i + 2) * 8 + n:(3 * i + 2) * 8 + n + 1]
        bank = lambda j: 4 + j % 4

        a.wait_ge(sem["layer_done"], at("layer_done", 1))
        a.dma_start(m.par[:], par_source[bass.ds(l, 1)].rearrange("a p n -> (a p) n")).then_inc(sem["par"], 16)

        def high(i, rounds=0):
            act(high_of(m, i), chunk_of(m, i), ACT.Copy).then_inc(sem["hi"], 1)

        def first_highs(cb):
            for i in range(cb, cb + HIGH):
                a.wait_ge(landed[i % RING], landed_at(i))
                high(i)

        def high_u(i, dst):
            for n in range(ND):
                a.wait_ge(sem["umod"], at("umod", 8 * i + n + 1))
                act(dst[:, n], m.u[:, n], ACT.Copy).then_inc(sem["uhi"], 1)

        def later_high(i, rounds=0):
            a.wait_ge(landed[i % RING], landed_at(i, rounds))
            a.wait_ge(done, done_at(i - HIGH, rounds))
            high(i)

        def ffn(q, cb, per):
            high_u(2 * q, m.uhi_ffn)

            def silu(i, f, rounds=0):
                a.wait_ge(done, done_at(i, rounds))
                act(m.silu[:, f % 3], ps[:, 4 + f % 3, 0:S], ACT.Silu).then_inc(sem["silu"], 1)

            def hidden_high(f, fk):
                a.wait_ge(sem["hid"], at("hid", q * NF + fk + 1))
                act(m.hidhi[:, f % 3], m.hid[:, f % 3], ACT.Copy).then_inc(sem["hidhi"], 1)

            def step(i, f, fk, rounds=0):
                silu(i, f, rounds)
                later_high(i + 3, rounds)
                hidden_high(f, fk)
                later_high(i + 4, rounds)
                later_high(i + 5, rounds)

            later_high(cb + 3)
            silu(cb + 1, 0)
            later_high(cb + 4)
            hidden_high(0, 0)
            later_high(cb + 5)
            with a.Fori(0, 18 // per) as it:
                for j in range(per):
                    step(cb + 3 + 3 * j, 1 + j, per * it + 1 + j, it * (per // 3))
            for f in range(19, 21):
                step(cb + 3 * f, f, f)
            silu(cb + 63, 21)
            hidden_high(21, 21)
            a.wait_ge(done, done_at(cb + 65))
            for n in range(ND):
                act(m.u[:, n], ps[:, n // 2, (n % 2) * S:(n % 2 + 1) * S], ACT.Identity, scale=gate(2 * q, n))\
                    .then_inc(sem["scaled"], 1)

        def squares(k, src, dst, signal, k0, var_bank):
            for n in range(ND):
                a.wait_ge(sem[signal], at(signal, k0 + n + 1))
                act(dst[:, n], src[:, n], ACT.Square).then_inc(sem["sq"], 1)
            a.wait_ge(sem["var"], at("var", k + 1))
            act(m.sd, ps[:, var_bank, 0:S], ACT.Sqrt, bias=con("eps", 1)).then_inc(sem["sd"], 1)

        first_highs(C_FFN0)
        ffn(0, C_FFN0, 3)
        first_highs(C_MIX)
        squares(0, m.h, m.u, "cent", 0, 5)
        a.wait_ge(sem["normed"], at("normed", 1))
        a.dma_start(aside, m.h).then_inc(sem["aside"], 16)
        a.wait_ge(sem["aside"], at("aside", 16))
        high_u(1, m.uhi)

        j = 0
        for n in range(8):
            later_high(C_GLU + 2 * n + 3)
            a.wait_ge(done, done_at(C_GLU + 2 * n + 1))
            if n >= 4:
                a.wait_ge(sem["glu"], at("glu", n - 3))
            act(m.sg[:, n % 4], ps[:, bank(j), S:2 * S], ACT.Sigmoid).then_inc(sem["sg"], 1)
            later_high(C_GLU + 2 * n + 4)
            j += 1
        copied = sem["copied"]
        for n in range(8):
            later_high(C_XBC + 2 * n + 3)
            a.wait_ge(done, done_at(C_XBC + 2 * n + 1))
            act(m.xpad[:, 2 * n:2 * n + 2, TAPS_B - 1:], two(ps, bank(j)), ACT.Copy).then_inc(copied, 1)
            later_high(C_XBC + 2 * n + 4)
            j += 1
        for n in range(4):
            later_high(C_Z + 2 * n + 3)
            a.wait_ge(done, done_at(C_Z + 2 * n + 1))
            act(m.z[:, 2 * n:2 * n + 2], two(ps, bank(j)), ACT.Silu).then_inc(copied, 1)
            later_high(C_Z + 2 * n + 4)
            j += 1
        a.wait_ge(done, done_at(C_SMALL))
        act(m.gates, two(ps, bank(j), 0, 48), ACT.Sigmoid)
        act(m.dtraw, ps[0:16, bank(j), S:2 * S], ACT.Identity, bias=par("dtb")[0:16]).then_inc(copied, 1)
        later_high(C_SMALL + 3)
        j += 1
        for n in range(4):
            later_high(C_Q + 2 * n + 3)
            a.wait_ge(done, done_at(C_Q + 2 * n + 1))
            act(m.qr[:, 2 * n:2 * n + 2], two(ps, bank(j)), ACT.Copy, scale=0.125).then_inc(copied, 1)
            later_high(C_Q + 2 * n + 4)
            j += 1
        for b, dst in enumerate((m.kc, m.vc)):
            later_high(C_KC + 2 * b + 3)
            a.wait_ge(done, done_at(C_KC + 2 * b + 1))
            for par_ in range(2):
                for nxt in range(2):
                    last = act(dst[64 * nxt:64 * nxt + 64, par_::2, 0:S - nxt],
                               two(ps[64 * par_:64 * par_ + 64], bank(j))[:, :, nxt:S], ACT.Copy)
            last.then_inc(copied, 1)
            later_high(C_KC + 2 * b + 4)
            j += 1
        for b in range(2):
            later_high(C_KS + 2 * b + 3)
            a.wait_ge(done, done_at(C_KS + 2 * b + 1))
            act(m.kraw[:, b], two(ps, bank(j)), ACT.Copy).then_inc(copied, 1)
            later_high(C_KS + 2 * b + 4)
            j += 1
        for n in range(ND):
            a.wait_ge(sem["cent"], at("cent", 8 + n + 1))
            act(m.sq_a[:, n], m.ac[:, n], ACT.Square).then_inc(sem["sq"], 1)
        for b in range(2):
            later_high(C_VS + 2 * b + 3)
            a.wait_ge(done, done_at(C_VS + 2 * b + 1))
            act(m.vt[:, b], two(ps, bank(j)), ACT.Copy).then_inc(copied, 1)
            later_high(C_VS + 2 * b + 4)
            j += 1
            if b == 0:
                a.wait_ge(sem["var"], at("var", 2))
                act(m.sd, ps[:, 1, 0:S], ACT.Sqrt, bias=con("eps", 1)).then_inc(sem["sd"], 1)
        for n in range(ND):
            a.wait_ge(sem["anrs"], at("anrs", n + 1))
            act(m.ac[:, n], m.ac[:, n], ACT.Silu, scale=par("ag", n), bias=par("abb", n)).then_inc(sem["anorm"], 1)
        for n in range(NXB):
            if n % 2 == 0:
                a.wait_ge(done, done_at(C_GA + n // 2))
                act(m.gate_a[:, n // 2], ps[:, 2 + n // 2 % 2, 0:S], ACT.Copy).then_inc(sem["gcopy"], 1)
                if n // 2 + 3 < 8:
                    later_high(C_GA + n // 2 + 3)
            a.wait_ge(sem["xconv"], at("xconv", n + 1))
            act(m.xc[:, n], m.xc[:, n], ACT.Silu).then_inc(sem["xsilu"], 1)
        j += 12
        a.wait_ge(done, done_at(C_CV + 1))
        act(m.gk, ps[:, bank(j), 0:60], ACT.Gelu_apprx_tanh)
        for r in range(4):
            last = act(m.gr[:, :, r, 0:CMP], ps[:, bank(j), 64:124].rearrange("p (g n) -> p g n", g=4),
                       ACT.Gelu_apprx_tanh)
        last.then_inc(sem["gelu"], 1)
        j += 1
        a.wait_ge(sem["kc1"], at("kc1", 1))
        act(m.kcr, ps[:, bank(j), 0:60], ACT.Copy).then_inc(sem["kcr"], 1)
        j += 3

        act(m.dtw[:, 0], m.dtraw, ACT.Abs)
        act(m.aexp[0:16], par("alog")[0:16], ACT.Exp)
        a.drain()
        act(m.dtw[:, 1], m.dtw[:, 0], ACT.Exp, scale=-1.0).then_inc(sem["dtexp"], 1)

        act(m.gate_a[:], m.gate_a[:], ACT.Sigmoid).then_inc(sem["outsg"], 1)
        j += 4
        for n in range(2):
            later_high(gate_b(n))

        j += 1
        a.wait_ge(sem["acs"], at("acs", 1))
        act(m.nacs, ps[:, bank(j), 0:32], ACT.Copy, scale=-1.0)
        act(m.dtw[:, 2], ps[0:16, bank(j), S:2 * S], ACT.Copy).then_inc(sem["acsc"], 1)
        j += 5
        for h in range(16):
            a.wait_ge(sem["arg"], at("arg", h + 1))
            act(m.ee[:, h % 2], m.ee[:, h % 2], ACT.Exp).then_inc(sem["ee"], 1)
            if h % 2 == 1:
                a.wait_ge(done, done_at(gate_b(h // 2)))
                act(m.gate_b_raw[h // 2], ps[:, bank(j + 8 * (h // 4) + (3, 7)[h % 4 // 2]), 0:S], ACT.Copy)\
                    .then_inc(sem["gcopy"], 1)
                if h // 2 < 7:
                    later_high(gate_b(h // 2) + 3)
        j += 32
        a.drain()
        squares(2, m.yb, m.sq, "ysil", 0, 0)
        for n in range(8):
            last = act(m.gate_b[:, n], m.gate_b_raw[n], ACT.Sigmoid)
        last.then_inc(sem["outsg"], 1)

        for k in range(2):
            a.wait_ge(sem["cmx"], at("cmx", k + 1))
            act(m.pcmp[:, k, :, 0:CMP], m.pcmp[:, k, :, 0:CMP], ACT.Exp).then_inc(sem["cex"], 1)
        j += 4
        for k in range(2):
            a.wait_ge(sem["ct"], at("ct", k + 1))
            act(m.ptc[:, 2 * k:2 * k + 2], two(ps, bank(j)), ACT.Copy).then_inc(sem["ptc"], 1)
            j += 1

        def exps(i):
            k = (i // 2) % 2
            a.wait_ge(sem["nmx"], at("nmx", i + 1))
            if i >= 2:
                a.wait_ge(sem["tr"], at("tr", i - 1))
            for r in range(4):
                last = act(m.e[:, i % 2, r, 0:P * (k + 1)], score_view(ps, i, k)[:, r], ACT.Exp,
                           bias=m.nmx[:, i % 2, r:r + 1], accum_out=m.sums[:, i % 2, r:r + 1])
            last.then_inc(sem["ex"], 1)

        def turned(i):
            k = (i // 2) % 2
            a.wait_ge(sem["tr"], at("tr", i + 1))
            if i >= 4:
                a.wait_ge(sem["pv"], at("pv", (i - 4) // 2 + 1))
            act(m.ptt[:, i % 4, 0:k + 1].rearrange("p k r q -> p k (r q)"), ps[:, 2:3 + k, :], ACT.Copy)\
                .then_inc(sem["ptt"], 1)

        def heads_out(g):
            a.wait_ge(sem["pv"], at("pv", 2 * g + 2))
            act(m.oT[:, 2 * g:2 * g + 2], two(ps, 0), ACT.Copy).then_inc(sem["oc"], 1)

        exps(0)
        for i in range(16):
            if i + 1 < 16:
                exps(i + 1)
            turned(i)
            if i % 4 == 0 and i:
                heads_out(i // 4 - 1)
            if i % 2 == 0:
                a.wait_ge(done, done_at(C_ATT + i))
                act(m.gate_c[:, i // 2], ps[:, 1, 0:S], ACT.Copy).then_inc(sem["gcopy"], 1)
                if i < 14:
                    later_high(C_ATT + 2 + i)
                else:
                    a.dma_start(m.h, aside).then_inc(sem["back"], 16)
        heads_out(3)
        a.drain()
        act(m.gate_c[:], m.gate_c[:], ACT.Sigmoid).then_inc(sem["outsg"], 1)
        j += 8

        for n in range(ND):
            a.wait_ge(done, done_at(C_WO + n))
            act(m.u[:, n], ps[:, bank(j), 0:S], ACT.Identity, scale=gate(1, n)).then_inc(sem["scaled"], 1)
            j += 1
        first_highs(C_FFN1)
        squares(3, m.h, m.u, "cent", 16, 1)
        ffn(1, C_FFN1, 6)
        squares(4, m.h, m.u, "cent", 24, 5)

    with a.Fori(0, DEPTH) as l:
        layer(l)



def add_modulation(nc, v, m, ada, g, k):
    v.wait_ge(ada.landed[k], 16 * (g + 1))
    c = m.cvec[:, k:k + 1]
    if k == 0:
        last = nc.vector.tensor_scalar(m.ada_acc, m.ada[k], c, None, ALU.mult)
    else:
        last = nc.vector.scalar_tensor_tensor(m.ada_acc, m.ada[k], c, m.ada_acc, ALU.mult, ALU.add)
    last.then_inc(ada.used, 1)
    v.drain()
    if k == ND - 1:
        v.nop().then_inc(ada.summed, 1)


def keep_columns(nc, v, m, ada, g):
    v.wait_ge(ada.columns, g + 1)
    nc.vector.tensor_copy(m.raw_moved[:], m.raw[:, 8:48])
    v.drain()
    nc.vector.tensor_copy(m.raw[:, 0:40], m.raw_moved[:])
    nc.vector.tensor_copy(m.raw[:, 40:48], m.ps[:, 7, 0:8])
    v.drain()


def vector1(nc, v, m, sem, stream, ada):
    ps, con = m.ps, m.con_of
    landed, done = stream.landed, stream.done
    tt, ts, stt = nc.vector.tensor_tensor, nc.vector.tensor_scalar, nc.vector.scalar_tensor_tensor

    def layer(l):
        at = lambda name, k: l * SIGNALS1[name] + k
        landed_at = lambda i, rounds=0: stream.landed_value(l, i, rounds)
        done_at = lambda i, rounds=0: stream.done_value(l, i, rounds)
        par = lambda name, at=0, n=1: m.par[:, PAR1[name] + at:PAR1[name] + at + n]
        c1 = lambda name, n=P, at=0: m.conb[:, CON1[name] + at:CON1[name] + at + n]
        bank = lambda j: 4 + j % 4
        HIGHS = 3 * NF + MIX1

        def low(i, count):
            v.wait_ge(sem["hi"], at("hi", count))
            tt(low_of(m, i), chunk_of(m, i), high_of(m, i), ALU.subtract).then_inc(sem["lo"], 1)

        def scale_and_gate(i):
            ts(m.sc1[:, 8 * i:8 * i + 8], m.mod[:, (3 * i + 1) * 8:(3 * i + 2) * 8], 1.0, None, ALU.add)
            if i != 1:
                g = m.mod[:, (3 * i + 2) * 8:(3 * i + 3) * 8]
                ts(g, g, 0.5, None, ALU.mult)

        v.wait_ge(sem["par"], at("par", 16))
        tt(m.mod[:, 0:24], m.raw[:, 24:48], par("ada_b", 0, 24), ALU.add)
        v.drain()
        scale_and_gate(0)
        v.drain()

        def modulate(i):
            for n in range(ND):
                last = ts(m.u[:, n], m.h[:, n], m.sc1[:, 8 * i + n:8 * i + n + 1],
                          m.mod[:, 24 * i + n:24 * i + n + 1], ALU.mult, ALU.add)
                last.then_inc(sem["umod"], 1)

        def low_u(i, uhi):
            for n in range(ND):
                v.wait_ge(sem["uhi"], at("uhi", 8 * i + n + 1))
                tt(m.ulo[:, n], m.u[:, n], uhi[:, n], ALU.subtract).then_inc(sem["ulo"], 1)

        def residual(k0):
            for n in range(ND):
                v.wait_ge(sem["scaled"], at("scaled", k0 + n + 1))
                stt(m.h[:, n], m.h[:, n], ALPHA, m.u[:, n], ALU.mult, ALU.add).then_inc(sem["resid"], 1)

        def centre(k, src, bank_, k0):
            v.wait_ge(sem["mu"], at("mu", k + 1))
            for n in range(ND):
                tt(src[:, n], src[:, n], ps[:, bank_, 0:S], ALU.subtract).then_inc(sem["cent"], 1)

        def inverse_root(k):
            v.wait_ge(sem["sd"], at("sd", k + 1))
            nc.vector.reciprocal(m.rs, m.sd)
            v.drain()

        def norm(i, at, bank_):
            centre(at[0], m.h, bank_, 0)
            if i == 1:
                first_lows(1, C_FFN1)
            inverse_root(at[1])
            for n in range(ND):
                tt(m.h[:, n], m.h[:, n], m.rs, ALU.mult)
            v.drain()
            for n in range(ND):
                last = ts(m.h[:, n], m.h[:, n], par("ln_g", 8 * i + n), par("ln_b", 8 * i + n), ALU.mult, ALU.add)
            v.drain()
            return last

        def first_lows(q, cb):
            for c in range(3):
                low(cb + c, HIGHS * q + c + 1)

        def ffn(q, cb, per):
            low_u(2 * q, m.uhi_ffn)

            def hidden(f, fk):
                v.wait_ge(sem["silu"], at("silu", q * NF + fk + 1))
                tt(m.hid[:, f % 3], ps[:, 4 + f % 3, S:2 * S], m.silu[:, f % 3], ALU.mult)\
                    .then_inc(sem["hid"], 1)

            def hidden_low(f, fk):
                v.wait_ge(sem["hidhi"], at("hidhi", q * NF + fk + 1))
                tt(m.hidlo[:, f % 3], m.hid[:, f % 3], m.hidhi[:, f % 3], ALU.subtract)\
                    .then_inc(sem["hidlo"], 1)

            low(cb + 3, HIGHS * q + 4)
            hidden(0, 0)
            hidden_low(0, 0)
            low(cb + 5, HIGHS * q + 6)
            each = 8 // (2 * per // 3)
            with v.Fori(0, 18 // per) as it:
                g = ada.group(l, q, it)
                for j in range(per):
                    i, f, fk = cb + 3 + 3 * j, 1 + j, per * it + 1 + j
                    hidden(f, fk)
                    low(i + 3, HIGHS * q + 3 * fk + 4)
                    hidden_low(f, fk)
                    if j < 8 // each:
                        for k in range(each * j, each * j + each):
                            add_modulation(nc, v, m, ada, g, k)
                    low(i + 5, HIGHS * q + 3 * fk + 6)
                    if j == per - 1:
                        keep_columns(nc, v, m, ada, g)
            for f in range(19, 21):
                hidden(f, f)
                low(cb + 3 * f + 3, HIGHS * q + 3 * f + 4)
                hidden_low(f, f)
                if f == 19:
                    low(cb + 3 * f + 5, HIGHS * q + 3 * f + 6)
            hidden(21, 21)
            hidden_low(21, 21)
            residual(16 * q)

        modulate(0)
        first_lows(0, C_FFN0)
        ffn(0, C_FFN0, 3)
        tt(m.mod[:, 24:72], m.raw[:], par("ada_b", 24, 48), ALU.add)
        v.drain()
        scale_and_gate(1)
        scale_and_gate(2)
        norm(0, (0, 0), 4)
        v.nop().then_inc(sem["normed"], 1)
        modulate(1)

        nc.vector.memset(m.apad[:, :, 0:TAPS_A - 1], 0.0)
        nc.vector.memset(m.xpad[:, :, 0:TAPS_B - 1], 0.0)
        low_u(1, m.uhi)

        def glu(n):
            v.wait_ge(sem["sg"], at("sg", n + 1))
            tt(m.apad[:, n, TAPS_A - 1:], ps[:, bank(n), 0:S], m.sg[:, n % 4], ALU.mult).then_inc(sem["glu"], 1)

        for n in range(4):
            glu(n)
        v.drain()

        def conv(dst, src, w, b, taps, lo, hi, signal, between=()):
            for k in range(taps):
                for n in range(lo, hi):
                    if k == 0:
                        ts(dst[:, n], src[:, n, 0:S], par(w, n * taps), par(b, n), ALU.mult, ALU.add)
                    else:
                        last = stt(dst[:, n], src[:, n, k:k + S], par(w, n * taps + k), dst[:, n], ALU.mult, ALU.add)
                        if k == taps - 1:
                            last.then_inc(sem[signal], 1)
                if k in between:
                    glu(hi + between.index(k))
                v.drain()

        conv(m.ac, m.apad, "aw", "ab", TAPS_A, 0, 4, "aconv", between=(3, 7, 11, 15))
        conv(m.ac, m.apad, "aw", "ab", TAPS_A, 4, ND, "aconv")
        for q in range(2):
            v.wait_ge(sem["copied"], at("copied", 4 * q + 4))
            conv(m.xc, m.xpad, "xw", "xb", TAPS_B, 8 * q, 8 * q + 8, "xconv")
        for b, (src, pe) in enumerate(((m.kc, "pek"), (m.vc, "pev"))):
            v.wait_ge(sem["copied"], at("copied", 18 + b))
            for q in range(16):
                last = ts(m.kp[b][:, q].rearrange("p (g n) -> p g n", g=4), src[:, :, 2 * q:2 * q + 225:16],
                          par(pe, q), None, ALU.add)
            last.then_inc(sem["kpe"], 1)

        centre(1, m.ac, 0, 8)
        inverse_root(1)
        for n in range(ND):
            tt(m.ac[:, n], m.ac[:, n], m.rs, ALU.mult).then_inc(sem["anrs"], 1)
        j = 31

        def both(t, n=2, k=S):
            return t.rearrange("p (a t) -> p a t", a=1).to_broadcast([P, n, k])
        cos, sin = c1("cos", S), c1("sin", S)
        for n in range(4):
            v.wait_ge(sem["rotp"], at("rotp", n + 1))
            q, tmp = m.qr[:, 2 * n:2 * n + 2], m.sg[:, 2 * (n % 2):2 * (n % 2) + 2]
            tt(tmp, two(ps, bank(j)), both(sin), ALU.mult)
            tt(q, q, both(cos), ALU.mult)
            v.drain()
            tt(q, q, tmp, ALU.add).then_inc(sem["rope"], 1)
            j += 1
        for n in range(8):
            v.wait_ge(sem["rotp"], at("rotp", 5 + n))
            k, tmp = m.kr[:, n // 4, n % 4], m.sg[:, n % 4]
            tt(tmp, ps[:, bank(j), S:2 * S], sin, ALU.mult)
            tt(k, ps[:, bank(j), 0:S], cos, ALU.mult)
            v.drain()
            tt(k, k, tmp, ALU.add).then_inc(sem["rope"], 1)
            j += 1
        j += 2
        v.drain()
        v.wait_ge(sem["kc2"], at("kc2", 1))
        g4 = lambda t: t.rearrange("p (g n) -> p g n", g=4)
        ends = lambda t: both(t[:, 31:S:16], 4, CMP)
        tmp = m.sg[:, 0, 0:60]
        tt(g4(tmp), g4(ps[:, bank(j), 0:60]), ends(sin), ALU.mult)
        tt(g4(m.kcmp), g4(m.kcr), ends(cos), ALU.mult)
        v.drain()
        tt(m.kcmp, m.kcmp, tmp, ALU.add).then_inc(sem["kcmp"], 1)
        j += 1
        v.wait_ge(sem["vb"], at("vb", 1))
        for r in range(4):
            last = nc.vector.tensor_copy(m.vb[32 * r:32 * r + 32, :, r // 2, (r % 2) * 64:(r % 2) * 64 + 64],
                                         ps[32 * r:32 * r + 32, bank(j), 0:256].rearrange("p (g d) -> p g d", g=4))
        last.then_inc(sem["vbc"], 1)
        j += 1

        v.wait_ge(sem["dtexp"], at("dtexp", 1))
        log1p(nc, v, m.dtw[:, 1], m.dtw[:, 0], m.dtw[:, 2], m.dtw[:, 3], m.dtw[:, 4])
        ts(m.dtw[:, 0], m.dtraw, 0.0, None, ALU.max)
        v.drain()
        tt(m.dtw[:, 3], m.dtw[:, 3], m.dtw[:, 0], ALU.add)
        v.drain()
        ts(m.dtw[:, 4], m.dtw[:, 3], m.aexp[0:16], -1.0, ALU.mult, ALU.mult).then_inc(sem["dtv"], 1)

        def add_branch(branch, n, y, chunk):
            g = (m.gate_b, m.gate_c)[branch - 1][:, n]
            if n == 0:
                v.wait_ge(sem["outsg"], at("outsg", 1 + branch))
            v.wait_ge(done, done_at(chunk))
            tt(g, y, g, ALU.mult)
            v.drain()
            tt(m.merged[:, n], m.merged[:, n], g, ALU.add).then_inc(sem["outm"], 1)

        def first_branch(n, chunk, b):
            v.wait_ge(done, done_at(chunk))
            tt(m.merged[:, n], ps[:, b, 0:S], m.gate_a[:, n], ALU.mult).then_inc(sem["outm"], 1)

        v.wait_ge(sem["outsg"], at("outsg", 1))
        for n in range(4):
            first_branch(n, C_PA + n, n)

        v.wait_ge(sem["dtt"], at("dtt", 1))
        nc.vector.tensor_copy(m.dtt, ps[:, bank(j), 0:64]).then_inc(sem["dttc"], 1)
        v.drain()
        j += 2
        for h in range(4):
            v.wait_ge(sem["xt"], at("xt", h + 1))
            a, o = h // 2, h % 2
            dt = m.dtt[:, 16 * a + 8 * o:16 * a + 8 * o + 8].rearrange("p (h d) -> p h d", d=1).to_broadcast([P, 8, 64])
            tt(m.xdt[:, a, 512 * o:512 * o + 512].rearrange("p (h d) -> p h d", h=8),
               ps[:, bank(j), :].rearrange("p (h d) -> p h d", h=8), dt, ALU.mult).then_inc(sem["xdt"], 1)
            j += 1
        def exponent(h, j):
            if h % 4 == 0:
                v.wait_ge(sem["cb"], at("cb", h // 4 + 1))
                tt(m.cbm[:, (h // 4) % 2], ps[:, bank(j), 0:384], con("tri", 384), ALU.mult)\
                    .then_inc(sem["cbm"], 1)
                j += 1
            v.wait_ge(sem["bc"], at("bc", h + 1))
            ts(m.ee[:, h % 2, 0:S], ps[:, bank(j), 0:S], m.nacs[:, h:h + 1], 0.0, ALU.add, ALU.min)
            ts(m.ee[:, h % 2, S:S + P], ps[:, bank(j), P:S], m.nacs[:, 16 + h:17 + h], 0.0, ALU.add, ALU.min)\
                .then_inc(sem["arg"], 1)
            return j + 1 + (h % 4 > 0)

        s_unit = j
        j = exponent(0, j)
        for h in range(16):
            if h + 1 < 16:
                j = exponent(h + 1, j)
            v.drain()
            v.wait_ge(sem["ee"], at("ee", h + 1))
            if h >= 2:
                v.wait_ge(sem["yh"], at("yh", h - 1))
            tt(m.mm[:, h % 2], m.ee[:, h % 2], m.cbm[:, (h // 4) % 2], ALU.mult).then_inc(sem["mm"], 1)
            if h % 4 == 2:
                first_branch(4 + h // 4, C_SSM + 3 * (h // 4) + 1, bank(s_unit + 5))
        for n in range(ND):
            v.wait_ge(sem["yh"], at("yh", 4 * (n // 2) + 4))
            stt(m.yb[:, n], m.xc[:, n], par("dsk", n), ps[:, n // 2, (n % 2) * S:(n % 2 + 1) * S], ALU.mult, ALU.add)
        v.drain()
        for n in range(ND):
            tt(m.yb[:, n], m.yb[:, n], m.z[:, n], ALU.mult).then_inc(sem["ysil"], 1)
        inverse_root(2)
        for n in range(ND):
            stt(m.yb[:, n], m.yb[:, n], par("nw", n), m.rs, ALU.mult, ALU.mult).then_inc(sem["bnorm"], 1)

        nc.vector.memset(m.pcmp, 0.0)
        v.drain()
        wide = lambda t, n, k: t.rearrange("p (h d) -> p h d", d=1).to_broadcast([P, n, k])
        for a in range(2):
            v.wait_ge(sem["cs"], at("cs", a + 1))
            p = m.pcmp[:, a, :, 0:CMP]
            for odd in range(2):
                s = ps[:, bank(j + odd), 0:128].rearrange("p (h n) -> p h n", h=8)[:, :, 0:CMP]
                tt(p[:, odd::2], s, both(c1("cmask", CMP, 16 * a), 8, CMP), ALU.add)
            v.drain()
            nc.vector.tensor_reduce(m.cst[:, 0, a], p, AX, ALU.max)
            v.drain()
            tt(p, p, wide(m.cst[:, 0, a], 16, CMP), ALU.subtract).then_inc(sem["cmx"], 1)
            j += 2
        for a in range(2):
            p, f = m.pcmp[:, a, :, 0:CMP], m.cst[:, 1, a]
            v.wait_ge(sem["cex"], at("cex", a + 1))
            nc.vector.tensor_reduce(f, p, AX, ALU.add)
            v.drain()
            nc.vector.reciprocal(f, f)
            v.drain()
            tt(f, f, m.gates[:, a, 0:48:3], ALU.mult)
            v.drain()
            if a == 0:
                ts(f, f, con("valid", 1), None, ALU.mult)
                v.drain()
            tt(p, p, wide(f, 16, CMP), ALU.mult).then_inc(sem["cp"], 1)
        j += 2

        def maxima(i):
            a = (i // 2) % 2
            v.wait_ge(sem["sc"], at("sc", i + 1))
            s = score_view(ps, i, a)
            diag = s[:, :, a * P:(a + 1) * P]
            tt(diag, diag, both(con("neg"), 4, P), ALU.add)
            v.drain()
            nc.vector.tensor_reduce(m.nmx[:, i % 2], s, AX, ALU.max, negate=True).then_inc(sem["nmx"], 1)

        def weights(i):
            g, a, b = i // 4, (i // 2) % 2, i % 2
            f = m.fac[:, i % 2]
            v.wait_ge(sem["ex"], at("ex", i + 1))
            nc.vector.reciprocal(f, m.sums[:, i % 2])
            v.drain()
            gate = m.gates[:, a, 12 * g:12 * g + 12].rearrange("p (i q c) -> p q i c", i=2, q=2)[:, :, :, 1 + b]
            ff = f.rearrange("p (q i) -> p q i", q=2)
            tt(ff, ff, gate, ALU.mult)
            v.drain()
            for r in range(4):
                p = m.e[:, i % 2, r, 0:P * (a + 1)]
                last = ts(p, p, f[:, r:r + 1], None, ALU.mult)
            last.then_inc(sem["pr"], 1)

        maxima(0)
        maxima(1)
        for i in range(16):
            weights(i)
            if i + 2 < 16:
                maxima(i + 2)
            if i % 2 == 1:
                add_branch(1, i // 2, ps[:, 1, 0:S], C_ATT + i)
        for n in range(8):
            add_branch(2, n, ps[:, bank(j), 0:S], C_PC + n)
            j += 1

        v.wait_ge(sem["back"], at("back", 16))
        residual(8)
        norm(1, (2, 3), 0)
        modulate(2)
        ffn(1, C_FFN1, 6)
        last = norm(2, (3, 4), 4)
        v.nop().then_inc(sem["layer_done"], 1)

    for g in range(3):
        for k in range(ND):
            add_modulation(nc, v, m, ada, g, k)
        keep_columns(nc, v, m, ada, g)
    with v.Fori(0, DEPTH) as l:
        layer(l)



def gpsimd1(nc, g, m, sem, stream, ada, ada_source):
    def load(group, k):
        g.dma_start(m.ada[k], ada_source[bass.ds(group * ND + k, 1)].rearrange("a p n -> (a p) n"))\
            .then_inc(ada.landed[k], 16)

    def load_later(group, k):
        g.wait_ge(ada.used, (group - 1) * ND + k + 1)
        load(group, k)

    for k in range(ND):
        g.dma_start(m.ada[k], ada_source[k]).then_inc(ada.landed[k], 16)
    for group in range(1, 3):
        for k in range(ND):
            g.wait_ge(ada.used, (group - 1) * ND + k + 1)
            g.dma_start(m.ada[k], ada_source[group * ND + k]).then_inc(ada.landed[k], 16)

    def layer(l):
        at = lambda name, k: l * SIGNALS1[name] + k

        def low_down(i, q, fk):
            g.wait_ge(sem["hi"], at("hi", (3 * NF + MIX1) * q + i_of(fk)))
            nc.gpsimd.tensor_tensor(low_of(m, i), chunk_of(m, i), high_of(m, i), ALU.subtract)\
                .then_inc(sem["lo_g"], 1)
        i_of = lambda fk: 3 * fk + 5

        def ffn(q, cb, per):
            each = 8 // (2 * per // 3)
            g.wait_ge(sem["umod"], at("umod", 16 * q + 1))
            for k in range(ND):
                load_later(ada.group(l, q), k)
            low_down(cb + 4, q, 0)

            def steps(it, more):
                for j in range(per):
                    low_down(cb + 7 + 3 * j, q, per * it + 1 + j)
                    if more and j < 8 // each:
                        for k in range(each * j, each * j + each):
                            load_later(ada.group(l, q, it + 1), k)

            with g.Fori(0, 18 // per - 1) as it:
                steps(it, True)
            steps(18 // per - 1, False)
            for f in range(19, 21):
                low_down(cb + 3 * f + 4, q, f)
            g.wait_ge(sem["hi"], at("hi", (3 * NF + MIX1) * q + 3 * NF))
            nc.gpsimd.tensor_tensor(low_of(m, cb + 65), chunk_of(m, cb + 65), high_of(m, cb + 65),
                                    ALU.subtract).then_inc(sem["lo_g"], 1)

        ffn(0, C_FFN0, 3)
        split = [*range(C_MIX, C_CK), *(gate_b(n) for n in range(8)), *range(C_ATT, C_ATT + 16, 2)]
        for i in split:
            g.wait_ge(sem["hi"], at("hi", 3 * NF + mix1(i) + 1))
            nc.gpsimd.tensor_tensor(low_of(m, i), chunk_of(m, i), high_of(m, i), ALU.subtract)\
                .then_inc(sem["lo_g"], 1)
        ffn(1, C_FFN1, 6)

    with g.Fori(0, DEPTH) as l:
        layer(l)


def log1p(nc, v, y, z, z2, out, p):
    tt, ts, stt = nc.vector.tensor_tensor, nc.vector.tensor_scalar, nc.vector.scalar_tensor_tensor
    ts(z, y, 2.0, None, ALU.add)
    v.drain()
    nc.vector.reciprocal(z, z)
    v.drain()
    tt(z, z, y, ALU.mult)
    v.drain()
    tt(z2, z, z, ALU.mult)
    v.drain()
    ts(p, z2, 1.0 / 15, None, ALU.mult)
    v.drain()
    for c in (13, 11, 9, 7, 5, 3):
        stt(p, p, 1.0 / c, z2, ALU.add, ALU.mult)
        v.drain()
    stt(out, p, 1.0, z, ALU.add, ALU.mult)
    v.drain()
    ts(out, out, 2.0, None, ALU.mult)
    v.drain()



def tensor2(nc, t, m, sem, stream):
    ps, con = m.ps, m.con_of
    landed, done = stream.landed, stream.done
    mm = nc.tensor.matmul

    def layer(l):
        at = lambda name, k: l * SIGNALS2[name] + k
        landed_at = lambda i, rounds=0: stream.landed_value(l, i, rounds)
        done_at = lambda i, rounds=0: stream.done_value(l, i, rounds)
        c2 = lambda name, n=P, at=0: m.conb[:, CON2[name] + at:CON2[name] + at + n]
        unit = lambda j: 4 + j % 4

        def project(i, out, cols=(0, P)):
            t.wait_ge(sem["lo_g"], at("lo_g", i + 1))
            for k in range(ND):
                if i == E_Q:
                    t.wait_ge(sem["ulo"], at("ulo", k + 1))
                last = product3(mm, out, m, i, k, m.uhi[:, k], m.ulo[:, k], start=k == 0, stop=k == ND - 1, cols=cols)
            return last

        def token_major(i, bank, width, col):
            t.wait_ge(sem["lo_g"], at("lo_g", i + 1))
            for a in range(2):
                for k in range(ND):
                    last = product3_tokens(mm, ps[:, bank, a * width + col:a * width + col + P], m, i, k,
                                           m.uhi[:, k, a * P:(a + 1) * P], m.ulo[:, k, a * P:(a + 1) * P],
                                           start=k == 0, stop=k == ND - 1)
            return last

        def rms(k):
            for n in range(ND):
                t.wait_ge(sem["usq"], at("usq", 8 * k + n + 1))
                last = mm(ps[:, 0, 0:S], con("mean"), m.sq[:, n], start=n == 0, stop=n == ND - 1)
            last.then_inc(sem["uvar"], 1)

        rms(0)
        j = 0
        def pair(i, j):
            project(i, ps[:, unit(j), 0:S]).then_inc(done, 1)
            project(i + 1, ps[:, unit(j), S:2 * S]).then_inc(done, 1)
            return j + 1
        j = pair(E_Q, j)
        j = pair(E_Q + 2, j)
        project(E_K, ps[:, unit(j), 0:S]).then_inc(done, 1)
        j += 1
        token_major(E_V, unit(j), P, 0).then_inc(done, 1)
        j += 1
        t.wait_ge(sem["copied"], at("copied", 1))
        project(E_IF, ps[0:4, unit(j), 0:S], cols=(0, 4))
        project(E_IF, ps[0:4, unit(j), S:2 * S], cols=(4, 8)).then_inc(done, 1)
        j += 1
        t.wait_ge(sem["copied"], at("copied", 2))
        j = pair(E_QM, j)
        t.wait_ge(sem["copied"], at("copied", 3))
        j = pair(E_KM, j)
        for q in range(2):
            t.wait_ge(sem["copied"], at("copied", 4 + q))
            for c in range(2):
                token_major(E_VM + 2 * q + c, unit(j), S, c * P).then_inc(done, 1)
            j += 1
        t.wait_ge(sem["copied"], at("copied", 6))
        j = pair(E_OM, j)
        t.wait_ge(sem["copied"], at("copied", 7))
        j = pair(E_OM + 2, j)
        def gate_pair(k):
            if k >= 4:
                t.wait_ge(sem["gcopy"], at("gcopy", k - 3))
            project(E_GATE + 2 * k, ps[:, k % 4, 0:S]).then_inc(done, 1)
            project(E_GATE + 2 * k + 1, ps[:, k % 4, S:2 * S]).then_inc(done, 1)

        gate_pair(0)
        for n in range(5):
            if n < 4:
                t.wait_ge(sem["copied"], at("copied", 8 + n))
            else:
                t.wait_ge(sem["hsd"], at("hsd", 1))
            mm(ps[:, unit(j), 0:S], c2("blk"), m.hsq[n], start=True, stop=True).then_inc(sem["hvar"], 1)
            j += 1
        gate_pair(1)
        for n in range(5):
            if n < 4:
                t.wait_ge(sem["hsd"], at("hsd", 2 + n))
            else:
                t.wait_ge(sem["rope"], at("rope", 1))
            t.wait_ge(sem["qn"], at("qn", n + 1))
            mm(ps[:, unit(j), 0:S], c2("rot"), m.qk_raw[n], start=True, stop=True).then_inc(sem["rotp"], 1)
            j += 1
        gate_pair(2)
        t.wait_ge(sem["rope"], at("rope", 5))
        mm(ps[:, unit(j), 0:S], c2("dup"), m.kda, start=True, stop=True)
        mm(ps[:, unit(j), S:2 * S], c2("dup", P, P), m.kda, start=True, stop=True).then_inc(sem["dup"], 1)
        j += 1
        for k in range(3, 8):
            gate_pair(k)
        t.wait_ge(sem["mt"], at("mt", 1))
        for a in range(2):
            last = mm(ps[:, unit(j), 4 * a:4 * a + 4], m.ow[:, 3, a * P:(a + 1) * P],
                      m.con[0:4, CON["ident"]:CON["ident"] + 4], start=True, stop=True)
        last.then_inc(sem["rt"], 1)

        def scores(i):
            g, a = i // 2, i % 2
            if i >= 2:
                t.wait_ge(sem["ex"], at("ex", i - 1))
            for r in range(4):
                lo = 64 * (r % 2)
                last = mm(score_view(ps, i, a)[:, place_of(r)], m.qa[lo:lo + 64, 2 * g + r // 2, a * P:(a + 1) * P],
                          m.ka[lo:lo + 64, g, 0:P * (a + 1)], start=True, stop=True)
            last.then_inc(sem["sc"], 1)

        def turn(i):
            t.wait_ge(sem["pr"], at("pr", i + 1))
            if i >= 1:
                t.wait_ge(sem["ptt"], at("ptt", i))
            for k in range(i % 2 + 1):
                for r in range(4):
                    last = nc.tensor.transpose(ps[:, 2 + k, r * P:(r + 1) * P], m.e[:, i % 2, r, k * P:(k + 1) * P],
                                               con("ident"))
            last.then_inc(sem["tr"], 1)

        def values(i):
            g, a = i // 2, i % 2
            o = ps[:, g, :].rearrange("p (i t) -> p i t", i=2)
            t.wait_ge(sem["ptt"], at("ptt", i + 1))
            for k in range(a + 1):
                for q in range(2):
                    last = mm(o[64 * q:64 * q + 64, :, a * P:(a + 1) * P], m.va[:, k, g * 64:(g + 1) * 64],
                              m.ptt[:, i, k, 2 * q:2 * q + 2], start=a == 0, stop=a == 1 and k == 1,
                              skip_group_check=True)
            last.then_inc(sem["pv"], 1)

        t.wait_ge(sem["dupc"], at("dupc", 1))
        t.wait_ge(sem["mtc"], at("mtc", 1))
        t.wait_ge(sem["gcopy"], at("gcopy", 8))
        scores(0)
        scores(1)
        for i in range(4):
            if i + 2 < 4:
                scores(i + 2)
            turn(i)
            if i >= 1:
                values(i - 1)
        values(3)

        t.wait_ge(sem["oc"], at("oc", 2))
        j = 0

        def head_out(h):
            t.wait_ge(sem["mm"], at("mm", h + 1))
            for a, lhs in enumerate((m.vm, None)):
                o = ps[:, h, a * S:(a + 1) * S]
                left = lambda s: con("ones") if lhs is None else m.vm[:, s, h * P:(h + 1) * P]
                mm(o, left(0), m.mm[:, h % 2, 0:S], start=True, stop=False)
                last = mm(o[:, P:S], left(1), m.mm[:, h % 2, S:S + P], start=False, stop=True)
            last.then_inc(sem["num"], 1)

        for h in range(4):
            lo = 64 * (h % 2)
            if h >= 2:
                t.wait_ge(sem["qkm"], at("qkm", h - 1))
            q, k = m.qm[lo:lo + 64, h // 2], m.km[lo:lo + 64, h // 2]
            mm(ps[:, unit(j), 0:S], k[:, 0:P], q, start=True, stop=True)
            mm(ps[:, unit(j), S:S + P], k[:, P:S], q[:, P:S], start=True, stop=True).then_inc(sem["qk"], 1)
            j += 1
            if h >= 2:
                t.wait_ge(sem["arg"], at("arg", h - 1))
            mm(ps[:, unit(j), :], m.con[0:4, CON["ident"] + h:CON["ident"] + h + 1].to_broadcast([4, P]),
               m.ow[:, 5:7].rearrange("p k t -> p (k t)"), start=True, stop=True).then_inc(sem["bc"], 1)
            j += 1
            if h >= 1:
                head_out(h - 1)
        head_out(3)
        for h in range(4):
            if h % 2 == 0:
                t.wait_ge(sem["qkm"], at("qkm", 3 + h // 2))
            else:
                t.wait_ge(sem["arg"], at("arg", 3 + h // 2))
            t.wait_ge(sem["hsq"], at("hsq", h + 1))
            mm(ps[:, unit(j), 0:S], c2("mean128"), m.sq[:, h], start=True, stop=True).then_inc(sem["hvar"], 1)
            j += 1

        for b, src in enumerate((m.att, m.hm)):
            for q in range(4):
                k4 = 4 * b + q
                if k4 < 4:
                    t.wait_ge(sem["hsd"], at("hsd", 6 + k4))
                else:
                    t.wait_ge(sem["outm"], at("outm", k4 - 3))
                if k4 == 4:
                    t.wait_ge(sem["hm"], at("hm", 4))
                i = E_BR + k4
                t.wait_ge(landed[i % RING], landed_at(i))
                for c in range(2):
                    for k in range(4):
                        last = mm(ps[:, unit(j), c * S:(c + 1) * S], chunk_tile(m, i, 4 * c + k), src[:, k],
                                  start=k == 0, stop=k == 3)
                last.then_inc(done, 1)
                j += 1
        t.wait_ge(sem["outm"], at("outm", 8))
        for q in range(4):
            for c in range(2):
                i = E_OUT + 2 * q + c
                t.wait_ge(landed[i % RING], landed_at(i))
                for k in range(ND):
                    last = mm(ps[:, unit(j), c * S:(c + 1) * S], chunk_tile(m, i, k), m.merged[:, k],
                              start=k == 0, stop=k == ND - 1)
                last.then_inc(done, 1)
            j += 1

        rms(1)
        t.wait_ge(sem["usd"], at("usd", 2))
        for b in range(4):
            mm(ps[:, b, :], m.zero[:, 0:P], m.zero[:], start=True, stop=False, skip_group_check=True)

        def up(i, f, fk):
            t.wait_ge(sem["lo"], at("lo", fk + 1))
            for k in range(ND):
                if f == 0:
                    t.wait_ge(sem["ulo"], at("ulo", 8 + k + 1))
                last = product3(mm, ps[:, 4 + f % 3, 0:S], m, i, k, m.uhi_ffn[:, k], m.ulo[:, k],
                                start=k == 0, stop=k == ND - 1)
            last.then_inc(done, 1)

        def down(i, f, fk, last=False):
            t.wait_ge(sem["lo_g"], at("lo_g", MIX2 + fk + 1))
            t.wait_ge(sem["hidlo"], at("hidlo", fk + 1))
            for n in range(ND):
                x = product3(mm, ps[:, n // 2, (n % 2) * S:(n % 2 + 1) * S], m, i, n, m.hidhi[:, f % 3],
                             m.hidlo[:, f % 3], start=False, stop=last, skip_group_check=True)
            x.then_inc(done, 1)

        up(E_FFN, 0, 0)
        with t.Fori(0, 3) as it:
            for q in range(9):
                up(E_FFN + 1 + 2 * q, 1 + q, 9 * it + 1 + q)
                down(E_FFN + 2 + 2 * q, q, 9 * it + q)
        for f in range(28, NF2):
            up(E_FFN + 2 * f - 1, f, f)
            down(E_FFN + 2 * f, f - 1, f - 1)
        down(E_FFN + 63, 31, 31, last=True)

    with t.Fori(0, DEPTH) as l:
        layer(l)


def scalar2(nc, a, m, sem, stream, par_source, aside):
    ps, con = m.ps, m.con_of
    landed, done = stream.landed, stream.done
    act = nc.scalar.activation

    def layer(l):
        at = lambda name, k: l * SIGNALS2[name] + k
        landed_at = lambda i, rounds=0: stream.landed_value(l, i, rounds)
        done_at = lambda i, rounds=0: stream.done_value(l, i, rounds)
        par = lambda name, at=0, n=1: m.par[:, PAR2[name] + at:PAR2[name] + at + n]
        bank = lambda j: 4 + j % 4
        a.wait_ge(sem["layer_done"], at("layer_done", 1))
        a.dma_start(m.par[:, 0:PAR2["all"]], par_source[bass.ds(l, 1)].rearrange("a p n -> (a p) n"))\
            .then_inc(sem["par"], 16)
        a.dma_start(aside, m.h).then_inc(sem["aside"], 16)

        def high(i):
            act(high_of(m, i), chunk_of(m, i), ACT.Copy).then_inc(sem["hi"], 1)

        def later_high(i, rounds=0):
            a.wait_ge(landed[i % RING], landed_at(i, rounds))
            a.wait_ge(done, done_at(i - HIGH, rounds))
            high(i)

        def rms(k):
            for n in range(ND):
                if k == 1 and n % 2 == 0:
                    a.wait_ge(sem["xres"], at("xres", n // 2 + 1))
                act(m.sq[:, n], m.h[:, n], ACT.Square).then_inc(sem["usq"], 1)
            a.wait_ge(sem["uvar"], at("uvar", k + 1))
            act(m.sd, ps[:, 0, 0:S], ACT.Sqrt, bias=con("eps2", 1)).then_inc(sem["usd"], 1)

        def high_u(i, dst):
            for n in range(ND):
                a.wait_ge(sem["umod"], at("umod", 8 * i + n + 1))
                act(dst[:, n], m.u[:, n], ACT.Copy).then_inc(sem["uhi"], 1)

        for i in range(HIGH):
            a.wait_ge(landed[i % RING], landed_at(i))
            high(i)
        rms(0)
        a.wait_ge(sem["aside"], at("aside", 16))
        high_u(0, m.uhi)
        copied = sem["copied"]
        a.wait_ge(sem["par"], at("par", 16))
        j = 0
        for n in range(3):
            if n < 2:
                later_high(E_Q + 2 * n + 3)
            a.wait_ge(done, done_at(E_Q + 2 * n + 1 if n < 2 else E_K))
            for c in range(2 if n < 2 else 1):
                act(m.qk_raw[2 * n + c], ps[:, bank(j), c * S:(c + 1) * S], ACT.Copy)
                last = act(m.hsq[2 * n + c], ps[:, bank(j), c * S:(c + 1) * S], ACT.Square)
            last.then_inc(copied, 1)
            later_high(E_Q + 2 * n + 4 if n < 2 else E_K + 3)
            j += 1
        a.wait_ge(done, done_at(E_V))
        act(m.va, two(ps, bank(j), 0, P), ACT.Copy).then_inc(copied, 1)
        later_high(E_V + 3)
        j += 1
        a.wait_ge(done, done_at(E_IF))
        act(m.ow[:, 0], ps[0:4, bank(j), 0:S], ACT.Identity, bias=par("ib")[0:4])
        act(m.ow[:, 1], ps[0:4, bank(j), S:2 * S], ACT.Identity, bias=par("fb")[0:4]).then_inc(copied, 1)
        later_high(E_IF + 3)
        j += 1
        for i, dst in ((E_QM, m.qm), (E_KM, m.km)):
            later_high(i + 3)
            a.wait_ge(done, done_at(i + 1))
            act(dst, two(ps, bank(j)), ACT.Copy).then_inc(copied, 1)
            later_high(i + 4)
            j += 1
        for q in range(2):
            later_high(E_VM + 2 * q + 3)
            a.wait_ge(done, done_at(E_VM + 2 * q + 1))
            act(m.vm[:, :, q * S:(q + 1) * S], two(ps, bank(j)), ACT.Copy).then_inc(copied, 1)
            later_high(E_VM + 2 * q + 4)
            j += 1
        for q in range(2):
            later_high(E_OM + 2 * q + 3)
            a.wait_ge(done, done_at(E_OM + 2 * q + 1))
            act(m.om[:, 2 * q:2 * q + 2], two(ps, bank(j)), ACT.Sigmoid).then_inc(copied, 1)
            later_high(E_OM + 2 * q + 4)
            j += 1
        act(m.ow[:, 2], m.ow[:, 1], ACT.Abs)
        a.drain()
        act(m.ow[:, 3], m.ow[:, 2], ACT.Exp, scale=-1.0).then_inc(sem["fexp"], 1)
        def gate_copy(k):
            if k < 7:
                later_high(E_GATE + 2 * k + 3)
            a.wait_ge(done, done_at(E_GATE + 2 * k + 1))
            act(m.gate2[:, 2 * k:2 * k + 2], two(ps, k % 4), ACT.Copy).then_inc(sem["gcopy"], 1)
            if k < 6:
                later_high(E_GATE + 2 * k + 4)
            if k == 7:
                a.dma_start(m.h, aside).then_inc(sem["back"], 16)

        gate_copy(0)
        for n in range(5):
            a.wait_ge(sem["hvar"], at("hvar", n + 1))
            act(m.hsq[n], ps[:, bank(j), 0:S], ACT.Sqrt, bias=con("eps2", 1)).then_inc(sem["hsd"], 1)
            j += 1
        j += 5
        gate_copy(1)
        gate_copy(2)
        a.wait_ge(sem["dup"], at("dup", 1))
        act(m.ka, two(ps, bank(j)), ACT.Copy).then_inc(sem["dupc"], 1)
        for k in range(3, 8):
            gate_copy(k)

        def exps(i):
            a.wait_ge(sem["nmx"], at("nmx", i + 1))
            if i >= 2:
                a.wait_ge(sem["tr"], at("tr", i - 1))
            for r in range(4):
                act(m.e[:, i % 2, r, 0:P * (i % 2 + 1)], score_view(ps, i, i % 2)[:, r], ACT.Exp,
                    bias=m.nmx[:, i % 2, r:r + 1], accum_out=m.sums[:, i % 2, r:r + 1])
            act(m.esink[:, i % 2], m.esink[:, i % 2], ACT.Exp).then_inc(sem["ex"], 1)

        def turned(i):
            a.wait_ge(sem["tr"], at("tr", i + 1))
            k = i % 2
            act(m.ptt[:, i, 0:k + 1].rearrange("p k r q -> p k (r q)"), ps[:, 2:3 + k, :], ACT.Copy)\
                .then_inc(sem["ptt"], 1)

        def heads_out(g):
            a.wait_ge(sem["pv"], at("pv", 2 * g + 2))
            act(m.att[:, 2 * g:2 * g + 2], two(ps, g), ACT.Copy).then_inc(sem["oc"], 1)

        exps(0)
        for i in range(4):
            if i + 1 < 4:
                exps(i + 1)
            turned(i)
        heads_out(0)
        heads_out(1)

        def numerator_side(h):
            a.wait_ge(sem["num"], at("num", h + 1))
            act(m.den[:, h % 2], ps[:, h, S:2 * S], ACT.Abs).then_inc(sem["absd"], 1)
            a.wait_ge(sem["hh"], at("hh", h + 1))
            act(m.sq[:, h], m.hm[:, h], ACT.Square).then_inc(sem["hsq"], 1)

        j = 0
        for h in range(4):
            a.wait_ge(sem["bc"], at("bc", h + 1))
            act(m.em[:, h % 2], ps[:, bank(2 * h + 1), S:2 * S], ACT.Exp).then_inc(sem["me"], 1)
            a.wait_ge(sem["arg"], at("arg", h + 1))
            act(m.ee[:, h % 2], m.ee[:, h % 2], ACT.Exp).then_inc(sem["ee"], 1)
            if h >= 1:
                numerator_side(h - 1)
        numerator_side(3)
        j = 8
        for h in range(4):
            a.wait_ge(sem["hvar"], at("hvar", 5 + h + 1))
            if h >= 2:
                a.wait_ge(sem["hm"], at("hm", h - 1))
            act((m.sd, m.hsq[4])[h % 2], ps[:, bank(j), 0:S], ACT.Sqrt, bias=con("eps2", 1))\
                .then_inc(sem["hsd"], 1)
            j += 1

        act(m.gate2[:], m.gate2[:], ACT.Sigmoid).then_inc(sem["outsg"], 1)

        for i in range(E_FFN, E_FFN + HIGH):
            a.wait_ge(landed[i % RING], landed_at(i))
            high(i)
        rms(1)
        high_u(1, m.uhi_ffn)

        def relu(i, f, rounds=0):
            a.wait_ge(done, done_at(i, rounds))
            act(m.silu[:, f % 3], ps[:, 4 + f % 3, 0:S], ACT.Relu).then_inc(sem["relu"], 1)

        def hidden_high(f, fk):
            a.wait_ge(sem["hid"], at("hid", fk + 1))
            act(m.hidhi[:, f % 3], m.hid[:, f % 3], ACT.Copy).then_inc(sem["hidhi"], 1)

        def step(i, f, fk, rounds=0):
            relu(i, f, rounds)
            later_high(i + 3, rounds)
            hidden_high(f, fk)
            later_high(i + 4, rounds)

        relu(E_FFN, 0)
        later_high(E_FFN + 3)
        hidden_high(0, 0)
        with a.Fori(0, 3) as it:
            for q in range(9):
                step(E_FFN + 1 + 2 * q, 1 + q, 9 * it + 1 + q, 2 * it)
        for f in range(28, 31):
            step(E_FFN + 2 * f - 1, f, f)
        relu(E_FFN + 61, 31)
        hidden_high(31, 31)

    with a.Fori(0, DEPTH) as l:
        layer(l)


def vector2(nc, v, m, sem, stream):
    ps, con = m.ps, m.con_of
    landed, done = stream.landed, stream.done
    tt, ts, stt = nc.vector.tensor_tensor, nc.vector.tensor_scalar, nc.vector.scalar_tensor_tensor

    def layer(l):
        at = lambda name, k: l * SIGNALS2[name] + k
        landed_at = lambda i, rounds=0: stream.landed_value(l, i, rounds)
        done_at = lambda i, rounds=0: stream.done_value(l, i, rounds)
        par = lambda name, at=0, n=1: m.par[:, PAR2[name] + at:PAR2[name] + at + n]
        c2 = lambda name, n=P, at=0: m.conb[:, CON2[name] + at:CON2[name] + at + n]
        bank = lambda j: 4 + j % 4

        def rms(k, gain):
            v.wait_ge(sem["par"], at("par", 16))
            v.wait_ge(sem["usd"], at("usd", k + 1))
            nc.vector.reciprocal(m.rs, m.sd)
            v.drain()
            for n in range(ND):
                last = stt(m.u[:, n], m.h[:, n], par(gain, n), m.rs, ALU.mult, ALU.mult)
                last.then_inc(sem["umod"], 1)

        def low_u(i, uhi):
            for n in range(ND):
                v.wait_ge(sem["uhi"], at("uhi", 8 * i + n + 1))
                tt(m.ulo[:, n], m.u[:, n], uhi[:, n], ALU.subtract).then_inc(sem["ulo"], 1)

        rms(0, "nmix")
        low_u(0, m.uhi)
        for n in range(5):
            v.wait_ge(sem["hsd"], at("hsd", n + 1))
            nc.vector.reciprocal(m.hsq[n], m.hsq[n])
            v.drain()
            stt(m.qk_raw[n], m.qk_raw[n], par("qn" if n < 4 else "kn"), m.hsq[n], ALU.mult, ALU.mult)\
                .then_inc(sem["qn"], 1)
        v.drain()
        for n in range(5):
            b = bank(16 + n)
            dst = m.qa[:, n] if n < 4 else m.kda
            v.wait_ge(sem["rotp"], at("rotp", n + 1))
            tt(m.tmp[n % 2], ps[:, b, 0:S], c2("sinq" if n < 4 else "sink", S), ALU.mult)
            tt(dst, m.qk_raw[n], c2("cosq" if n < 4 else "cosk", S), ALU.mult)
            v.drain()
            tt(dst, dst, m.tmp[n % 2], ALU.add).then_inc(sem["rope"], 1)

        w = lambda k: m.ow[:, k]
        v.wait_ge(sem["fexp"], at("fexp", 1))
        log1p(nc, v, w(3), w(2), w(4), w(5), w(6))
        ts(w(1), w(1), 0.0, None, ALU.min)
        v.drain()
        tt(w(1), w(1), w(5), ALU.subtract)
        v.drain()
        nc.vector.tensor_tensor_scan(w(2), w(7), w(1), 0.0, ALU.mult, ALU.add)
        v.drain()
        tt(w(3), w(0), w(2), ALU.subtract)
        v.drain()
        nc.vector.tensor_tensor_scan(w(4), w(3), w(3), 0.0, ALU.max, ALU.max)
        v.drain()
        ts(w(5), w(4), -1.0, None, ALU.mult)
        v.drain()
        tt(w(6), w(5), w(2), ALU.subtract).then_inc(sem["mt"], 1)
        v.wait_ge(sem["rt"], at("rt", 1))
        nc.vector.tensor_copy(m.rt, ps[:, bank(22), 0:8].rearrange("p (a h) -> p a h", a=2))\
            .then_inc(sem["mtc"], 1)

        def maxima(i):
            g, a = i // 2, i % 2
            mx, sink = m.mx[:, i % 2], par("sink", 4 * g, 4)
            v.wait_ge(sem["sc"], at("sc", i + 1))
            s = score_view(ps, i, a)
            mask = lambda t: t.rearrange("p (a t) -> p a t", a=1).to_broadcast([P, 4, P])
            tt(s[:, :, a * P:(a + 1) * P], s[:, :, a * P:(a + 1) * P], mask(con("neg")), ALU.add)
            if a == 1:
                tt(s[:, :, 0:P], s[:, :, 0:P], mask(c2("band")), ALU.add)
            v.drain()
            nc.vector.tensor_reduce(mx, s, AX, ALU.max)
            v.drain()
            tt(mx, mx, sink, ALU.max)
            v.drain()
            ts(m.nmx[:, i % 2], mx, -1.0, None, ALU.mult)
            tt(m.esink[:, i % 2], sink, mx, ALU.subtract)
            v.drain()
            v.nop().then_inc(sem["nmx"], 1)

        def weights(i):
            f = m.fac[:, i % 2]
            v.wait_ge(sem["ex"], at("ex", i + 1))
            tt(f, m.sums[:, i % 2], m.esink[:, i % 2], ALU.add)
            v.drain()
            nc.vector.reciprocal(f, f)
            v.drain()
            for r in range(4):
                p = m.e[:, i % 2, r, 0:P * (i % 2 + 1)]
                last = ts(p, p, f[:, r:r + 1], None, ALU.mult)
            last.then_inc(sem["pr"], 1)

        maxima(0)
        maxima(1)
        for i in range(4):
            weights(i)
            if i + 2 < 4:
                maxima(i + 2)

        def quotient(h):
            d = m.den[:, h % 2]
            v.wait_ge(sem["absd"], at("absd", h + 1))
            tt(d, d, m.em[:, h % 2], ALU.max)
            v.drain()
            nc.vector.reciprocal(d, d)
            v.drain()
            tt(m.hm[:, h], ps[:, h, 0:S], d, ALU.mult).then_inc(sem["hh"], 1)

        for h in range(4):
            b = bank(2 * h + 1)
            v.wait_ge(sem["qk"], at("qk", h + 1))
            tt(m.qkm[:, h % 2], ps[:, bank(2 * h), 0:384], c2("tri8", 384), ALU.mult).then_inc(sem["qkm"], 1)
            v.wait_ge(sem["me"], at("me", h + 1))
            ts(m.ee[:, h % 2, 0:S], ps[:, b, 0:S], m.rt[:, 0, h:h + 1], 0.0, ALU.add, ALU.min)
            ts(m.ee[:, h % 2, S:S + P], ps[:, b, P:S], m.rt[:, 1, h:h + 1], 0.0, ALU.add, ALU.min)\
                .then_inc(sem["arg"], 1)
            v.drain()
            if h >= 2:
                v.wait_ge(sem["num"], at("num", h - 1))
            v.wait_ge(sem["ee"], at("ee", h + 1))
            tt(m.mm[:, h % 2], m.ee[:, h % 2], m.qkm[:, h % 2], ALU.mult).then_inc(sem["mm"], 1)
            if h >= 1:
                quotient(h - 1)
        quotient(3)
        for h in range(4):
            v.wait_ge(sem["hsd"], at("hsd", 5 + h + 1))
            d = (m.sd, m.hsq[4])[h % 2]
            nc.vector.reciprocal(m.rs, d)
            v.drain()
            stt(m.hm[:, h], m.hm[:, h], par("hn", h), m.rs, ALU.mult, ALU.mult)
            v.drain()
            tt(m.hm[:, h], m.hm[:, h], m.om[:, h], ALU.mult).then_inc(sem["hm"], 1)

        j = 12
        for b in range(2):
            for q in range(4):
                if b == 0 and q == 0:
                    v.wait_ge(sem["outsg"], at("outsg", 1))
                v.wait_ge(done, done_at(E_BR + 4 * b + q))
                y, g, out = two(ps, bank(j)), m.gate2[:, 8 * b + 2 * q:8 * b + 2 * q + 2], m.merged[:, 2 * q:2 * q + 2]
                if b == 0:
                    last = tt(out, y, g, ALU.mult)
                else:
                    tt(g, y, g, ALU.mult)
                    v.drain()
                    last = tt(out, out, g, ALU.add)
                last.then_inc(sem["outm"], 1)
                j += 1
        v.wait_ge(sem["back"], at("back", 16))
        for q in range(4):
            v.wait_ge(done, done_at(E_OUT + 2 * q + 1))
            tt(m.h[:, 2 * q:2 * q + 2], two(ps, bank(j)), m.h[:, 2 * q:2 * q + 2], ALU.add)\
                .then_inc(sem["xres"], 1)
            j += 1
        v.drain()
        def low(i, count):
            v.wait_ge(sem["hi"], at("hi", MIX2 + count))
            tt(low_of(m, i), chunk_of(m, i), high_of(m, i), ALU.subtract).then_inc(sem["lo"], 1)

        low(E_FFN, 1)
        low(E_FFN + 1, 2)
        rms(1, "nffn")
        low_u(1, m.uhi_ffn)

        def hidden(f, fk):
            v.wait_ge(sem["relu"], at("relu", fk + 1))
            tt(m.hid[:, f % 3], m.silu[:, f % 3], m.silu[:, f % 3], ALU.mult).then_inc(sem["hid"], 1)

        def hidden_low(f, fk):
            v.wait_ge(sem["hidhi"], at("hidhi", fk + 1))
            tt(m.hidlo[:, f % 3], m.hid[:, f % 3], m.hidhi[:, f % 3], ALU.subtract)\
                .then_inc(sem["hidlo"], 1)

        def step(f, fk):
            hidden(f, fk)
            hidden_low(f, fk)
            if not isinstance(fk, int) or fk < 30:
                low(E_FFN + 2 * f + 3, 2 * fk + 4)

        step(0, 0)
        with v.Fori(0, 3) as it:
            for q in range(9):
                step(1 + q, 9 * it + 1 + q)
        for f in range(28, NF2):
            step(f, f)
        v.wait_ge(done, done_at(E_FFN + 63))
        for q in range(4):
            tt(m.h[:, 2 * q:2 * q + 2], two(ps, q), m.h[:, 2 * q:2 * q + 2], ALU.add).then_inc(sem["xres"], 1)
        v.drain()
        v.nop().then_inc(sem["layer_done"], 1)

    with v.Fori(0, DEPTH) as l:
        layer(l)


def gpsimd2(nc, g, m, sem):
    def layer(l):
        at = lambda name, k: l * SIGNALS2[name] + k

        def low_down(i, count):
            g.wait_ge(sem["hi"], at("hi", MIX2 + count))
            nc.gpsimd.tensor_tensor(low_of(m, i), chunk_of(m, i), high_of(m, i), ALU.subtract)\
                .then_inc(sem["lo_g"], 1)

        for i in range(MIX2):
            g.wait_ge(sem["hi"], at("hi", i + 1))
            nc.gpsimd.tensor_tensor(low_of(m, i), chunk_of(m, i), high_of(m, i), ALU.subtract)\
                .then_inc(sem["lo_g"], 1)
        low_down(E_FFN + 2, 3)
        with g.Fori(0, 3) as it:
            for q in range(9):
                low_down(E_FFN + 4 + 2 * q, 2 * (9 * it + 1 + q) + 3)
        for f in range(28, 31):
            low_down(E_FFN + 2 * f + 2, 2 * f + 3)
        low_down(E_FFN + 63, 64)

    with g.Fori(0, DEPTH) as l:
        layer(l)


def build(nc, x, c, con, con1, con2, stream1, ada_w, stream2, par1, par2, aside, out):
    with ExitStack() as ctx:
        m = memory(nc, ctx)
        sem = lambda name: ctx.enter_context(nc.semaphore(name))
        sem1 = {name: sem("a_" + name) for name in SIGNALS1}
        first = Stream(N1, [sem(f"landed{s}") for s in range(RING)], sem("done"))
        sem2 = {name: sem("b_" + name) for name in SIGNALS2}
        second = Stream(N2, first.landed, first.done, first)
        ada = Modulation(sem)
        inputs, ready, silu_c, stored, con_b = sem("inputs"), sem("ready"), sem("silu_c"), sem("stored"), sem("con_b")
        block = ctx.enter_context(nc.Block())

        @block.sync
        def _(sp):
            sp.dma_start(m.cvec[:, 8:16], c).then_inc(inputs, 16)
            sp.dma_start(m.h, x).then_inc(inputs, 16)
            sp.dma_start(m.con[:], con).then_inc(inputs, 16)
            sp.dma_start(m.conb[:, 0:CON1["all"]], con1).then_inc(inputs, 16)
            sp.wait_ge(ada.used, 12)
            stream_weights(sp, m, stream1, first)
            stream_weights(sp, m, stream2, second)
            sp.wait_ge(sem2["layer_done"], 1 + DEPTH)
            sp.dma_start(out, m.h).then_inc(stored, 16)
            sp.wait_ge(stored, 16)

        @block.tensor
        def _(t):
            t.wait_ge(inputs, 64)
            t.wait_ge(ready, 2)
            t.nop().then_inc(first.done, RING)
            tensor1(nc, t, m, sem1, first, ada)
            t.wait_ge(con_b, 16)
            tensor2(nc, t, m, sem2, second)

        @block.scalar
        def _(a):
            a.wait_ge(inputs, 64)
            nc.scalar.activation(m.cvec[:, 0:8], m.cvec[:, 8:16], ACT.Silu).then_inc(silu_c, 1)
            scalar1(nc, a, m, sem1, first, par1, aside)
            a.dma_start(m.conb[:, 0:CON2["all"]], con2).then_inc(con_b, 16)
            a.wait_ge(con_b, 16)
            scalar2(nc, a, m, sem2, second, par2, aside)

        @block.vector
        def _(v):
            nc.vector.memset(m.zero[:], 0.0)
            nc.vector.memset(m.gr, 0.0)
            nc.vector.memset(m.raw[:], 0.0)
            nc.vector.memset(m.vb, 0.0).then_inc(ready, 2)
            v.wait_ge(inputs, 64)
            v.wait_ge(silu_c, 1)
            v.nop().then_inc(sem1["layer_done"], 1)
            vector1(nc, v, m, sem1, first, ada)
            v.wait_ge(con_b, 16)
            nc.vector.memset(m.ow[:, 7], 1.0)
            v.drain()
            v.nop().then_inc(sem2["layer_done"], 1)
            vector2(nc, v, m, sem2, second)

        @block.gpsimd
        def _(g):
            gpsimd1(nc, g, m, sem1, first, ada, ada_w)
            gpsimd2(nc, g, m, sem2)



def by_column_tile(w):
    k, n = w.shape
    return w.reshape(k // P, P, n // P, P).transpose(2, 1, 0, 3).reshape(n // P, P, k)


def by_row_tile(w):
    return w.reshape(-1, P, 1024)


def columns(v):
    return v.reshape(-1, P).T


def interleave(a, b):
    return np.stack([a, b], 1).reshape(-1, *a.shape[1:])


def ffn_chunks(gate, up, down):
    gu, d = interleave(by_column_tile(gate), by_column_tile(up)), by_row_tile(down)
    parts = [gu[0:2]]
    for f in range(1, NF):
        parts += [gu[2 * f:2 * f + 2], d[f - 1:f]]
    return parts + [d[NF - 1:]]


def pack1(i):
    streams, pars = [], []
    for l in range(DEPTH):
        parts = ffn_chunks(i["ffn_w_gate"][l, 0], i["ffn_w_up"][l, 0], i["ffn_w_down"][l, 0])
        w = i["w_in"][l]
        cut = lambda a, n: by_column_tile(w[:, a:a + n])
        parts += [interleave(cut(0, 1024), cut(1024, 1024)), cut(3072, 2048), cut(2048, 1024)]
        small = np.zeros((D, P), np.float32)
        small[:, 0:48] = w[:, 7696:7744]
        small[:, 64:80] = w[:, 5120:5136]
        parts += [by_column_tile(small), cut(5136, 1024), cut(6160, 256), cut(6416, 256), cut(6672, 256),
                  cut(7184, 256), cut(6928, 256), cut(7440, 256)]
        gate = [cut(7744 + 1024 * b, 1024) for b in range(3)]
        out = [by_column_tile(i[name][l]) for name in ("w_a_out", "w_b_out", "w_c_out")]
        parts.append(gate[0])
        for name in ("cmp_k_w1", "cmp_v_w1"):
            parts.append(i[name][l].reshape(2, 8, P, P).transpose(0, 2, 1, 3).reshape(2, P, 1024))
        parts.append(out[0][0:4])
        for g in range(4):
            parts += [gate[1][2 * g:2 * g + 1], out[0][4 + g:5 + g], gate[1][2 * g + 1:2 * g + 2]]
        parts += [interleave(gate[2], out[1]), out[2]]
        parts.append(by_column_tile(i["w_o"][l]))
        parts += ffn_chunks(i["ffn_w_gate"][l, 1], i["ffn_w_up"][l, 1], i["ffn_w_down"][l, 1])
        streams.append(np.concatenate(parts))
        assert len(streams[-1]) == N1, (len(streams[-1]), N1)
        p = np.zeros((P, PAR1["all"]), np.float32)
        def put(name, v):
            p[0:v.shape[0], PAR1[name]:PAR1[name] + v.shape[1]] = v
        put("ada_b", columns(i["ada_b"][l]))
        put("ln_g", columns(i["ln_g"][l].reshape(-1)))
        put("ln_b", columns(i["ln_b"][l].reshape(-1)))
        put("aw", i["conv_a_w"][l].reshape(TAPS_A, ND, P).transpose(2, 1, 0).reshape(P, -1))
        put("ab", columns(i["conv_a_b"][l]))
        put("ag", columns(i["norm_a_g"][l]))
        put("abb", columns(i["norm_a_b"][l]))
        put("xw", i["ssm_conv_w"][l].reshape(TAPS_B, NXB, P).transpose(2, 1, 0).reshape(P, -1))
        put("xb", columns(i["ssm_conv_b"][l]))
        put("nw", columns(i["ssm_norm_w"][l]))
        put("dsk", columns(np.repeat(i["ssm_d"][l], 64)))
        put("dtb", i["ssm_dt_bias"][l][:, None])
        put("alog", i["ssm_a_log"][l][:, None])
        for name, src in (("pek", "cmp_pe_k"), ("pev", "cmp_pe_v")):
            put(name, i[src][l].reshape(16, P).T)
        put("w2k", np.tile(i["cmp_k_w2"][l], (1, 2)))
        put("w2v", i["cmp_v_w2"][l])
        pars.append(p)
    return np.concatenate(streams), np.stack(pars)


def pack_modulation(i):
    w = [i["ada_w"][l].reshape(8, P, 9, 1024).transpose(2, 0, 1, 3).reshape(9 * 8, P, 1024) for l in range(DEPTH)]
    parts = [w[0][0:24]]
    for l in range(DEPTH):
        parts += [w[l][24:72], w[(l + 1) % DEPTH][0:24]]
    return np.concatenate(parts)


def pack2(i):
    i = {k[:-2]: v for k, v in i.items() if k.endswith("_2")}
    streams, pars = [], []
    for l in range(DEPTH):
        w = i["w_in"][l]
        cut = lambda a, n: by_column_tile(w[:, a:a + n])
        small = np.zeros((D, P), np.float32)
        small[:, 0:8] = w[:, 2304:2312]
        parts = [cut(0, 512), cut(512, 128), cut(640, 128), by_column_tile(small), cut(768, 256), cut(1024, 256),
                 cut(1280, 512), cut(1792, 512)]
        parts.append(cut(2312, 2048))
        for name in ("w_att_branch", "w_m_branch"):
            parts.append(by_column_tile(i[name][l]).reshape(4, 2, P, 512).transpose(0, 2, 1, 3).reshape(4, P, 1024))
        parts.append(by_column_tile(i["w_out"][l]))
        up, down = by_column_tile(i["w_ff1"][l]), by_row_tile(i["w_ff2"][l])
        parts += [up[0:1]] + [np.stack([up[f], down[f - 1]]) for f in range(1, NF2)] + [down[NF2 - 1:]]
        streams.append(np.concatenate(parts))
        assert len(streams[-1]) == N2
        p = np.zeros((P, PAR2["all"]), np.float32)
        def put(name, v):
            p[0:v.shape[0], PAR2[name]:PAR2[name] + v.shape[1]] = v
        put("nmix", columns(i["norm_mix"][l]))
        put("nffn", columns(i["norm_ffn"][l]))
        put("qn", np.tile(i["att_q_norm"][l], 2)[:, None])
        put("kn", np.tile(i["att_k_norm"][l], 2)[:, None])
        order = [4 * g + r for g in range(2) for r in (0, 2, 1, 3)]
        put("sink", np.tile(i["att_sinks"][l][order], (P, 1)))
        put("ib", i["m_gate_bias"][l][0:4, None])
        put("fb", i["m_gate_bias"][l][4:8, None])
        put("hn", columns(i["m_head_norm"][l]))
        pars.append(p)
    return np.concatenate(streams), np.stack(pars)


def kernel(**inputs):
    import concourse.bacc as bacc
    from concourse.bass_utils import run_bass_kernel_spmd

    i = {k: np.asarray(v) for k, v in inputs.items()}
    con, con1, con2 = constants()
    stream1, par1 = pack1(i)
    stream2, par2 = pack2(i)
    arrays = {
        "x_t": np.ascontiguousarray(i["x"][0].T.reshape(ND, P, S).transpose(1, 0, 2)),
        "c_t": np.ascontiguousarray(columns(i["c"][0])),
        "con": con, "con1": con1, "con2": con2,
        "stream1": stream1, "ada": pack_modulation(i), "stream2": stream2, "par1": par1, "par2": par2,
    }
    nc = bacc.Bacc("TRN2", target_bir_lowering=False, num_devices=1)
    args = [nc.dram_tensor(k + "_dram", a.shape, F32, kind="ExternalInput").ap() for k, a in arrays.items()]
    out = nc.dram_tensor("out_t", (P, ND, S), F32, kind="ExternalOutput").ap()
    aside = nc.dram_tensor("h_aside", (P, ND, S), F32, kind="Internal").ap()
    build(nc, *args, aside, out)
    got = run_bass_kernel_spmd(nc, [{k + "_dram": a for k, a in arrays.items()}], core_ids=[0]).results[0]["out_t"]
    return np.ascontiguousarray(np.asarray(got).transpose(2, 1, 0)).reshape(1, S, D)
```
